# Optimizing a Trainium2 kernel written in Bass

```python
import jax
import jax.numpy as jnp
from jax import lax
import numpy as np

D_MODEL = 2048
BATCH = 1
SEQ = 256
DEPTH = 2

PLE_DIM = 256
EPS = 1e-6

RW_HEAD_DIM = 64
RW_WIDTH = D_MODEL // 4
RW_HEADS = RW_WIDTH // RW_HEAD_DIM
RW_DECAY_RANK = 32
RW_AAA_RANK = 32
RW_GATE_RANK = 96
RW_LN_EPS = 64e-5
RW_COLS = 3 * RW_WIDTH + RW_DECAY_RANK + RW_AAA_RANK + RW_GATE_RANK

GD_HEAD_DIM = 128
GD_WIDTH = 3 * D_MODEL // 8
GD_HEADS = GD_WIDTH // GD_HEAD_DIM
GD_CONV = 5
GD_CHUNK = 64
GD_COLS = 4 * GD_WIDTH + 4 * GD_HEADS

ML_V_DIM = 128
ML_QK_DIM = 64
ML_WIDTH = D_MODEL - RW_WIDTH - GD_WIDTH
ML_HEADS = ML_WIDTH // ML_V_DIM
ML_CHUNK = 64
ML_GATE_CAP = 15.0
ML_COLS = 2 * ML_HEADS * ML_QK_DIM + 2 * ML_WIDTH + 4 * ML_HEADS

N_IN = RW_COLS + GD_COLS + ML_COLS
D_FF = 11 * D_MODEL // 4
FFN_CONV = 3

kernel_name = "hybrid_rwkv7_gdn_mlstm_encoder"

def _rms_norm(x, g):
    xf = x.astype(jnp.float32)
    y = xf * lax.rsqrt(jnp.mean(xf * xf, axis=-1, keepdims=True) + EPS)
    return (y * g.astype(jnp.float32)).astype(x.dtype)

def _l2_normalize(x):
    xf = x.astype(jnp.float32)
    return xf * lax.rsqrt(jnp.sum(xf * xf, axis=-1, keepdims=True) + 1e-6)

def _softcap(x):
    return ML_GATE_CAP * jnp.tanh(x / ML_GATE_CAP)

def _dwconv_centred(x, w):
    K, C = w.shape
    return lax.conv_general_dilated(
        x, w[:, None, :].astype(x.dtype), window_strides=(1,),
        padding=[(K // 2, K // 2)], dimension_numbers=("NWC", "WIO", "NWC"),
        feature_group_count=C)

def _token_shift_bidir(z, mu):
    prev = jnp.pad(z[:, :-1], ((0, 0), (1, 0), (0, 0)))
    nxt = jnp.pad(z[:, 1:], ((0, 0), (0, 1), (0, 0)))
    return z + mu[0] * (prev - z) + mu[1] * (nxt - z)

def _heads_first(x):
    return jnp.swapaxes(x, 1, 2)

def _dir_stack_shared(x):
    return jnp.stack([x, jnp.flip(x, axis=2)])

def _dir_stack_gate(g):
    g = jnp.transpose(g, (2, 0, 3, 1))
    return jnp.stack([g[0], jnp.flip(g[1], axis=-1)])

def _dir_merge(y):
    return jnp.swapaxes(y[0] + jnp.flip(y[1], axis=2), 1, 2)

def _rw_time_major(fwd, bwd):
    B, T = fwd.shape[:2]
    s = jnp.stack([fwd, jnp.flip(bwd, axis=1)])
    return jnp.moveaxis(s, 2, 0).reshape(T, 2, B, RW_HEADS, RW_HEAD_DIM)

def _rwkv7_mix(z, mu, w0, w2, a0, a2, g2, k_k, k_a, r_k, ln_g, ln_b):
    B, T, _ = z.shape
    z = _token_shift_bidir(z, mu).astype(jnp.float32)
    W = RW_WIDTH
    r, k, v, zw, za, zg = jnp.split(
        z, [W, 2 * W, 3 * W, 3 * W + RW_DECAY_RANK, 3 * W + RW_DECAY_RANK + RW_AAA_RANK], axis=-1)
    w_log = -jax.nn.softplus(-(w0 + jnp.einsum("btr,drc->btdc", jnp.tanh(zw), w2))) - 0.5
    decay = jnp.exp(-jnp.exp(w_log))
    a = jax.nn.sigmoid(a0 + jnp.einsum("btr,drc->btdc", za, a2))
    g = jax.nn.sigmoid(zg) @ g2
    kk = _l2_normalize((k * k_k).reshape(B, T, RW_HEADS, RW_HEAD_DIM)).reshape(B, T, W)
    kd = k[:, :, None, :] * (1.0 + (a - 1.0) * k_a)
    bvec = kk[:, :, None, :] * a
    xs = (_rw_time_major(r, r), _rw_time_major(decay[:, :, 0], decay[:, :, 1]),
          _rw_time_major(kd[:, :, 0], kd[:, :, 1]), _rw_time_major(v, v),
          _rw_time_major(-kk, -kk), _rw_time_major(bvec[:, :, 0], bvec[:, :, 1]))

    def step(S, inp):
        r_t, w_t, k_t, v_t, a_t, b_t = inp
        sa = jnp.einsum("dbhij,dbhj->dbhi", S, a_t)
        S = S * w_t[..., None, :] + sa[..., :, None] * b_t[..., None, :] + v_t[..., :, None] * k_t[..., None, :]
        return S, jnp.einsum("dbhij,dbhj->dbhi", S, r_t)

    S0 = jnp.zeros((2, B, RW_HEADS, RW_HEAD_DIM, RW_HEAD_DIM), jnp.float32)
    _, ys = lax.scan(step, S0, xs)
    y = jnp.moveaxis(ys[:, 0] + jnp.flip(ys[:, 1], axis=0), 0, 1)
    mean = jnp.mean(y, axis=-1, keepdims=True)
    var = jnp.mean(jnp.square(y - mean), axis=-1, keepdims=True)
    y = ((y - mean) * lax.rsqrt(var + RW_LN_EPS)).reshape(B, T, W) * ln_g + ln_b
    coef = jnp.sum(r.reshape(B, T, 1, RW_HEADS, RW_HEAD_DIM) * kd.reshape(B, T, 2, RW_HEADS, RW_HEAD_DIM) * r_k,
                   axis=(2, 4))
    bonus = (coef[..., None] * v.reshape(B, T, RW_HEADS, RW_HEAD_DIM)).reshape(B, T, W)
    return (y + bonus) * g

def _chunk_gated_delta(q, k, v, g, beta):
    *lead, T, dk = q.shape
    dv = v.shape[-1]
    C = GD_CHUNK
    n = T // C
    q = q.reshape(*lead, n, C, dk)
    k = k.reshape(*lead, n, C, dk)
    v = v.reshape(*lead, n, C, dv)
    g = jnp.cumsum(g.reshape(*lead, n, C), axis=-1)
    beta = beta.reshape(*lead, n, C)
    incl = jnp.tril(jnp.ones((C, C), dtype=bool))
    strict = jnp.tril(jnp.ones((C, C), dtype=bool), -1)
    diff = g[..., :, None] - g[..., None, :]
    decay = jnp.where(incl, jnp.exp(jnp.where(incl, diff, 0.0)), 0.0)
    kb = k * beta[..., None]
    L = jnp.where(strict, jnp.einsum("...id,...jd->...ij", kb, k) * decay, 0.0)
    eye = jnp.eye(C, dtype=q.dtype)
    rhs = jnp.concatenate([v * beta[..., None], kb * jnp.exp(g)[..., None]], axis=-1)
    sol = lax.linalg.triangular_solve(eye + L, rhs, left_side=True, lower=True, unit_diagonal=True)
    u, w = sol[..., :dv], sol[..., dv:]
    intra = jnp.where(incl, jnp.einsum("...id,...jd->...ij", q, k) * decay, 0.0)
    front = lambda a: jnp.moveaxis(a, len(lead), 0)

    def step(S, inp):
        q_c, k_c, u_c, w_c, g_c, a_c = inp
        v_new = u_c - jnp.einsum("...cd,...de->...ce", w_c, S)
        o = jnp.einsum("...cd,...de->...ce", q_c * jnp.exp(g_c)[..., None], S) + a_c @ v_new
        g_last = g_c[..., -1:]
        k_w = k_c * jnp.exp(g_last - g_c)[..., None]
        S = S * jnp.exp(g_last)[..., None] + jnp.einsum("...cd,...ce->...de", k_w, v_new)
        return S, o

    S0 = jnp.zeros((*lead, dk, dv), jnp.float32)
    _, o = lax.scan(step, S0, (front(q), front(k), front(u), front(w), front(g), front(intra)))
    return jnp.moveaxis(o, 0, len(lead)).reshape(*lead, T, dv)

def _gated_deltanet_mix(z, conv_w, a_log, dt_bias, norm_g):
    B, T, _ = z.shape
    qkv, zgate, za, zb = jnp.split(z, [3 * GD_WIDTH, 4 * GD_WIDTH, 4 * GD_WIDTH + 2 * GD_HEADS], axis=-1)
    qkv = jax.nn.silu(_dwconv_centred(qkv, conv_w)).astype(jnp.float32)
    q, k, v = jnp.split(qkv, 3, axis=-1)
    q = _l2_normalize(q.reshape(B, T, GD_HEADS, GD_HEAD_DIM)) * GD_HEAD_DIM ** -0.5
    k = _l2_normalize(k.reshape(B, T, GD_HEADS, GD_HEAD_DIM))
    v = v.reshape(B, T, GD_HEADS, GD_HEAD_DIM)
    za = za.astype(jnp.float32).reshape(B, T, 2, GD_HEADS)
    g = -jnp.exp(a_log) * jax.nn.softplus(za + dt_bias)
    beta = jax.nn.sigmoid(zb.astype(jnp.float32).reshape(B, T, 2, GD_HEADS))
    o = _chunk_gated_delta(_dir_stack_shared(_heads_first(q)), _dir_stack_shared(_heads_first(k)),
                           _dir_stack_shared(_heads_first(v)), _dir_stack_gate(g), _dir_stack_gate(beta))
    o = _dir_merge(o)
    o = _rms_norm(o, norm_g) * jax.nn.silu(zgate.astype(jnp.float32).reshape(B, T, GD_HEADS, GD_HEAD_DIM))
    return o.reshape(B, T, GD_WIDTH)

def _mlstm_chunked(q, k, v, ig, lf):
    *lead, T, dk = q.shape
    dv = v.shape[-1]
    C = ML_CHUNK
    n = T // C
    q = q.reshape(*lead, n, C, dk)
    k = k.reshape(*lead, n, C, dk)
    v = v.reshape(*lead, n, C, dv)
    ig = ig.reshape(*lead, n, C)
    b = jnp.cumsum(lf.reshape(*lead, n, C), axis=-1)
    incl = jnp.tril(jnp.ones((C, C), dtype=bool))
    front = lambda a: jnp.moveaxis(a, len(lead), 0)

    def step(carry, inp):
        c_mat, n_vec, m = carry
        q_c, k_c, v_c, i_c, b_c = inp
        log_w = jnp.where(incl, b_c[..., :, None] - b_c[..., None, :] + i_c[..., None, :], -jnp.inf)
        log_prev = b_c + m[..., None]
        m_t = jnp.maximum(log_prev, jnp.max(log_w, axis=-1))
        prev_scale = jnp.exp(log_prev - m_t)
        w = jnp.exp(log_w - m_t[..., None]) * jnp.einsum("...td,...sd->...ts", q_c, k_c)
        num = prev_scale[..., None] * jnp.einsum("...td,...de->...te", q_c, c_mat) + w @ v_c
        den = prev_scale * jnp.einsum("...td,...d->...t", q_c, n_vec) + jnp.sum(w, axis=-1)
        h = num / jnp.maximum(jnp.abs(den), jnp.exp(-m_t))[..., None]
        log_end = b_c[..., -1:] - b_c + i_c
        m_new = jnp.maximum(b_c[..., -1] + m, jnp.max(log_end, axis=-1))
        decay_prev = jnp.exp(b_c[..., -1] + m - m_new)
        k_w = k_c * jnp.exp(log_end - m_new[..., None])[..., None]
        c_mat = decay_prev[..., None, None] * c_mat + jnp.einsum("...sd,...se->...de", k_w, v_c)
        n_vec = decay_prev[..., None] * n_vec + jnp.sum(k_w, axis=-2)
        return (c_mat, n_vec, m_new), h

    init = (jnp.zeros((*lead, dk, dv), jnp.float32), jnp.zeros((*lead, dk), jnp.float32),
            jnp.zeros(tuple(lead), jnp.float32))
    _, h = lax.scan(step, init, (front(q), front(k), front(v), front(ig), front(b)))
    return jnp.moveaxis(h, 0, len(lead)).reshape(*lead, T, dv)

def _mlstm_mix(z, i_bias, f_bias, norm_g):
    B, T, _ = z.shape
    qk = ML_HEADS * ML_QK_DIM
    q, k, v, o, zi, zf = jnp.split(
        z.astype(jnp.float32),
        [qk, 2 * qk, 2 * qk + ML_WIDTH, 2 * qk + 2 * ML_WIDTH, 2 * qk + 2 * ML_WIDTH + 2 * ML_HEADS], axis=-1)
    q = _heads_first(q.reshape(B, T, ML_HEADS, ML_QK_DIM))
    k = _heads_first(k.reshape(B, T, ML_HEADS, ML_QK_DIM)) * ML_QK_DIM ** -0.5
    v = _heads_first(v.reshape(B, T, ML_HEADS, ML_V_DIM))
    ig = _softcap(zi.reshape(B, T, 2, ML_HEADS) + i_bias)
    lf = jax.nn.log_sigmoid(_softcap(zf.reshape(B, T, 2, ML_HEADS) + f_bias))
    h = _mlstm_chunked(_dir_stack_shared(q), _dir_stack_shared(k), _dir_stack_shared(v),
                       _dir_stack_gate(ig), _dir_stack_gate(lf))
    h = _dir_merge(h)
    h = _rms_norm(h, norm_g.reshape(ML_HEADS, ML_V_DIM)) * jax.nn.sigmoid(o.reshape(B, T, ML_HEADS, ML_V_DIM))
    return h.reshape(B, T, ML_WIDTH)

def setup_inputs(seed: int = 0) -> dict:
    key = jax.random.key(seed)
    ks = jax.random.split(key, 32)
    nrm = lambda i, shape: jax.random.normal(ks[i], shape, jnp.float32)
    uni = lambda i, shape, lo, hi: jax.random.uniform(ks[i], shape, jnp.float32, lo, hi)
    L, D = DEPTH, D_MODEL
    return {
        "x": nrm(0, (BATCH, SEQ, D)),
        "p": nrm(1, (L, BATCH, SEQ, PLE_DIM)),
        "norm_mix": 1.0 + 0.02 * nrm(2, (L, D)),
        "w_in": nrm(3, (L, D, N_IN)) * D ** -0.5,
        "rw_shift_mu": uni(4, (L, 2, RW_COLS), 0.0, 0.5),
        "rw_w0": uni(5, (L, 2, RW_WIDTH), -4.0, 1.0),
        "rw_w2": nrm(6, (L, 2, RW_DECAY_RANK, RW_WIDTH)) * RW_DECAY_RANK ** -0.5,
        "rw_a0": 0.1 * nrm(7, (L, 2, RW_WIDTH)),
        "rw_a2": nrm(8, (L, 2, RW_AAA_RANK, RW_WIDTH)) * RW_AAA_RANK ** -0.5,
        "rw_g2": nrm(9, (L, RW_GATE_RANK, RW_WIDTH)) * RW_GATE_RANK ** -0.5,
        "rw_k_k": 0.85 + 0.02 * nrm(10, (L, RW_WIDTH)),
        "rw_k_a": 1.0 + 0.02 * nrm(11, (L, RW_WIDTH)),
        "rw_r_k": 0.1 * nrm(12, (L, RW_HEADS, RW_HEAD_DIM)),
        "rw_ln_g": 1.0 + 0.02 * nrm(13, (L, RW_WIDTH)),
        "rw_ln_b": 0.02 * nrm(14, (L, RW_WIDTH)),
        "gd_conv_w": nrm(15, (L, GD_CONV, 3 * GD_WIDTH)) * GD_CONV ** -0.5,
        "gd_a_log": jnp.log(uni(16, (L, 2, GD_HEADS), 1.0, 16.0)),
        "gd_dt_bias": uni(17, (L, 2, GD_HEADS), -4.6, -2.3),
        "gd_norm_g": 1.0 + 0.02 * nrm(18, (L, GD_HEAD_DIM)),
        "ml_i_bias": 0.1 * nrm(19, (L, 2, ML_HEADS)),
        "ml_f_bias": uni(20, (L, 2, ML_HEADS), 3.0, 6.0),
        "ml_norm_g": 1.0 + 0.02 * nrm(21, (L, ML_WIDTH)),
        "w_out": nrm(22, (L, D, D)) * D ** -0.5,
        "norm_ffn": 1.0 + 0.02 * nrm(23, (L, D)),
        "w_up": nrm(24, (L, D, 2 * D_FF)) * D ** -0.5,
        "ffn_conv_w": nrm(25, (L, FFN_CONV, 2 * D_FF)) * FFN_CONV ** -0.5,
        "ffn_conv_b": 0.02 * nrm(26, (L, 2 * D_FF)),
        "w_down": nrm(27, (L, D_FF, D)) * D_FF ** -0.5,
        "norm_ple": 1.0 + 0.02 * nrm(28, (L, D)),
        "w_ple_gate": nrm(29, (L, D, D)) * D ** -0.5,
        "w_ple_proj": nrm(30, (L, PLE_DIM, D)) * PLE_DIM ** -0.5,
        "norm_final": 1.0 + 0.02 * nrm(31, (D,)),
    }

def reference(x, p, norm_mix, w_in, rw_shift_mu, rw_w0, rw_w2, rw_a0, rw_a2, rw_g2, rw_k_k, rw_k_a,
              rw_r_k, rw_ln_g, rw_ln_b, gd_conv_w, gd_a_log, gd_dt_bias, gd_norm_g, ml_i_bias, ml_f_bias,
              ml_norm_g, w_out, norm_ffn, w_up, ffn_conv_w, ffn_conv_b, w_down, norm_ple, w_ple_gate,
              w_ple_proj, norm_final):
    h = x
    for i in range(DEPTH):
        u = _rms_norm(h, norm_mix[i])
        z = u @ w_in[i]
        z_rw, z_gd, z_ml = jnp.split(z, [RW_COLS, RW_COLS + GD_COLS], axis=-1)
        y_rw = _rwkv7_mix(z_rw, rw_shift_mu[i], rw_w0[i], rw_w2[i], rw_a0[i], rw_a2[i], rw_g2[i],
                          rw_k_k[i], rw_k_a[i], rw_r_k[i], rw_ln_g[i], rw_ln_b[i])
        y_gd = _gated_deltanet_mix(z_gd, gd_conv_w[i], gd_a_log[i], gd_dt_bias[i], gd_norm_g[i])
        y_ml = _mlstm_mix(z_ml, ml_i_bias[i], ml_f_bias[i], ml_norm_g[i])
        y = jnp.concatenate([y_rw, y_gd, y_ml], axis=-1).astype(h.dtype)
        h = h + y @ w_out[i]
        u = _rms_norm(h, norm_ffn[i])
        up = _dwconv_centred(u @ w_up[i], ffn_conv_w[i]) + ffn_conv_b[i]
        gate, val = jnp.split(up, 2, axis=-1)
        h = h + (jax.nn.silu(gate) * val) @ w_down[i]
        u = _rms_norm(h, norm_ple[i])
        h = h + jax.nn.sigmoid(u @ w_ple_gate[i]) * (p[i] @ w_ple_proj[i])
    return _rms_norm(h, norm_final)


_drawn_inputs = setup_inputs


def setup_inputs(seed=0):
    import zlib

    import numpy as np

    out = dict(_drawn_inputs(seed))
    spreads = {}
    factors = {'rw_a0': 3.849,
     'rw_k_k': 8.0,
     'rw_k_a': 6.556,
     'rw_ln_g': 7.572,
     'rw_ln_b': 6.572,
     'gd_norm_g': 5.737,
     'ml_i_bias': 8.0,
     'ml_norm_g': 6.421,
     'norm_ffn': 2.924,
     'ffn_conv_b': 2.965,
     'norm_ple': 8.0,
     'norm_final': 2.881}
    for name, (base, spread) in spreads.items():
        noise = np.random.default_rng([zlib.crc32(name.encode()), seed]).standard_normal(out[name].shape)
        drawn = base * np.exp(spread * noise) if base else spread * noise
        out[name] = jnp.asarray(drawn.astype(out[name].dtype))
    for name, factor in factors.items():
        out[name] = (out[name] * factor).astype(out[name].dtype)
    return out
```

```python
from contextlib import ExitStack
import math

import concourse.bass as bass
from concourse import mybir
from concourse.bass import ds

F32 = mybir.dt.float32
BF16 = mybir.dt.bfloat16
I16 = mybir.dt.int16
ALU = mybir.AluOpType
ACT = mybir.ActivationFunctionType
AX_X = mybir.AxisListType.X

P = 128
EPS = 1e-6
RW_LN_EPS = 64e-5
ML_GATE_CAP = 15.0
KAPPA = math.exp(-0.5)


def trunk(nc, x, p, norm_mix, w_in, rw_shift_mu, rw_w0, rw_w2, rw_a0, rw_a2, rw_g2, rw_k_k, rw_k_a,
          rw_r_k, rw_ln_g, rw_ln_b, gd_conv_w, gd_a_log, gd_dt_bias, gd_norm_g, ml_i_bias, ml_f_bias,
          ml_norm_g, w_out, norm_ffn, w_up, ffn_conv_w, ffn_conv_b, w_down, norm_ple, w_ple_gate,
          w_ple_proj, norm_final, out):
    DEPTH, D, N_IN = w_in.shape
    T = x.shape[1]
    NT = T // P
    KT = D // P
    RW = rw_w0.shape[2]
    RC = RW // P
    RD, RG = rw_w2.shape[2], rw_g2.shape[1]
    GH = gd_a_log.shape[2]
    GW = GH * P
    MH = ml_i_bias.shape[2]
    MW = MH * P
    GP, MP = GH // 2, MH // 2
    TAPS, FTAPS = gd_conv_w.shape[1], ffn_conv_w.shape[1]
    FF = w_down.shape[1]
    FT = FF // P
    PLE = p.shape[3]
    assert NT == 2 and rw_a2.shape[2] == RD and 2 * RD <= 64 and GH % 2 == 0 and MH % 2 == 0

    RING, KS = 4, 4
    RW_C0, GQ_C0 = 0, 3 * RW + 2 * RD + RG
    GT_C0 = GQ_C0 + 3 * GW
    MQ_C0 = GT_C0 + GW + 4 * GH
    MT_C0 = MQ_C0 + MH * P
    GT_W, MT_W = GW + 4 * GH, 2 * MW + 4 * MH
    assert MT_C0 + MT_W == N_IN
    blocks = [("rw", b, RW_C0 + RW * b, [P] * RC) for b in range(3)]
    blocks += [("lora", 0, 3 * RW, [2 * RD, RG])]
    blocks += [("gdq", b, GQ_C0 + 3 * P * b, [P] * 3) for b in range(3 * GH // 3)]
    blocks += [("gdt", b, GT_C0 + GT_W // 2 * b, None) for b in range(2)]
    blocks += [("mlq", b, MQ_C0 + 3 * P * b, [P] * 3) for b in range(MH // 3)]
    blocks += [("mlt", b, MT_C0 + MT_W // 4 * b, None) for b in range(4)]
    NB = len(blocks)

    def width(block):
        return sum(block[3]) if block[3] else (GT_W // 2 if block[0] == "gdt" else MT_W // 4)

    NO = D // 512
    NU = FT // 4
    SL_IN = 0
    SL_OUT = SL_IN + 4 * NB
    SL_UP = SL_OUT + 4 * NO
    SL_DOWN = SL_UP + 8 * NU
    SL_PLE = SL_DOWN + NO * FT // KS
    SL = SL_PLE + 4 * NO
    assert SL % RING == 0 and all(s % RING == 0 for s in (SL_OUT, SL_UP, SL_DOWN, SL_PLE))

    rows, NR = {}, 0
    for name, n in (("norm0", KT), ("norm1", KT), ("norm2", KT), ("mu", 6 * RC), ("w0", 2 * RC), ("a0", 2 * RC),
                    ("k_k", RC), ("k_a", RC), ("r_k", RC), ("conv", TAPS * 3 * GH), ("fconv", FTAPS * 2 * FT),
                    ("fbias", 2 * FT), ("mu_wa", 2), ("mu_g", 2)):
        rows[name] = NR
        NR += n
    PT = -(-NR // P)

    with ExitStack() as ctx:
        def sb(name, shape, dt=F32):
            return ctx.enter_context(nc.sbuf_tensor(name, shape, dt))

        def sem(name):
            return ctx.enter_context(nc.semaphore(name))

        H = sb("H", [P, NT, D])
        UT = sb("UT", [P, KT, T])
        YB = sb("YB", [P, NT, D])
        ring = sb("ring", [P, RING, KS, 512])
        zwords = RC * 3 * T + 2 * T + 3 * GH * T + NT * GT_W + MH * T + NT * MT_W
        Z = sb("Z", [P, max(zwords, FT * T)])
        o = 0

        def zpart(n):
            nonlocal o
            o += n
            return Z[:, o - n:o]
        zrw = zpart(3 * RC * T).rearrange("p (c t) -> p c t", t=T)
        zlora = zpart(2 * T).rearrange("p (c t) -> p c t", t=T)
        zgd = zpart(3 * GH * T).rearrange("p (c t) -> p c t", t=T)
        zgt = zpart(NT * GT_W).rearrange("p (t c) -> p t c", t=NT)
        zmq = zpart(MH * T).rearrange("p (c t) -> p c t", t=T)
        zmt = zpart(NT * MT_W).rearrange("p (t c) -> p t c", t=NT)
        gT = Z[:, 0:FT * T].rearrange("p (c t) -> p c t", t=T)
        swa = UT[:, :, :].rearrange("p (k c d) t -> p k d c t", k=2, d=2)
        u_tmp = YB
        projw = YB[:, :, :].rearrange("p k n -> p (k n)").rearrange("p (k n) -> p k n", k=PLE // P)

        par = sb("par", [P, PT * P])
        mu_mid = sb("mu_mid", [P, 3 * RC + 2])
        lnp = sb("lnp", [P, 2, RW])
        gdn = sb("gdn", [P, P])
        w2sb = YB[0:2 * RD, 0, RW:3 * RW].rearrange("p (d c) -> p d c", d=2)
        g2sb = YB[0:RG, 1, RW:2 * RW]
        gpar = sb("gpar", [P, 4, 2 * GH])
        ident = sb("ident", [P, P])
        ones = sb("ones", [P, P])
        headones = sb("headones", [P, P])
        incl = [sb(f"incl{d}", [P, P]) for d in range(2)]
        negstrict = [sb(f"negstrict{d}", [P, P]) for d in range(2)]
        LEVELS = 7
        lev = [sb(f"lev{d}", [P, LEVELS, P], BF16) for d in range(2)]
        pred = [sb(f"pred{d}", [P, 4, P], BF16) for d in range(2)]
        one_h = sb("one_h", [P, P], BF16)
        epsb = sb("epsb", [P, 4])
        small = sb("small", [P, 16])
        sgate = sb("sgate", [P, NT, RW])
        scores = [sb(f"scores{d}", [P, 4, 4, P]) for d in range(2)]
        TN = [sb(f"TN{d}", [P, 4, P]) for d in range(2)]
        TT = [sb(f"TT{d}", [P, 4, P]) for d in range(2)]
        XS = [sb(f"XS{d}", [P, 4, P]) for d in range(2)]
        AR = [sb(f"AR{d}", [P, NT, 2, P]) for d in range(2)]
        KB = [sb(f"KB{d}", [P, 2, T]) for d in range(2)]
        cs = [sb(f"cs{d}", [P, T]) for d in range(2)]
        ew = [YB[:, 1, RW + 3 * T * d:RW + 3 * T * (d + 1)].rearrange("p (k t) -> p k t", k=3) for d in range(2)]
        mid = [sb(f"mid{d}", [P, 4]) for d in range(2)]
        ch = YB[:, 0, RW:RW + 6 * T].rearrange("p (k t) -> p k t", k=6)
        chg = UT[:, 0:2, :]
        ewg = [UT[:, 2 + 2 * j:4 + 2 * j, :] for j in range(2)]
        mln = UT[:, 6:9, :].rearrange("p k t -> p (k t)")[:, 0:MW]
        V1 = UT[:, 9:12, :].rearrange("p k t -> p (k t)")[:, 0:NT * 2 * (P + 2)]\
            .rearrange("p (j h c) -> p j h c", j=NT, h=2)
        heads = sb("heads", [P, 12, P])
        OL, OT, Vt = heads[:, 0:4, :], heads[:, 4:8, :], heads[:, 8:12, :]
        prow = heads[:, 0:PT, :]
        KBt = [sb(f"KBt{d}", [P, 2, P]) for d in range(2)]
        rf = [sb(f"rf{d}", [P, 2, P]) for d in range(2)]
        uf = [XS[d][:, 2:4, :] for d in range(2)]
        S0 = [XS[d][:, 0:2, :] for d in range(2)]
        ufg = [scores[d][:, 0, 2:4, :] for d in range(2)]
        S0g = [scores[d][:, 0, 0:2, :] for d in range(2)]
        coef = sb("coef", [P, NT, 2])
        st = sb("st", [P, 4, 4])
        gates = sb("gates", [P, 6, NT, 2 * GH])
        gs = sb("gs", [P, 24, 2])
        gx = sb("gx", [P, 3, NT, 4 * GH])
        pT = XS[0][:, :, :].rearrange("p a c -> p (a c)").rearrange("p (k t) -> p k t", t=T)
        pin = XS[1][:, :, :].rearrange("p a c -> p (a c)").rearrange("p (t c) -> p t c", t=NT)

        ps = [ctx.enter_context(nc.psum_tensor(f"ps{i}", [P, 512], F32)) for i in range(8)]


        NAMES = """consts h_in rows_in mixp_in pin_in proj_in nf_in row_free mixp_free w2_in mln_in
            landed0 landed1 landed2 landed3 slot_free par_turned par_ready h_ready rms_ready u_ready ut_psum ut_ready
            blk_scaled blk_evac lora_act lora_psum lora_ready gate_psum gate_ready
            rw_sq rw_ssq rw_rn rw_vt rw_vtc rw_cs rw_exp rw_cf rw_coef rw_coefc rw_ops rw_sc rw_masked rw_pv rw_rf
            inv_t1 inv_t1p inv_tn1 inv_x inv_xs inv_t inv_tn inv_tt
            rw_u rw_uf rw_state rw_s0 rw_pv2 rw_rf2 rw_u2 rw_uf2 rw_y rw_yc rw_var rw_rstd rw_done
            gd_sp gd_ln gd_gl gd_cum gd_cumc gd_exp gd_silu gd_sq gd_ssq gd_rn gd_vt gd_vtc gd_qk gd_kt gd_ktc gd_sc
            gd_gb gd_arg gd_d gd_dm gd_nt gd_rhs gd_u gd_uf gd_state gd_s0 gd_ks gd_rs gd_us gd_usc gd_y gd_yc
            gd_ss gd_rstd gd_done
            ml_x ml_tanh ml_f ml_ln ml_g ml_rt ml_rows ml_back ml_backc ml_expm ml_sig ml_in ml_sc ml_mb ml_arg ml_d
            ml_dm ml_p ml_num ml_numc ml_ss ml_rstd ml_done
            yt_psum yt_ready up_gact up_gconv up_silu up_vact up_done p_turned pt_ready ple_psum ple_sig ple_done
            fin_out out_done""".split()
        S = {n: sem(n) for n in NAMES}

        block = ctx.enter_context(nc.Block())
        FIRST = (0, NT - 1)
        LAST_COL = (P - 1, 0)
        LEV = LEVELS - 1

        def bc(ap, n):
            return ap.unsqueeze(2).to_broadcast([ap.shape[0], ap.shape[1], n])

        def bmid(ap, n):
            return ap.unsqueeze(1).to_broadcast([ap.shape[0], n, ap.shape[1]])

        w_in_v = w_in.rearrange("l (k p) n -> l p k n", p=P)
        w_out_v = w_out.rearrange("l (k p) n -> l p k n", p=P)
        w_up_v = w_up.rearrange("l (k p) n -> l p k n", p=P)
        w_down_v = w_down.rearrange("l (k p) n -> l p k n", p=P)
        w_pg_v = w_ple_gate.rearrange("l (k p) n -> l p k n", p=P)


        ROW_SRC = (("norm0", lambda L: norm_mix[L].rearrange("(c p) -> c p", p=P), KT),
                   ("norm1", lambda L: norm_ffn[L].rearrange("(c p) -> c p", p=P), KT),
                   ("norm2", lambda L: norm_ple[L].rearrange("(c p) -> c p", p=P), KT),
                   ("mu", lambda L: rw_shift_mu[L, 0, 0:3 * RW].rearrange("(c p) -> c p", p=P), 3 * RC),
                   ("mu1", lambda L: rw_shift_mu[L, 1, 0:3 * RW].rearrange("(c p) -> c p", p=P), 3 * RC),
                   ("w0", lambda L: rw_w0[L].rearrange("d (c p) -> (d c) p", p=P), 2 * RC),
                   ("a0", lambda L: rw_a0[L].rearrange("d (c p) -> (d c) p", p=P), 2 * RC),
                   ("k_k", lambda L: rw_k_k[L].rearrange("(c p) -> c p", p=P), RC),
                   ("k_a", lambda L: rw_k_a[L].rearrange("(c p) -> c p", p=P), RC),
                   ("r_k", lambda L: rw_r_k[L].rearrange("(c h) j -> c (h j)", h=2), RC),
                   ("conv", lambda L: gd_conv_w[L].rearrange("k (c p) -> (k c) p", p=P), TAPS * 3 * GH),
                   ("fconv", lambda L: ffn_conv_w[L].rearrange("k (c p) -> (k c) p", p=P), FTAPS * 2 * FT),
                   ("fbias", lambda L: ffn_conv_b[L].rearrange("(c p) -> c p", p=P), 2 * FT),
                   ("mu_wa", lambda L: rw_shift_mu[L, :, 3 * RW:3 * RW + 2 * RD], 2),
                   ("mu_g", lambda L: rw_shift_mu[L, :, 3 * RW + 2 * RD:3 * RW + 2 * RD + RG], 2))
        rows["mu1"] = rows["mu"] + 3 * RC

        def row_pieces():
            for name, src, n in ROW_SRC:
                r, done = rows[name], 0
                while done < n:
                    k = min(n - done, P - (r + done) % P)
                    yield done, (r + done) // P, (r + done) % P, k, src
                    done += k
        ROWS_TOTAL = 16 * len(list(row_pieces()))

        def mixer_params(L):
            yield lnp[:, 0, :], rw_ln_g[L].partition_broadcast(P)
            yield lnp[:, 1, :], rw_ln_b[L].partition_broadcast(P)
            yield gdn[:, :], gd_norm_g[L].partition_broadcast(P)
            for i, src in enumerate((gd_dt_bias, gd_a_log, ml_i_bias, ml_f_bias)):
                yield gpar[:, i, :], src[L].rearrange("d h -> (d h)").partition_broadcast(P)
        MIXP_TOTAL = 16 * len(list(mixer_params(0)))

        def ml_flat(d):
            return scores[d][:, :, :, :].rearrange("p a b c -> p (a b c)")[:, 0:4 * T]\
                .rearrange("p (h j t) -> p h j t", h=2, j=2)

        def ml_diag(d):
            flat = scores[d][:, :, :, :].rearrange("p a b c -> p (a b c)")
            return [flat[:, h * 2 * T:(h + 1) * 2 * T].rearrange("p (u c) -> p u c", c=P)[:, 0:4:3, :] for h in range(2)]

        def third(ap, k):
            return ap.rearrange("p (k c) -> p k c", k=k)

        def mono(ap, k):
            return ap.rearrange("p a c -> p (a c)")

        def up_buf(g):
            return scores[g][:, :, :, :].rearrange("p a b c -> p (a b c)")[:, 0:4 * T].rearrange("p (c t) -> p c t", t=T)

        @block.sync
        def _(sp):
            for t in range(NT):
                sp.dma_start(H[:, t, :], x[0, t * P:(t + 1) * P, :]).then_inc(S["h_in"], 16)
            with sp.Fori(0, DEPTH) as L:
                base = sp.snap(L * SL)

                def load(slot, src, w, n):
                    sp.wait_ge(S["slot_free"], n + (slot + 1))
                    sp.dma_start(ring[:, slot % RING, :, 0:w], src).then_inc(S[f"landed{slot % RING}"], 16)

                sp.wait_ge(S["consts"], 1)
                sp.wait_ge(S["row_free"], L + 1)
                sp.wait_ge(S["mixp_free"], L + 1)
                for r, tile, p0, k, src in row_pieces():
                    a = src(L)[r:r + k, :]
                    sp.dma_start(prow[p0:p0 + k, tile, 0:a.shape[1]], a).then_inc(S["rows_in"], 16)
                for dst, src in mixer_params(L):
                    sp.dma_start(dst, src).then_inc(S["mixp_in"], 16)
                for i, b in enumerate(blocks):
                    if i == 1:
                        sp.wait_ge(S["ut_ready"], L * 24 + 8)
                        sp.dma_start(w2sb[0:RD], rw_w2[L].rearrange("d r c -> r d c")).then_inc(S["w2_in"], 16)
                        sp.dma_start(w2sb[RD:2 * RD], rw_a2[L].rearrange("d r c -> r d c")).then_inc(S["w2_in"], 16)
                        sp.dma_start(g2sb, rw_g2[L]).then_inc(S["w2_in"], 16)
                    for k in range(4):
                        load(SL_IN + 4 * i + k, w_in_v[L, :, KS * k:KS * k + KS, b[2]:b[2] + width(b)], width(b), base)
                for i in range(NO):
                    if i == 1:
                        sp.wait_ge(S["rw_done"], L * RC + RC)
                        sp.dma_start(mln, ml_norm_g[L].partition_broadcast(P)).then_inc(S["mln_in"], 16)
                    for k in range(4):
                        load(SL_OUT + 4 * i + k, w_out_v[L, :, KS * k:KS * k + KS, 512 * i:512 * i + 512], 512, base)
                with sp.Fori(0, NU) as i:
                    n = sp.snap(base + i * 8)
                    for g in range(2):
                        for k in range(4):
                            load(SL_UP + 4 * g + k, w_up_v[L, :, KS * k:KS * k + KS, ds(i * 512 + g * FF, 512)], 512, n)
                sp.wait_ge(S["ut_ready"], L * 24 + 16)
                sp.dma_start(pin, p[L, 0].rearrange("(t q) c -> q t c", q=P)).then_inc(S["pin_in"], 16)
                for i in range(NO):
                    for k in range(FT // KS):
                        load(SL_DOWN + FT // KS * i + k,
                             w_down_v[L, :, KS * k:KS * k + KS, 512 * i:512 * i + 512], 512, base)
                for i in range(NO):
                    if i == 1:
                        sp.wait_ge(S["ut_ready"], L * 24 + 24)
                        sp.dma_start(projw, w_ple_proj[L].rearrange("(k q) n -> q k n", q=P)).then_inc(S["proj_in"], 16)
                    for k in range(4):
                        load(SL_PLE + 4 * i + k, w_pg_v[L, :, KS * k:KS * k + KS, 512 * i:512 * i + 512], 512, base)
            sp.wait_ge(S["h_ready"], 3 * DEPTH + 1)
            sp.dma_start(Z[:, 0:D], norm_final.partition_broadcast(P)).then_inc(S["nf_in"], 16)
            for t in range(NT):
                sp.wait_ge(S["fin_out"], t + 1)
                sp.dma_start(out[0, t * P:(t + 1) * P, :], YB[:, t, :]).then_inc(S["out_done"], 16)
            sp.wait_ge(S["out_done"], 16 * NT)

        @block.gpsimd
        def _(pool):
            def sel(dst, src, op, base, pattern, cm, fill=0.0):
                return pool.affine_select(out=dst, in_=src, compare_op=op, fill=fill, base=base,
                                          pattern=pattern, channel_multiplier=cm)
            for dst, v in ((ones[:], 1.0), (one_h[:], 1.0), (ident[:], 0.0), (headones[:], 0.0), (prow, 0.0),
                           (epsb[:, 0:1], EPS), (epsb[:, 1:2], RW_LN_EPS), (epsb[:, 2:3], 1.0)):
                pool.memset(dst, v)
            pool.drain()
            pool.memset(headones[0:64, 0:64], 1.0)
            pool.memset(headones[64:128, 64:128], 1.0)
            pool.drain()
            sel(ident[:], ident[:], ALU.not_equal, 0, [[-1, P]], 1, 1.0)
            sel(incl[0][:], ones[:], ALU.is_ge, 0, [[1, P]], -1)
            sel(incl[1][:], ones[:], ALU.is_ge, 0, [[-1, P]], 1)
            for d in range(2):
                step, cm = ((1, -1), (-1, 1))[d]
                for kind, op in enumerate((ALU.is_gt, ALU.is_ge, ALU.is_gt, ALU.is_ge)):
                    sel(pred[d][:, kind, :], one_h[:], op, 0, [[step, P]], cm)
            pool.drain()
            for m in range(LEVELS):
                b = 1 << m
                for d in range(2):
                    cols = lev[d][:, m, :].rearrange("p (n w) -> p n w", w=2 * b)
                    early, late = (cols[:, :, 0:b], cols[:, :, b:2 * b])[::1 - 2 * d]
                    one3 = one_h[:, :].rearrange("p (n w) -> p n w", w=2 * b)[:, :, 0:b]
                    lo, nb = (b, 0)[d], P // (2 * b)
                    sel(early, one3, ALU.is_ge, -lo, [[-2 * b, nb], [0, b]], 1)
                    pool.memset(late, 0.0)
                    pool.drain()
                    sel(early, early, ALU.is_ge, lo + b - 1, [[2 * b, nb], [0, b]], -1)
                    pool.drain()
                    sel(lev[d][:, m, :], lev[d][:, m, :], ALU.not_equal, 0, [[-1, P]], 1, 1.0)
            for d in range(2):
                pool.tensor_tensor(negstrict[d][:], ident[:], incl[d][:], ALU.subtract)
            pool.drain().then_inc(S["consts"], 1)

            with pool.Fori(0, DEPTH) as L:
                with pool.Fori(0, GP) as i:
                    n = pool.snap(L * (2 * GP) + i * 2)
                    for d in range(2):
                        pool.wait_ge(S["gd_d"], n + (d + 1))
                        pool.tensor_tensor(scores[d][:, 0, :, :], scores[d][:, 0, :, :], bmid(negstrict[d][:], 4),
                                           ALU.mult)
                        pool.tensor_tensor(scores[d][:, 1, :, :], scores[d][:, 1, :, :], bmid(incl[d][:], 4),
                                           ALU.mult).then_inc(S["gd_dm"], 1)
                with pool.Fori(0, MP) as i:
                    n = pool.snap(L * (2 * MP) + i * 2)
                    for d in range(2):
                        pool.wait_ge(S["ml_d"], n + (d + 1))
                        dg = ml_diag(d)
                        for h in range(2):
                            pool.tensor_tensor(dg[h], dg[h], bmid(incl[d][:], 2), ALU.mult)
                        pool.drain().then_inc(S["ml_dm"], 1)

        @block.tensor
        def _(pe):
            pe.sem_inc(S["slot_free"], RING)
            for credit in ("row_free", "mixp_free", "up_gconv", "up_done"):
                pe.sem_inc(S[credit], 1)
            pe.wait_ge(S["consts"], 1)

            def mm(o_, a, b, start, stop):
                return pe.matmul(o_, a, b, start=start, stop=stop, skip_group_check=True)

            def turn(o_, a):
                n = a.shape[0]
                return pe.transpose(o_, a, ident[0:n, 0:n])

            def slot_wait(landed, slot):
                pe.wait_ge(S[f"landed{slot % RING}"], landed + 16 * (slot // RING + 1))

            def turn_rows(src, psum_sem):
                for t in range(NT):
                    if psum_sem == "ut_psum":
                        pe.wait_ge(S["u_ready"], uq + (t + 1))
                    for g in range(4):
                        for c in range(4):
                            last = turn(ps[4 * t + g][:, c * P:(c + 1) * P], src[:, t, (4 * g + c) * P:(4 * g + c + 1) * P])
                        last.then_inc(S[psum_sem], 1)

            def token_product(lhs, slot0, landed, kt, bank_of, before=None, after=None):
                for i in range(NO):
                    if before:
                        before(i)
                    for k in range(kt // KS):
                        slot = slot0 + kt // KS * i + k
                        slot_wait(landed, slot)
                        for t in range(NT):
                            for kk in range(KS):
                                c = KS * k + kk
                                last = mm(ps[bank_of(i, t)][:, :], lhs[:, c, t * P:(t + 1) * P], ring[:, slot % RING, kk, :],
                                          c == 0, c == kt - 1)
                        last.then_inc(S["slot_free"], 1)
                    if after:
                        after(i)

            def invert(m2, nt):
                for d in range(2):
                    pe.wait_ge(S["inv_t1"], m2 + (d + 1))
                    for j in range(4):
                        last = turn(ps[4 * d + 1][:, j * P:(j + 1) * P], TT[d][:, j, :])
                    last.then_inc(S["inv_t1p"], 1)
                ml = pe.snap(m2 * LEV)
                mn = pe.snap(m2 * (LEV - 1))
                for lv in range(LEV):
                    for d in range(2):
                        if lv == 0:
                            pe.wait_ge(S["inv_tn1"], m2 + (d + 1))
                        else:
                            pe.wait_ge(S["inv_tn"], mn + (2 * lv - 1 + d))
                        for j in range(4):
                            last = mm(ps[4 * d][:, j * P:(j + 1) * P], nt(d, j), TN[d][:, j, :], True, True)
                        last.then_inc(S["inv_x"], 1)
                    for d in range(2):
                        pe.wait_ge(S["inv_xs"], ml + (2 * lv + d + 1))
                        if lv:
                            pe.wait_ge(S["inv_tt"], ml + (2 * lv - 1 + d))
                        if lv < LEV - 1:
                            for j in range(4):
                                mm(ps[4 * d + 1][:, j * P:(j + 1) * P], TT[d][:, j, :], XS[d][:, j, :], True, True)
                        for j in range(4):
                            last = mm(ps[4 * d + 2][:, j * P:(j + 1) * P], XS[d][:, j, :], TT[d][:, j, :], True, True)
                        last.then_inc(S["inv_t"], 1)

            with pe.Fori(0, DEPTH) as L:
                landed = pe.snap(L * (16 * SL // RING))
                pe.wait_ge(S["h_ready"], L * 3 + 1)
                pe.wait_ge(S["rows_in"], L * ROWS_TOTAL + ROWS_TOTAL)
                for j in range(PT):
                    last = turn(ps[j // 4][:, (j % 4) * P:(j % 4 + 1) * P], prow[:, j, :])
                last.then_inc(S["par_turned"], 1)
                pe.wait_ge(S["par_ready"], L + 1)
                uq = pe.snap(L * 6)
                turn_rows(YB, "ut_psum")
                pe.wait_ge(S["ut_ready"], L * 24 + 8)
                nb = pe.snap(L * NB)
                for i, (kind, b, c0, tiles) in enumerate(blocks):
                    if i >= 2:
                        pe.wait_ge(S["blk_evac"], nb + (i - 1))
                    g = 4 * (i % 2)
                    for k in range(4):
                        slot = SL_IN + 4 * i + k
                        slot_wait(landed, slot)
                        off = 0
                        for c, w in enumerate(tiles or ()):
                            for kk in range(KS):
                                last = mm(ps[g + c][0:w, 0:T], ring[:, slot % RING, kk, off:off + w], UT[:, KS * k + kk, :],
                                          k == kk == 0, k == kk == 3)
                            off += w
                        for t in range(0 if tiles else NT):
                            w = width((kind, b, c0, tiles))
                            for kk in range(KS):
                                last = mm(ps[g + t][:, 0:w], UT[:, KS * k + kk, t * P:(t + 1) * P],
                                          ring[:, slot % RING, kk, 0:w], k == kk == 0, k == kk == 3)
                        last.then_inc(S["slot_free"], 1)

                pe.wait_ge(S["lora_act"], L + 1)
                pe.wait_ge(S["w2_in"], L * 48 + 48)
                pe.wait_ge(S["blk_evac"], nb + NB)
                for j in range(2):
                    for c in range(RC):
                        for d in range(2):
                            last = mm(ps[4 * j + c][:, d * T:(d + 1) * T], w2sb[RD * j:RD * (j + 1), d, c * P:(c + 1) * P],
                                      zlora[RD * j:RD * (j + 1), 0, :], True, True)
                        last.then_inc(S["lora_psum"], 1)
                pe.wait_ge(S["lora_ready"], L * 8 + 8)
                for t in range(NT):
                    last = mm(ps[t][:, :], zlora[0:RG, 1, t * P:(t + 1) * P], g2sb, True, True)
                last.then_inc(S["gate_psum"], 1)
                with pe.Fori(0, RC) as c:
                    pe.wait_ge(S["gate_ready"], L + 1)
                    n = pe.snap(L * RC + c)
                    n2 = pe.snap(n * 2)
                    m2 = pe.snap(L * (2 * (RC + GP)) + c * 2)
                    pe.wait_ge(S["rw_sq"], n + 1)
                    mm(ps[0][:, 0:T], headones[:], ch[:, 2, :], True, True).then_inc(S["rw_ssq"], 1)
                    for t in range(NT):
                        last = turn(ps[1][:, t * P:(t + 1) * P], ch[:, 0, t * P:(t + 1) * P])
                    last.then_inc(S["rw_vt"], 1)
                    pe.wait_ge(S["rw_cf"], n + 1)
                    for t in range(NT):
                        last = mm(ps[0][:, 2 * t:2 * t + 2], ch[:, 3, t * P:(t + 1) * P], headones[:, 0:P:64], True, True)
                    last.then_inc(S["rw_coef"], 1)
                    pe.wait_ge(S["rw_coefc"], n + 1)
                    pe.wait_ge(S["rw_vtc"], n + 1)
                    for d in range(2):
                        pe.wait_ge(S["rw_ops"], n2 + (d + 1))
                        for h in range(2):
                            for t in range(NT):
                                for j in range(2):
                                    hp = slice(64 * h, 64 * h + 64)
                                    last = mm(ps[4 * d + 2 * h + t][:, j * T:(j + 1) * T], KB[d][hp, j, t * P:(t + 1) * P],
                                              AR[d][hp, t, :, :], True, True)
                        last.then_inc(S["rw_sc"], 1)
                    for d in range(2):
                        F = FIRST[d]
                        pe.wait_ge(S["rw_masked"], n2 + (d + 1))
                        for h in range(2):
                            mm(ps[4 * d + 3][:, 64 * h:64 * h + 64], scores[d][:, 2 * h + F, 0, :],
                               Vt[:, F, 64 * h:64 * h + 64], True, True)
                        for j in range(2):
                            last = turn(ps[4 * d + 3][:, T + j * P:T + (j + 1) * P], KB[d][:, j, F * P:(F + 1) * P])
                        last.then_inc(S["rw_pv"], 1)
                    invert(m2, lambda d, j: scores[d][:, j, 2, :])
                    for d in range(2):
                        F = FIRST[d]
                        pe.wait_ge(S["inv_tt"], m2 * LEV + (2 * LEV - 1 + d))
                        pe.wait_ge(S["rw_rf"], n2 + (d + 1))
                        for h in range(2):
                            last = mm(ps[4 * d][:, 64 * h:64 * h + 64], TT[d][:, 2 * h + F, :], rf[d][:, 0, 64 * h:64 * h + 64],
                                      True, True)
                        last.then_inc(S["rw_u"], 1)
                    for d in range(2):
                        F = FIRST[d]
                        pe.wait_ge(S["rw_uf"], n2 + (d + 1))
                        mm(ps[4 * d + 1][:, 0:P], KBt[d][:, 0, :], Vt[:, F, :], True, False)
                        mm(ps[4 * d + 1][:, 0:P], KBt[d][:, 1, :], uf[d][:, 0, :], False, True).then_inc(S["rw_state"], 1)
                    for d in range(2):
                        B = 1 - FIRST[d]
                        pe.wait_ge(S["rw_s0"], n2 + (d + 1))
                        mm(ps[4 * d + 2][:, 0:P], AR[d][:, B, 0, :], S0[d][:, 0, :], True, False)
                        for h in range(2):
                            last = mm(ps[4 * d + 2][:, 64 * h:64 * h + 64], scores[d][:, 2 * h + B, 0, :],
                                      Vt[:, B, 64 * h:64 * h + 64], False, h == 1)
                        last.then_inc(S["rw_pv2"], 1)
                    for d in range(2):
                        B = 1 - FIRST[d]
                        pe.wait_ge(S["rw_rf2"], n2 + (d + 1))
                        for h in range(2):
                            last = mm(ps[4 * d][:, P + 64 * h:P + 64 * h + 64], TT[d][:, 2 * h + B, :],
                                      rf[d][:, 1, 64 * h:64 * h + 64], True, True)
                        last.then_inc(S["rw_u2"], 1)
                    for d in range(2):
                        F, B = FIRST[d], 1 - FIRST[d]
                        pe.wait_ge(S["rw_uf2"], n2 + (d + 1))
                        y = ps[4 * d + 3]
                        mm(y[:, B * P:(B + 1) * P], AR[d][:, B, 1, :], S0[d][:, 0, :], True, False)
                        for t, u in ((B, 1), (F, 0)):
                            for h in range(2):
                                o_ = y[:, t * P + 64 * h:t * P + 64 * h + 64]
                                mm(o_, scores[d][:, 2 * h + t, 1, :], Vt[:, t, 64 * h:64 * h + 64], False, False)
                                last = mm(o_, scores[d][:, 2 * h + t, 3, :], uf[d][:, u, 64 * h:64 * h + 64], False, True)
                        last.then_inc(S["rw_y"], 1)

                pe.wait_ge(S["gd_gl"], L + 1)
                for d in range(2):
                    for t in range(NT):
                        mm(ps[0][:, 2 * GH * t + GH * d:2 * GH * t + GH * d + GH], incl[d][:],
                           gates[:, 0, t, GH * d:GH * d + GH], True, True)
                for t in range(NT):
                    last = mm(ps[0][:, 64 + 2 * GH * t:64 + 2 * GH * (t + 1)], ones[:], gates[:, 0, t, :], True, True)
                last.then_inc(S["gd_cum"], 1)
                with pe.Fori(0, GP) as i:
                    n = pe.snap(L * GP + i)
                    n2 = pe.snap(n * 2)
                    m2 = pe.snap(L * (2 * (RC + GP)) + (i * 2 + 2 * RC))
                    pe.wait_ge(S["gd_sq"], n + 1)
                    for j in range(2):
                        last = mm(ps[j][:, :], ones[:], mono(KB[j][:, :, :], 2), True, True)
                    last.then_inc(S["gd_ssq"], 1)
                    for h in range(2):
                        for t in range(NT):
                            last = turn(ps[2][:, (2 * h + t) * P:(2 * h + t + 1) * P], chg[:, h, t * P:(t + 1) * P])
                    last.then_inc(S["gd_vt"], 1)
                    pe.wait_ge(S["gd_qk"], n + 1)
                    for h in range(2):
                        for t in range(NT):
                            last = turn(ps[3][:, (2 * h + t) * P:(2 * h + t + 1) * P], AR[h][:, t, 0, :])
                    last.then_inc(S["gd_kt"], 1)
                    for h in range(2):
                        for t in range(NT):
                            last = mm(ps[6 + h][:, t * T:(t + 1) * T], AR[h][:, t, 0, :], AR[h][:, t, :, :], True, True)
                    last.then_inc(S["gd_sc"], 1)
                    for d in range(2):
                        for h in range(2):
                            for t in range(NT):
                                o_ = slice((2 * h + t) * P, (2 * h + t + 1) * P)
                                lg = gs[:, 0 + 2 * t + d, h:h + 1].to_broadcast([P, P])
                                lb = gs[:, 4 + 2 * t + d, h:h + 1].to_broadcast([P, P])
                                mm(ps[4 * d + 1][:, o_], lg, incl[d][:], True, True)
                                mm(ps[4 * d][:, o_], lg, incl[d][:], True, False)
                                last = mm(ps[4 * d][:, o_], lb, ident[:], False, True)
                        last.then_inc(S["gd_gb"], 1)
                    pe.wait_ge(S["gd_nt"], n2 + 2)
                    pe.wait_ge(S["gd_vtc"], n + 1)
                    pe.wait_ge(S["gd_ktc"], n + 1)
                    invert(m2, lambda d, j: scores[d][:, 2, j, :])
                    for d in range(2):
                        F = FIRST[d]
                        pe.wait_ge(S["inv_tt"], m2 * LEV + (2 * LEV - 1 + d))
                        pe.wait_ge(S["gd_rhs"], n2 + (d + 1))
                        for h in range(2):
                            last = mm(ps[4 * d][:, h * P:(h + 1) * P], TT[d][:, 2 * h + F, :], TN[d][:, 2 * h + F, :], True, True)
                        last.then_inc(S["gd_u"], 1)
                    for d in range(2):
                        F = FIRST[d]
                        pe.wait_ge(S["gd_uf"], n2 + (d + 1))
                        for h in range(2):
                            last = mm(ps[4 * d + 1][:, h * P:(h + 1) * P], XS[d][:, h, :], ufg[d][:, h, :], True, True)
                        last.then_inc(S["gd_state"], 1)
                        for h in range(2):
                            j = 2 * h + F
                            mm(ps[4 * d + 3][:, j * P:(j + 1) * P], scores[d][:, 3, j, :], ufg[d][:, h, :], True, True)
                    for d in range(2):
                        B = 1 - FIRST[d]
                        pe.wait_ge(S["gd_s0"], n2 + (d + 1))
                        for j in range(2):
                            for h in range(2):
                                last = mm(ps[4 * d + 2][:, (2 * j + h) * P:(2 * j + h + 1) * P], AR[h][:, B, j, :],
                                          S0g[d][:, h, :], True, True)
                        last.then_inc(S["gd_ks"], 1)
                    for d in range(2):
                        B = 1 - FIRST[d]
                        pe.wait_ge(S["gd_rs"], n2 + (d + 1))
                        for h in range(2):
                            last = mm(ps[4 * d][:, (2 + h) * P:(3 + h) * P], TT[d][:, 2 * h + B, :], rf[d][:, h, :], True, True)
                        last.then_inc(S["gd_us"], 1)
                    for d in range(2):
                        B = 1 - FIRST[d]
                        pe.wait_ge(S["gd_usc"], n2 + (d + 1))
                        for h in range(2):
                            j = 2 * h + B
                            last = mm(ps[4 * d + 3][:, j * P:(j + 1) * P], scores[d][:, 3, j, :], KBt[d][:, h, :], True, True)
                        last.then_inc(S["gd_y"], 1)

                pe.wait_ge(S["ml_g"], L + 1)
                for j in range(2):
                    for d in range(2):
                        for t in range(NT):
                            last = turn(ps[j][0:MH, d * T + t * P:d * T + (t + 1) * P],
                                        gx[:, 0, t, 2 * MH * j + MH * d:2 * MH * j + MH * d + MH])
                last.then_inc(S["ml_rt"], 1)
                pe.wait_ge(S["ml_rows"], L + 1)
                for j, rowt in enumerate((TN[0], TT[0])):
                    rr = mono(rowt[0:MH, :, :], 4)
                    for d in range(2):
                        for t in range(NT):
                            q = (4 * j + 2 * d + t) * MH
                            last = mm(ps[2][:, q:q + MH], rr[:, d * T + t * P:d * T + (t + 1) * P], ident[0:MH, 0:MH], True, True)
                last.then_inc(S["ml_back"], 1)
                with pe.Fori(0, MP) as i:
                    n = pe.snap(L * MP + i)
                    n2 = pe.snap(n * 2)
                    pe.wait_ge(S["ml_in"], n + 1)
                    for h in range(2):
                        hp = slice(64 * h, 64 * h + 64)
                        for j in range(NT):
                            last = mm(ps[h][:, j * T:(j + 1) * T], KB[0][hp, 1, j * P:(j + 1) * P], KB[0][hp, 0, :], True, True)
                    last.then_inc(S["ml_sc"], 1)
                    mrow = mono(TN[1][0:MH, :, :], 4)
                    for d in range(2):
                        for h in range(2):
                            last = mm(ps[4 + d][:, h * T:(h + 1) * T], small[0:MH, 8 + h:9 + h].to_broadcast([MH, P]),
                                      mrow[:, d * T:(d + 1) * T], True, True)
                        last.then_inc(S["ml_mb"], 1)
                    for d in range(2):
                        pe.wait_ge(S["ml_p"], n2 + (d + 1))
                        for h in range(2):
                            for t in range(NT):
                                js = [j for j in range(NT) if (j <= t if d == 0 else j >= t)]
                                for j in js:
                                    last = mm(ps[4 * d + 2 + h][:, t * (P + 1):(t + 1) * (P + 1)],
                                              ml_flat(d)[:, h, j, t * P:(t + 1) * P], V1[:, j, h, 0:P + 1], j == js[0],
                                              j == js[-1])
                        last.then_inc(S["ml_num"], 1)

                pe.wait_ge(S["ml_done"], L * MP + MP)
                turn_rows(YB, "yt_psum")
                pe.wait_ge(S["yt_ready"], L * 8 + 8)
                token_product(UT, SL_OUT, landed, KT, lambda i, t: 2 * i + t)

                uq = pe.snap(L * 6 + 2)
                turn_rows(YB, "ut_psum")
                with pe.Fori(0, NU) as i:
                    pe.wait_ge(S["ut_ready"], L * 24 + 16)
                    n = pe.snap(L * NU + i)
                    la = pe.snap(landed + i * (16 * 8 // RING))
                    for g in range(2):
                        pe.wait_ge(S["up_done" if g else "up_gconv"], n + 1)
                        for k in range(4):
                            slot = SL_UP + 4 * g + k
                            slot_wait(la, slot)
                            for c in range(4):
                                for kk in range(KS):
                                    last = mm(ps[4 * g + c][:, 0:T], ring[:, slot % RING, kk, c * P:(c + 1) * P],
                                              UT[:, KS * k + kk, :], k == kk == 0, k == kk == 3)
                            last.then_inc(S["slot_free"], 1)
                pe.wait_ge(S["up_done"], L * NU + (NU + 1))
                token_product(gT, SL_DOWN, landed, FT, lambda i, t: 2 * i + t)

                uq = pe.snap(L * 6 + 4)
                turn_rows(YB, "ut_psum")
                pe.wait_ge(S["ut_ready"], L * 24 + 24)
                pe.wait_ge(S["pin_in"], L * 16 + 16)
                for k in range(PLE // P):
                    for t in range(NT):
                        last = turn(ps[7][:, (2 * k + t) * P:(2 * k + t + 1) * P], pin[:, t, k * P:(k + 1) * P])
                last.then_inc(S["p_turned"], 1)
                pe.wait_ge(S["pt_ready"], L + 1)

                def before(i):
                    if i >= 2:
                        pe.wait_ge(S["ple_done"], L * NO + (i - 1))

                def after(i):
                    if i == 0:
                        pe.wait_ge(S["proj_in"], L * 16 + 16)
                    for t in range(NT):
                        for k in range(PLE // P):
                            last = mm(ps[4 * (i % 2) + 2 + t][:, :], pT[:, k, t * P:(t + 1) * P],
                                      projw[:, k, 512 * i:512 * i + 512], k == 0, k == PLE // P - 1)
                    last.then_inc(S["ple_psum"], 1)
                token_product(UT, SL_PLE, landed, KT, lambda i, t: 4 * (i % 2) + t, before, after)

        @block.scalar
        def _(act):
            act.wait_ge(S["consts"], 1)

            def a(o_, i_, f, **kw):
                return act.activation(o_, i_, f, **kw)

            def rms(q):
                act.wait_ge(S["h_ready"], q)
                for t in range(NT):
                    a(YB[:, t, :], H[:, t, :], ACT.Square, accum_out=small[:, t:t + 1])
                act.drain()
                a(small[:, 2:2 + NT], small[:, 0:NT], ACT.Sqrt, scale=1.0 / D, bias=epsb[:, 0:1]).then_inc(S["rms_ready"], 1)

            def rsqrt(o_, i_, scale, bias):
                a(o_, i_, ACT.Ln, scale=scale, bias=bias)
                act.drain()
                return a(o_, o_, ACT.Exp, scale=-0.5)

            def t1(m2):
                for d in range(2):
                    act.wait_ge(S["inv_t1p"], m2 + (d + 1))
                    a(mono(TN[d][:, :, :], 4), ps[4 * d + 1][:, :], ACT.Copy).then_inc(S["inv_tn1"], 1)
                ml = act.snap(m2 * LEV)
                for lv in range(LEV - 1):
                    for d in range(2):
                        act.wait_ge(S["inv_t"], ml + (2 * lv + d + 1))
                        a(mono(TN[d][:, :, :], 4), ps[4 * d + 1][:, :], ACT.Copy).then_inc(S["inv_tn"], 1)

            with act.Fori(0, DEPTH) as L:
                rms(L * 3 + 1)
                NSC = sum(b[0] in ("rw", "lora", "gdq") for b in blocks)
                act.wait_ge(S["par_ready"], L + 1)
                for i, (kind, b, c0, tiles) in enumerate(blocks):
                    if kind not in ("rw", "lora", "gdq"):
                        continue
                    act.wait_ge(S["slot_free"], L * SL + (RING + SL_IN + 4 * i + 4))
                    for c, w in enumerate(tiles):
                        if kind == "rw":
                            sc, dst = mu_mid[:, RC * b + c:RC * b + c + 1], zrw[:, RC * b + c, :]
                        elif kind == "lora":
                            sc, dst = mu_mid[0:w, 3 * RC + c:3 * RC + c + 1], zlora[0:w, c, :]
                        else:
                            col = rows["conv"] + TAPS // 2 * 3 * GH + 3 * b + c
                            sc, dst = par[:, col:col + 1], zgd[:, 3 * b + c, :]
                        last = a(dst, ps[4 * (i % 2) + c][0:w, 0:T], ACT.Copy, scale=sc)
                    last.then_inc(S["blk_scaled"], 1)
                act.wait_ge(S["blk_evac"], L * NB + 4)
                a(zlora[0:RD, 0, :], zlora[0:RD, 0, :], ACT.Tanh)
                a(zlora[0:RG, 1, :], zlora[0:RG, 1, :], ACT.Sigmoid).then_inc(S["lora_act"], 1)
                for j, nm in enumerate(("w0", "a0")):
                    for c in range(RC):
                        act.wait_ge(S["lora_psum"], L * 8 + (4 * j + c + 1))
                        for d in range(2):
                            col = rows[nm] + RC * d + c
                            last = a(swa[:, j, d, c, :], ps[4 * j + c][:, d * T:(d + 1) * T], ACT.Sigmoid,
                                     bias=par[:, col:col + 1])
                        last.then_inc(S["lora_ready"], 1)
                act.wait_ge(S["gate_psum"], L + 1)
                for t in range(NT):
                    last = a(sgate[:, t, :], ps[t][:, :], ACT.Copy)
                last.then_inc(S["gate_ready"], 1)
                with act.Fori(0, RC) as c:
                    n = act.snap(L * RC + c)
                    n2 = act.snap(n * 2)
                    m2 = act.snap(L * (2 * (RC + GP)) + c * 2)
                    act.wait_ge(S["rw_ssq"], n + 1)
                    rsqrt(ch[:, 3, :], ps[0][:, 0:T], 1.0, epsb[:, 0:1]).then_inc(S["rw_rn"], 1)
                    act.wait_ge(S["rw_vt"], n + 1)
                    a(mono(Vt[:, 0:2, :], 2), ps[1][:, 0:T], ACT.Copy).then_inc(S["rw_vtc"], 1)
                    for d in range(2):
                        act.wait_ge(S["rw_cs"], n2 + (d + 1))
                        a(ew[d][:, 0, :], cs[d][:, :], ACT.Exp, scale=-KAPPA)
                        a(ew[d][:, 1, :], cs[d][:, :], ACT.Exp, scale=KAPPA)
                        a(ew[d][:, 2, :], ew[d][:, 2, :], ACT.Exp, scale=-KAPPA)
                        a(mid[d][:, 3:4], mid[d][:, 2:3], ACT.Exp, scale=-KAPPA).then_inc(S["rw_exp"], 1)
                    t1(m2)
                    for src, dst, k, done in (("rw_u", uf, 0, "rw_uf"), ("rw_pv2", rf, 1, "rw_rf2"), ("rw_u2", uf, 1, "rw_uf2")):
                        for d in range(2):
                            bank = {"rw_u": ps[4 * d][:, 0:P], "rw_pv2": ps[4 * d + 2][:, 0:P], "rw_u2": ps[4 * d][:, P:2 * P]}[src]
                            act.wait_ge(S[src], n2 + (d + 1))
                            a(dst[d][:, k, :], bank, ACT.Copy).then_inc(S[done], 1)
                    act.wait_ge(S["rw_var"], n + 1)
                    rsqrt(st[:, 2, :], st[:, 1, :], 1.0 / 64, epsb[:, 1:2]).then_inc(S["rw_rstd"], 1)
                act.wait_ge(S["gd_sp"], L + 1)
                a(gpar[:, 1, :], gpar[:, 1, :], ACT.Exp)
                a(gx[:, 1, :, :], gx[:, 1, :, :], ACT.Exp, scale=-1.0)
                act.drain()
                a(gx[:, 1, :, :], gx[:, 1, :, :], ACT.Ln, bias=epsb[:, 2:3]).then_inc(S["gd_ln"], 1)
                act.wait_ge(S["gd_cumc"], L + 1)
                a(gates[:, 3, :, :], gates[:, 2, :, :], ACT.Exp)
                a(gates[:, 4, :, :], gates[:, 4, :, :], ACT.Exp)
                a(gates[:, 5, :, :], gates[:, 1, :, :], ACT.Exp).then_inc(S["gd_exp"], 1)
                a(zgd, zgd, ACT.Silu)
                a(zgt[:, :, 0:GW], zgt[:, :, 0:GW], ACT.Silu).then_inc(S["gd_silu"], 1)
                with act.Fori(0, GP) as i:
                    n = act.snap(L * GP + i)
                    n2 = act.snap(n * 2)
                    m2 = act.snap(L * (2 * (RC + GP)) + (i * 2 + 2 * RC))
                    act.wait_ge(S["gd_ssq"], n + 1)
                    for j in range(2):
                        a(mono(ewg[j], 2), ps[j][:, :], ACT.Ln, bias=epsb[:, 0:1])
                    act.drain()
                    for j in range(2):
                        last = a(ewg[j], ewg[j], ACT.Exp, scale=-0.5)
                    last.then_inc(S["gd_rn"], 1)
                    act.wait_ge(S["gd_vt"], n + 1)
                    a(mono(Vt, 4), ps[2][:, :], ACT.Copy).then_inc(S["gd_vtc"], 1)
                    act.wait_ge(S["gd_kt"], n + 1)
                    a(mono(OT, 4), ps[3][:, :], ACT.Copy).then_inc(S["gd_ktc"], 1)
                    for d in range(2):
                        act.wait_ge(S["gd_arg"], n2 + (d + 1))
                        a(scores[d][:, 0:2, :, :], scores[d][:, 0:2, :, :], ACT.Exp).then_inc(S["gd_d"], 1)
                    t1(m2)
                    for src, dst, lo, done in (("gd_u", ufg, 0, "gd_uf"), ("gd_us", KBt, T, "gd_usc")):
                        for d in range(2):
                            act.wait_ge(S[src], n2 + (d + 1))
                            a(mono(dst[d][:, :, :], 2), ps[4 * d][:, lo:lo + T], ACT.Copy).then_inc(S[done], 1)
                    act.wait_ge(S["gd_ss"], n + 1)
                    rsqrt(st[:, 2, :], st[:, 1, :], 1.0 / P, epsb[:, 0:1]).then_inc(S["gd_rstd"], 1)
                act.wait_ge(S["ml_x"], L + 1)
                a(gx[:, 1, :, :], gx[:, 0, :, :], ACT.Tanh, scale=1.0 / ML_GATE_CAP).then_inc(S["ml_tanh"], 1)
                act.wait_ge(S["ml_f"], L + 1)
                fg = gx[:, 1, :, 2 * MH:4 * MH]
                a(fg, fg, ACT.Exp, scale=-1.0)
                act.drain()
                a(fg, fg, ACT.Ln, bias=epsb[:, 2:3]).then_inc(S["ml_ln"], 1)
                a(zmt[:, :, MW:2 * MW], zmt[:, :, MW:2 * MW], ACT.Sigmoid).then_inc(S["ml_sig"], 1)
                act.wait_ge(S["ml_backc"], L + 1)
                a(gates[:, 2, :, :], gates[:, 1, :, :], ACT.Exp, scale=-1.0).then_inc(S["ml_expm"], 1)
                with act.Fori(0, MP) as i:
                    n = act.snap(L * MP + i)
                    n2 = act.snap(n * 2)
                    for d in range(2):
                        act.wait_ge(S["ml_arg"], n2 + (d + 1))
                        a(ml_flat(d), ml_flat(d), ACT.Exp, scale=-1.0).then_inc(S["ml_d"], 1)
                    act.wait_ge(S["ml_ss"], n + 1)
                    rsqrt(st[:, 2, :], st[:, 1, :], 1.0 / P, epsb[:, 0:1]).then_inc(S["ml_rstd"], 1)
                rms(L * 3 + 2)
                with act.Fori(0, NU) as i:
                    n = act.snap(L * NU + i)
                    sl = act.snap(L * SL + i * 8)
                    act.wait_ge(S["up_done"], n + 1)
                    for g in range(2):
                        act.wait_ge(S["slot_free"], sl + (RING + SL_UP + 4 * g + 4))
                        for c in range(4):
                            tap = rows["fconv"] + FTAPS // 2 * 2 * FT + FT * g + c
                            bias = rows["fbias"] + FT * g + c
                            last = a(up_buf(g)[:, c, :], ps[4 * g + c][:, 0:T], ACT.Identity, scale=par[:, ds(i * 4 + tap, 1)],
                                     bias=par[:, ds(i * 4 + bias, 1)])
                        last.then_inc(S["up_vact" if g else "up_gact"], 1)
                        if g == 0:
                            act.wait_ge(S["up_gconv"], n + 2)
                            a(up_buf(0), up_buf(0), ACT.Silu).then_inc(S["up_silu"], 1)
                rms(L * 3 + 3)
                for i in range(NO):
                    act.wait_ge(S["slot_free"], L * SL + (RING + SL_PLE + 4 * i + 4))
                    if i:
                        act.wait_ge(S["ple_done"], L * NO + i)
                    for t in range(NT):
                        last = a(mono(TN[t][:, :, :], 4), ps[4 * (i % 2) + t][:, :], ACT.Sigmoid)
                    last.then_inc(S["ple_sig"], 1)
            rms(3 * DEPTH + 1)

        @block.vector
        def _(v):
            v.wait_ge(S["consts"], 1)
            v.wait_ge(S["h_in"], 16 * NT)
            v.sem_inc(S["h_ready"], 1)
            MUL, ADD, SUB, MAX, MIN = ALU.mult, ALU.add, ALU.subtract, ALU.max, ALU.min

            def norm(q):
                v.wait_ge(S["rms_ready"], q)
                v.reciprocal(small[:, 4:4 + NT], small[:, 2:2 + NT])
                v.drain()
                for t in range(NT):
                    v.tensor_scalar(YB[:, t, :], H[:, t, :], small[:, 4 + t:5 + t], None, MUL).then_inc(S["u_ready"], 1)

            def norm_turned(q8, row):
                for t in range(NT):
                    for g in range(4):
                        v.wait_ge(S["ut_psum"], q8 + (4 * t + g + 1))
                        v.tensor_tensor(UT[:, 4 * g:4 * g + 4, t * P:(t + 1) * P], third(ps[4 * t + g][:, :], 4),
                                        bc(par[:, row + 4 * g:row + 4 * g + 4], P), MUL).then_inc(S["ut_ready"], 1)

            def add_taps(groups):
                for k in range(len(groups[0][2])):
                    for psum, z, taps in groups:
                        off, w = taps[k]
                        lo, hi = max(0, -off), T - max(0, off)
                        last = v.scalar_tensor_tensor(z[:, lo:hi], psum[:, lo + off:hi + off], w, z[:, lo:hi], MUL, ADD)
                    if k < len(groups[0][2]) - 1:
                        v.drain()
                return last

            def residual(slot0, kt, sl):
                for i in range(NO):
                    v.wait_ge(S["slot_free"], sl + (RING + slot0 + kt // KS * (i + 1)))
                    for t in range(NT):
                        hh = H[:, t, 512 * i:512 * i + 512]
                        last = v.tensor_tensor(hh, hh, ps[2 * i + t][:, :], ADD)
                last.then_inc(S["h_ready"], 1)

            def invert(m2, nt):
                for d in range(2):
                    v.tensor_tensor(TT[d][:, :, :], nt(d), bmid(lev[1 - d][:, 0, :], 4), MUL).then_inc(S["inv_t1"], 1)
                ml = v.snap(m2 * LEV)
                for lv in range(LEV):
                    for d in range(2):
                        v.wait_ge(S["inv_x"], ml + (2 * lv + d + 1))
                        v.tensor_tensor(XS[d][:, :, :], third(ps[4 * d][:, :], 4), bmid(lev[d][:, lv + 1, :], 4), MUL)\
                            .then_inc(S["inv_xs"], 1)
                    for d in range(2):
                        v.wait_ge(S["inv_t"], ml + (2 * lv + d + 1))
                        v.tensor_copy(mono(TT[d][:, :, :], 4), ps[4 * d + 2][:, :]).then_inc(S["inv_tt"], 1)

            def head_out(i, n, fam, gain, gate, col):
                v.drain()
                v.tensor_tensor(OT, OL, OL, MUL)
                v.drain()
                v.tensor_reduce(st[:, 1, :], OT, AX_X, ADD).then_inc(S[fam + "_ss"], 1)
                v.wait_ge(S[fam + "_rstd"], n + 1)
                v.tensor_tensor(OL, OL, bc(st[:, 2, :], P), MUL)
                v.drain()
                for h in range(2):
                    v.tensor_tensor(OL[:, 2 * h:2 * h + 2, :], OL[:, 2 * h:2 * h + 2, :], gain(h), MUL)
                v.drain()
                o4 = OL.rearrange("p (h t) c -> p h t c", h=2)
                for t in range(NT):
                    last = v.tensor_tensor(YB[:, t, ds(i * T + col, T)].rearrange("p (h c) -> p h c", h=2), o4[:, :, t, :],
                                           gate(t), MUL)
                last.then_inc(S[fam + "_done"], 1)

            with v.Fori(0, DEPTH) as L:
                sl = v.snap(L * SL)
                v.wait_ge(S["par_turned"], L + 1)
                v.tensor_copy(par[:, 0:4 * P], ps[0][:, :])
                v.tensor_copy(par[:, 4 * P:PT * P], ps[1][:, 0:(PT - 4) * P])
                v.drain().then_inc(S["row_free"], 1)
                for dst, m0, m1, k in ((0, rows["mu"], rows["mu"] + 3 * RC, 3 * RC), (3 * RC, rows["mu_wa"], rows["mu_wa"] + 1, 1),
                                       (3 * RC + 1, rows["mu_g"], rows["mu_g"] + 1, 1)):
                    v.tensor_tensor(mu_mid[:, dst:dst + k], par[:, m0:m0 + k], par[:, m1:m1 + k], ADD)
                v.drain()
                v.tensor_scalar(mu_mid[:, :], mu_mid[:, :], -1.0, 1.0, MUL, ADD).then_inc(S["par_ready"], 1)
                norm(L * 3 + 1)
                norm_turned(L * 24, rows["norm0"])
                for d in range(2):
                    v.memset(scores[d][:, :, :, :], 0.0)
                v.drain()
                for d in range(2):
                    v.tensor_copy(scores[d][:, :, 2, :], bmid(ident[:, :], 4))
                v.drain()
                nsc = 0
                NSC = sum(b[0] in ("rw", "lora", "gdq") for b in blocks)
                for i, (kind, b, c0, tiles) in enumerate(blocks):
                    g = 4 * (i % 2)
                    if kind in ("rw", "lora", "gdq"):
                        nsc += 1
                        v.wait_ge(S["blk_scaled"], L * NSC + nsc)
                        groups = []
                        for c, w in enumerate(tiles):
                            if kind == "gdq":
                                z = zgd[:, 3 * b + c, :]
                                cols = [(k - TAPS // 2, rows["conv"] + k * 3 * GH + 3 * b + c) for k in range(TAPS) if k != TAPS // 2]
                            elif kind == "rw":
                                z = zrw[:, RC * b + c, :]
                                cols = [(-1, rows["mu"] + RC * b + c), (1, rows["mu1"] + RC * b + c)]
                            else:
                                z = zlora[0:w, c, :]
                                m = rows[("mu_wa", "mu_g")[c]]
                                cols = [(-1, m), (1, m + 1)]
                            groups.append((ps[g + c][0:w, :], z, [(o_, par[0:w, m:m + 1]) for o_, m in cols]))
                        last = add_taps(groups)
                    else:
                        v.wait_ge(S["slot_free"], sl + (RING + SL_IN + 4 * i + 4))
                        if kind == "mlq":
                            for c in range(3):
                                last = v.tensor_copy(zmq[:, 3 * b + c, :], ps[g + c][:, 0:T])
                        else:
                            zt, w = (zgt, GT_W // 2) if kind == "gdt" else (zmt, MT_W // 4)
                            for t in range(NT):
                                last = v.tensor_copy(zt[:, t, w * b:w * b + w], ps[g + t][:, 0:w])
                    last.then_inc(S["blk_evac"], 1)

                with v.Fori(0, RC) as c:
                    v.wait_ge(S["gate_ready"], L + 1)
                    v.wait_ge(S["mixp_in"], L * MIXP_TOTAL + MIXP_TOTAL)
                    n = v.snap(L * RC + c)
                    n2 = v.snap(n * 2)
                    m2 = v.snap(L * (2 * (RC + GP)) + c * 2)
                    r_, k_, v_ = zrw[:, c, :], zrw[:, c + RC, :], zrw[:, c + 2 * RC, :]

                    def pcol(name):
                        return par[:, ds(c + rows[name], 1)]
                    v.tensor_copy(ch[:, 0, :], v_)
                    v.tensor_scalar(ch[:, 1, :], k_, pcol("k_k"), None, MUL)
                    v.drain()
                    v.tensor_tensor(ch[:, 2, :], ch[:, 1, :], ch[:, 1, :], MUL).then_inc(S["rw_sq"], 1)
                    for d in range(2):
                        sw = ew[d][:, 0, :]
                        v.tensor_copy(sw, swa[:, 0, d, c, :])
                        v.drain()
                        for t in range(NT):
                            o_, i_ = cs[d][:, t * P:(t + 1) * P], sw[:, t * P:(t + 1) * P]
                            if d:
                                o_, i_ = o_[:, ::-1], i_[:, ::-1]
                            v.tensor_tensor_scan(o_, i_, i_, 0.0, ADD, ALU.bypass)
                        v.drain()
                        v.tensor_copy(mid[d][:, 0:NT], cs[d][:, P // 2 - 1 + d:T:P])
                        v.drain()
                        for t in range(NT):
                            tt = cs[d][:, t * P:(t + 1) * P]
                            v.tensor_scalar(tt, tt, mid[d][:, t:t + 1], None, SUB)
                        v.drain()
                        F = FIRST[d]
                        e = F * P + LAST_COL[d]
                        v.tensor_tensor(mid[d][:, 2:3], cs[d][:, e:e + 1], mid[d][:, 1 - F:2 - F], ADD)
                        v.tensor_tensor(ew[d][:, 2, :], cs[d][:, :], sw, SUB).then_inc(S["rw_cs"], 1)
                    v.wait_ge(S["rw_rn"], n + 1)
                    v.tensor_tensor(ch[:, 4, :], ch[:, 1, :], ch[:, 3, :], MUL)
                    for d in range(2):
                        v.tensor_scalar(ch[:, 5, :], swa[:, 1, d, c, :], 1.0, pcol("k_a"), SUB, MUL)
                        v.drain()
                        v.scalar_tensor_tensor(KB[d][:, 0, :], ch[:, 5, :], 1.0, k_, ADD, MUL)
                        v.tensor_tensor(KB[d][:, 1, :], ch[:, 4, :], swa[:, 1, d, c, :], MUL)
                        v.drain()
                    v.tensor_tensor(ch[:, 3, :], KB[0][:, 0, :], KB[1][:, 0, :], ADD)
                    v.drain()
                    v.tensor_tensor(ch[:, 3, :], ch[:, 3, :], r_, MUL)
                    v.drain()
                    v.tensor_scalar(ch[:, 3, :], ch[:, 3, :], pcol("r_k"), None, MUL).then_inc(S["rw_cf"], 1)
                    for d in range(2):
                        v.wait_ge(S["rw_exp"], n2 + (d + 1))
                        v.tensor_tensor(KB[d][:, :, :], KB[d][:, :, :], bmid(ew[d][:, 1, :], 2), MUL)
                        v.scalar_tensor_tensor(AR[d][:, :, 0, :], third(ch[:, 4, :], 2), -1.0, third(ew[d][:, 2, :], 2), MUL, MUL)
                        v.tensor_tensor(AR[d][:, :, 1, :], third(r_, 2), third(ew[d][:, 0, :], 2), MUL).then_inc(S["rw_ops"], 1)
                    v.wait_ge(S["rw_coef"], n + 1)
                    v.tensor_copy(coef[:, :, :].rearrange("p t h -> p (t h)"), ps[0][:, 0:2 * NT]).then_inc(S["rw_coefc"], 1)
                    for d in range(2):
                        v.wait_ge(S["rw_sc"], n2 + (d + 1))
                        v.tensor_copy(st[:, 3, d:d + 1], ps[4 * d][:, 0:1])
                        for j in range(4):
                            last = v.copy_predicated(scores[d][:, j, :, :].rearrange("p a c -> p (a c)"),
                                                     pred[d][:, :, :].rearrange("p a c -> p (a c)").bitcast(I16), ps[4 * d + j][:, :])
                        last.then_inc(S["rw_masked"], 1)
                    v.drain()
                    for d in range(2):
                        v.wait_ge(S["rw_pv"], n2 + (d + 1))
                        v.tensor_copy(rf[d][:, 0, :], ps[4 * d + 3][:, 0:P])
                        v.tensor_copy(mono(KBt[d][:, :, :], 2), ps[4 * d + 3][:, T:2 * T]).then_inc(S["rw_rf"], 1)
                    invert(m2, lambda d: scores[d][:, :, 2, :])
                    for d in range(2):
                        v.wait_ge(S["rw_state"], n2 + (d + 1))
                        v.scalar_tensor_tensor(S0[d][:, 0, :], ps[4 * d + 1][:, 0:P], mid[d][:, 3:4], headones[:, :], MUL, MUL)\
                            .then_inc(S["rw_s0"], 1)
                    o2 = mono(OL[:, 0:2, :], 2)
                    v.wait_ge(S["rw_y"], n2 + 1)
                    v.tensor_copy(o2, ps[3][:, 0:T])
                    v.drain()
                    v.wait_ge(S["rw_y"], n2 + 2)
                    v.tensor_tensor(o2, o2, ps[7][:, 0:T], ADD)
                    v.drain()
                    h4 = o2.rearrange("p (g c) -> p g c", c=64)
                    t4 = mono(OT[:, 0:2, :], 2).rearrange("p (g c) -> p g c", c=64)
                    q4 = mono(OT[:, 2:4, :], 2).rearrange("p (g c) -> p g c", c=64)
                    v4 = mono(Vt[:, 0:2, :], 2).rearrange("p (g c) -> p g c", c=64)
                    v.tensor_reduce(st[:, 0, :], h4, AX_X, ADD)
                    v.drain()
                    v.tensor_scalar(st[:, 0, :], st[:, 0, :], 1.0 / 64, None, MUL)
                    v.drain()
                    v.tensor_tensor(t4, h4, bc(st[:, 0, :], 64), SUB)
                    v.drain()
                    v.tensor_tensor(q4, t4, t4, MUL)
                    v.drain()
                    v.tensor_reduce(st[:, 1, :], q4, AX_X, ADD).then_inc(S["rw_var"], 1)
                    v.tensor_tensor(h4, v4, bc(coef[:, :, :].rearrange("p t h -> p (t h)"), 64), MUL)
                    v.wait_ge(S["rw_rstd"], n + 1)
                    v.tensor_tensor(t4, t4, bc(st[:, 2, :], 64), MUL)
                    v.drain()
                    tt = OT[:, 0:2, :]
                    v.tensor_tensor(tt, tt, bmid(lnp[:, 0, ds(c * P, P)], 2), MUL)
                    v.drain()
                    v.tensor_tensor(tt, tt, bmid(lnp[:, 1, ds(c * P, P)], 2), ADD)
                    v.drain()
                    v.tensor_tensor(tt, tt, OL[:, 0:2, :], ADD)
                    v.drain()
                    v.tensor_tensor(YB[:, :, ds(c * P, P)], tt, sgate[:, :, ds(c * P, P)], MUL).then_inc(S["rw_done"], 1)

                NG = 2 * GH
                v.memset(V1[:, :, :, P:P + 1], 1.0)
                v.tensor_tensor(gx[:, 0, :, 0:NG], zgt[:, :, GW:GW + NG], bmid(gpar[:, 0, :], NT), ADD)
                v.tensor_scalar(gx[:, 0, :, NG:2 * NG], zgt[:, :, GW + NG:GW + 2 * NG], -1.0, None, MUL)
                v.drain()
                v.scalar_tensor_tensor(gx[:, 1, :, :], gx[:, 0, :, :], -1.0, gx[:, 0, :, :], MUL, MAX).then_inc(S["gd_sp"], 1)
                v.wait_ge(S["gd_ln"], L + 1)
                v.scalar_tensor_tensor(gx[:, 2, :, :], gx[:, 0, :, :], 0.0, gx[:, 1, :, :], MAX, ADD)
                v.drain()
                v.scalar_tensor_tensor(gates[:, 0, :, :], gx[:, 2, :, 0:NG], -1.0, bmid(gpar[:, 1, :], NT), MUL, MUL)
                v.tensor_scalar(gates[:, 1, :, :], gx[:, 2, :, NG:2 * NG], -1.0, None, MUL).then_inc(S["gd_gl"], 1)
                v.wait_ge(S["gd_cum"], L + 1)
                v.tensor_copy(gates[:, 2, :, :].rearrange("p t g -> p (t g)"), ps[0][:, 0:NT * NG])
                v.drain()
                v.tensor_tensor(gates[:, 4, :, :].rearrange("p t g -> p (t g)"), ps[0][:, 64:64 + NT * NG],
                                gates[:, 2, :, :].rearrange("p t g -> p (t g)"), SUB).then_inc(S["gd_cumc"], 1)
                gflat = gates[:, :, :, :].rearrange("p k t g -> p (k t g)").rearrange("p (a h) -> p a h", h=GH)
                with v.Fori(0, GP) as i:
                    v.wait_ge(S["gd_exp"], L + 1)
                    v.wait_ge(S["gd_silu"], L + 1)
                    n = v.snap(L * GP + i)
                    n2 = v.snap(n * 2)
                    m2 = v.snap(L * (2 * (RC + GP)) + (i * 2 + 2 * RC))
                    q_, k_, v_ = (zgd[:, ds(i * 2 + GH * j, 2), :] for j in range(3))
                    v.tensor_copy(gs[:, :, :], gflat[:, :, ds(i * 2, 2)])
                    v.tensor_copy(chg, v_)
                    v.tensor_tensor(KB[0][:, :, :], q_, q_, MUL)
                    v.tensor_tensor(KB[1][:, :, :], k_, k_, MUL).then_inc(S["gd_sq"], 1)
                    v.wait_ge(S["gd_rn"], n + 1)
                    for h in range(2):
                        kh, qh = zgd[:, i * 2 + (GH + h), :], zgd[:, i * 2 + h, :]
                        v.tensor_tensor(AR[h][:, :, 0, :], third(kh, 2), third(ewg[1][:, h, :], 2), MUL)
                        last = v.scalar_tensor_tensor(AR[h][:, :, 1, :], third(qh, 2), P ** -0.5, third(ewg[0][:, h, :], 2), MUL, MUL)
                    last.then_inc(S["gd_qk"], 1)
                    for d in range(2):
                        v.wait_ge(S["gd_gb"], n2 + (d + 1))
                        for j in range(2):
                            for h in range(2):
                                for t in range(NT):
                                    u = 2 * h + t
                                    last = v.tensor_scalar(scores[d][:, j, u, :], ps[4 * d + j][:, u * P:(u + 1) * P],
                                                           gs[:, 8 + 2 * t + d, h:h + 1], 0.0, SUB, MIN)
                        last.then_inc(S["gd_arg"], 1)
                    v.wait_ge(S["gd_sc"], n + 1)
                    for d in range(2):
                        v.wait_ge(S["gd_dm"], n2 + (d + 1))
                        for h in range(2):
                            pp = ps[6 + h][:, :].rearrange("p (t j c) -> p t j c", t=2, j=2)
                            for j in range(2):
                                v.tensor_tensor(scores[d][:, 2 + j, 2 * h:2 * h + 2, :], pp[:, :, j, :],
                                                scores[d][:, j, 2 * h:2 * h + 2, :], MUL)
                        v.drain()
                        v.tensor_tensor(scores[d][:, 2, :, :], scores[d][:, 2, :, :], bmid(ident[:, :], 4), ADD)\
                            .then_inc(S["gd_nt"], 1)
                    v.drain()
                    invert(m2, lambda d: scores[d][:, 2, :, :])
                    v.wait_ge(S["gd_vtc"], n + 1)
                    v.wait_ge(S["gd_ktc"], n + 1)
                    for d in range(2):
                        F = FIRST[d]
                        for h in range(2):
                            for t in range(NT):
                                v.tensor_scalar(TN[d][:, 2 * h + t, :], Vt[:, 2 * h + t, :], gs[:, 20 + 2 * t + d, h:h + 1], None, MUL)
                            v.tensor_scalar(XS[d][:, h, :], OT[:, 2 * h + F, :], gs[:, 16 + 2 * F + d, h:h + 1], None, MUL)
                        v.scalar_tensor_tensor(gs[:, 4 + d:8 + d:2, :], gs[:, 20 + d:24:2, :], -1.0, gs[:, 12 + d:16:2, :], MUL, MUL)\
                            .then_inc(S["gd_rhs"], 1)
                    for d in range(2):
                        v.wait_ge(S["gd_state"], n2 + (d + 1))
                        v.tensor_copy(mono(S0g[d], 2), ps[4 * d + 1][:, 0:T]).then_inc(S["gd_s0"], 1)
                    for d in range(2):
                        B = 1 - FIRST[d]
                        v.wait_ge(S["gd_ks"], n2 + (d + 1))
                        for h in range(2):
                            v.scalar_tensor_tensor(rf[d][:, h, :], ps[4 * d + 2][:, h * P:(h + 1) * P], gs[:, 4 + 2 * B + d, h:h + 1],
                                                   TN[d][:, 2 * h + B, :], MUL, ADD)
                            last = v.tensor_scalar(XS[d][:, 2 + h, :], ps[4 * d + 2][:, (2 + h) * P:(3 + h) * P],
                                                   gs[:, 12 + 2 * B + d, h:h + 1], None, MUL)
                        last.then_inc(S["gd_rs"], 1)
                    o4 = OL.rearrange("p (h t) c -> p h t c", h=2)
                    for d in range(2):
                        v.wait_ge(S["gd_y"], n2 + (d + 1))
                        if d == 0:
                            v.tensor_copy(mono(OL, 4), ps[3][:, :])
                        else:
                            v.tensor_tensor(mono(OL, 4), mono(OL, 4), ps[7][:, :], ADD)
                        v.drain()
                        ob = o4[:, :, 1 - FIRST[d], :]
                        v.tensor_tensor(ob, ob, XS[d][:, 2:4, :], ADD)
                        v.drain()
                    head_out(i, n, "gd", lambda h: bmid(gdn[:, :], 2),
                             lambda t: zgt[:, t, ds(i * T, T)].rearrange("p (h c) -> p h c", h=2), RW)

                NM = 2 * MH
                for j in range(2):
                    last = v.tensor_tensor(gx[:, 0, :, NM * j:NM * (j + 1)], zmt[:, :, 2 * MW + NM * j:2 * MW + NM * (j + 1)],
                                           bmid(gpar[:, 2 + j, :], NT), ADD)
                last.then_inc(S["ml_x"], 1)
                v.wait_ge(S["ml_tanh"], L + 1)
                v.tensor_scalar(gx[:, 0, :, 0:NM], gx[:, 1, :, 0:NM], ML_GATE_CAP, None, MUL)
                v.tensor_scalar(gx[:, 0, :, NM:2 * NM], gx[:, 1, :, NM:2 * NM], -ML_GATE_CAP, None, MUL)
                v.drain()
                fy = gx[:, 0, :, NM:2 * NM]
                v.scalar_tensor_tensor(gx[:, 1, :, NM:2 * NM], fy, -1.0, fy, MUL, MAX).then_inc(S["ml_f"], 1)
                v.wait_ge(S["ml_ln"], L + 1)
                v.scalar_tensor_tensor(fy, fy, 0.0, gx[:, 1, :, NM:2 * NM], MAX, ADD)
                v.drain()
                v.tensor_scalar(fy, fy, -1.0, None, MUL).then_inc(S["ml_g"], 1)
                v.wait_ge(S["ml_rt"], L + 1)
                lf_r, F_r, e_r, M_r, m_r = (mono(b_[0:MH, :, :], 4) for b_ in (XS[0], XS[1], TN[0], TN[1], TT[0]))
                v.tensor_copy(lf_r, ps[1][0:MH, :])
                v.drain()

                def halves(ap):
                    return ap[:, 0:T], ap[:, T:2 * T][:, ::-1]
                for o_, i_ in zip(halves(F_r), halves(lf_r)):
                    v.tensor_tensor_scan(o_, i_, i_, 0.0, ADD, ALU.bypass)
                v.drain()
                v.tensor_tensor(e_r, ps[0][0:MH, :], F_r, SUB)
                v.drain()
                for o_, i_ in zip(halves(M_r), halves(e_r)):
                    v.tensor_tensor_scan(o_, i_, i_, 0.0, MAX, ALU.bypass)
                v.drain()
                v.tensor_tensor(m_r, F_r, M_r, ADD).then_inc(S["ml_rows"], 1)
                v.wait_ge(S["ml_back"], L + 1)
                v.tensor_copy(gates[:, 0:2, :, :].rearrange("p k t g -> p (k t g)"), ps[2][:, 0:8 * MH]).then_inc(S["ml_backc"], 1)
                with v.Fori(0, MP) as i:
                    v.wait_ge(S["ml_expm"], L + 1)
                    v.wait_ge(S["ml_sig"], L + 1)
                    v.wait_ge(S["mln_in"], L * 16 + 16)
                    n = v.snap(L * MP + i)
                    n2 = v.snap(n * 2)
                    v.tensor_copy(gs[:, 0:12, :], gflat[:, 0:12, ds(i * 2, 2)])
                    v.tensor_scalar(KB[0][:, 0, :], zmq[:, i, :], 64 ** -0.5, None, MUL)
                    v.tensor_copy(KB[0][:, 1, :], zmq[:, i + MP, :])
                    for j in range(NT):
                        v.tensor_copy(V1[:, j, :, 0:P], zmt[:, j, ds(i * T, T)].rearrange("p (h c) -> p h c", h=2))
                    v.tensor_copy(small[0:MH, 8:10], ident[0:MH, ds(i * 2, 2)]).then_inc(S["ml_in"], 1)
                    v.drain()
                    for d in range(2):
                        v.wait_ge(S["ml_mb"], n2 + (d + 1))
                        for h in range(2):
                            for j in range(NT):
                                last = v.tensor_scalar(ml_flat(d)[:, h, j, :], ps[4 + d][:, h * T:(h + 1) * T],
                                                       gs[:, 2 * d + j, h:h + 1], 0.0, SUB, MAX)
                        last.then_inc(S["ml_arg"], 1)
                    v.wait_ge(S["ml_sc"], n + 1)
                    for d in range(2):
                        v.wait_ge(S["ml_dm"], n2 + (d + 1))
                        for h in range(2):
                            w = ml_flat(d)[:, h, :, :].rearrange("p j t -> p (j t)")
                            last = v.tensor_tensor(w, w, ps[h][:, :], MUL)
                        last.then_inc(S["ml_p"], 1)
                    o4 = OL.rearrange("p (h t) c -> p h t c", h=2)
                    for d in range(2):
                        v.wait_ge(S["ml_num"], n2 + (d + 1))
                        nd = [ps[4 * d + 2 + h][:, 0:2 * (P + 1)].rearrange("p (t c) -> p t c", t=2) for h in range(2)]
                        for h in range(2):
                            v.tensor_scalar(st[:, 3, 2 * h:2 * h + 2], nd[h][:, :, P], -1.0, None, MUL)
                        v.drain()
                        for h in range(2):
                            v.tensor_tensor(st[:, 0, 2 * h:2 * h + 2], nd[h][:, :, P], st[:, 3, 2 * h:2 * h + 2], MAX)
                        v.drain()
                        for h in range(2):
                            v.tensor_tensor(st[:, 0, 2 * h:2 * h + 2], st[:, 0, 2 * h:2 * h + 2], gs[:, 8 + 2 * d:10 + 2 * d, h], MAX)
                        v.drain()
                        v.reciprocal(st[:, 0, :], st[:, 0, :])
                        v.drain()
                        dst = OL if d == 0 else OT
                        for h in range(2):
                            v.tensor_tensor(dst[:, 2 * h:2 * h + 2, :], nd[h][:, :, 0:P], bc(st[:, 0, 2 * h:2 * h + 2], P), MUL)
                        v.drain()
                    v.tensor_tensor(OL, OL, OT, ADD)
                    head_out(i, n, "ml", lambda h: bmid(mln[:, ds(i * T + h * P, P)], 2),
                             lambda t: zmt[:, t, ds(i * T + MW, T)].rearrange("p (h c) -> p h c", h=2), RW + GW)
                v.drain().then_inc(S["mixp_free"], 1)

                for j in range(8):
                    t, g = j // 4, j % 4
                    v.wait_ge(S["yt_psum"], L * 8 + (j + 1))
                    v.tensor_copy(UT[:, 4 * g:4 * g + 4, t * P:(t + 1) * P], third(ps[j][:, :], 4)).then_inc(S["yt_ready"], 1)
                residual(SL_OUT, KT, sl)
                norm(L * 3 + 2)
                norm_turned(L * 24 + 8, rows["norm1"])
                with v.Fori(0, NU) as i:
                    n = v.snap(L * NU + i)
                    for g in range(2):
                        v.wait_ge(S["up_vact" if g else "up_gact"], n + 1)
                        groups = []
                        for c in range(4):
                            taps = [(k - FTAPS // 2, par[:, ds(i * 4 + (rows["fconv"] + k * 2 * FT + FT * g + c), 1)])
                                    for k in range(FTAPS) if k != FTAPS // 2]
                            groups.append((ps[4 * g + c], up_buf(g)[:, c, :], taps))
                        last = add_taps(groups)
                        if g == 0:
                            last.then_inc(S["up_gconv"], 1)
                    v.drain()
                    v.wait_ge(S["up_silu"], n + 1)
                    v.tensor_tensor(gT[:, ds(i * 4, 4), :], up_buf(0), up_buf(1), MUL).then_inc(S["up_done"], 1)
                residual(SL_DOWN, FT, sl)
                norm(L * 3 + 3)
                norm_turned(L * 24 + 16, rows["norm2"])
                v.wait_ge(S["p_turned"], L + 1)
                v.tensor_copy(pT[:, :, :].rearrange("p k t -> p (k t)"), ps[7][:, :])
                v.drain().then_inc(S["pt_ready"], 1)
                for i in range(NO):
                    v.wait_ge(S["ple_sig"], L * NO + (i + 1))
                    v.wait_ge(S["ple_psum"], L * NO + (i + 1))
                    for t in range(NT):
                        s_ = mono(TN[t][:, :, :], 4)
                        v.tensor_tensor(s_, s_, ps[4 * (i % 2) + 2 + t][:, :], MUL)
                    v.drain()
                    for t in range(NT):
                        hh = H[:, t, 512 * i:512 * i + 512]
                        last = v.tensor_tensor(hh, hh, mono(TN[t][:, :, :], 4), ADD)
                    last.then_inc(S["ple_done"], 1)
                v.drain().then_inc(S["h_ready"], 1)
            v.wait_ge(S["rms_ready"], 3 * DEPTH + 1)
            v.reciprocal(small[:, 4:4 + NT], small[:, 2:2 + NT])
            v.wait_ge(S["nf_in"], 16)
            v.drain()
            for t in range(NT):
                v.scalar_tensor_tensor(YB[:, t, :], H[:, t, :], small[:, 4 + t:5 + t], Z[:, 0:D], MUL, MUL).then_inc(S["fin_out"], 1)


_INS = ["x", "p", "norm_mix", "w_in", "rw_shift_mu", "rw_w0", "rw_w2", "rw_a0", "rw_a2", "rw_g2", "rw_k_k", "rw_k_a",
        "rw_r_k", "rw_ln_g", "rw_ln_b", "gd_conv_w", "gd_a_log", "gd_dt_bias", "gd_norm_g", "ml_i_bias", "ml_f_bias",
        "ml_norm_g", "w_out", "norm_ffn", "w_up", "ffn_conv_w", "ffn_conv_b", "w_down", "norm_ple", "w_ple_gate",
        "w_ple_proj", "norm_final"]


def kernel(**inputs):
    import numpy as _np
    import concourse.bacc as _bacc
    from concourse import mybir as _mybir
    from concourse.bass_utils import run_bass_kernel_spmd as _run

    nc = _bacc.Bacc("TRN2", target_bir_lowering=False, num_devices=1)
    arrays, args = {}, []
    for name in _INS:
        a = _np.ascontiguousarray(inputs[name])
        arrays[f"in_{name}_dram"] = a
        args.append(nc.dram_tensor(f"in_{name}_dram", a.shape, _mybir.dt.from_np(a.dtype), kind="ExternalInput").ap())
    shape = _np.asarray(inputs["x"]).shape
    args.append(nc.dram_tensor("out_0_dram", shape, _mybir.dt.float32, kind="ExternalOutput").ap())
    trunk(nc, *args)
    r = _run(nc, [arrays], core_ids=[0])
    return r.results[0]["out_0_dram"]
```

```python
from contextlib import ExitStack
import math

import concourse.bass as bass
from concourse import mybir
from concourse.bass import ds

F32 = mybir.dt.float32
F32R = mybir.dt.float32r
BF16 = mybir.dt.bfloat16
I16 = mybir.dt.int16
ALU = mybir.AluOpType
ACT = mybir.ActivationFunctionType
AX_X = mybir.AxisListType.X

P = 128
EPS = 1e-6
RW_LN_EPS = 64e-5
ML_GATE_CAP = 15.0
KAPPA = math.exp(-0.5)


def trunk(nc, x, p, norm_mix, w_in, rw_shift_mu, rw_w0, rw_w2, rw_a0, rw_a2, rw_g2, rw_k_k, rw_k_a,
          rw_r_k, rw_ln_g, rw_ln_b, gd_conv_w, gd_a_log, gd_dt_bias, gd_norm_g, ml_i_bias, ml_f_bias,
          ml_norm_g, w_out, norm_ffn, w_up, ffn_conv_w, ffn_conv_b, w_down, norm_ple, w_ple_gate,
          w_ple_proj, norm_final, out):
    DEPTH, D, N_IN = w_in.shape
    T = x.shape[1]
    NT = T // P
    KT = D // P
    RW = rw_w0.shape[2]
    RC = RW // P
    RD, RG = rw_w2.shape[2], rw_g2.shape[1]
    GH = gd_a_log.shape[2]
    GW = GH * P
    MH = ml_i_bias.shape[2]
    MW = MH * P
    GP, MP = GH // 2, MH // 2
    TAPS, FTAPS = gd_conv_w.shape[1], ffn_conv_w.shape[1]
    FF = w_down.shape[1]
    FT = FF // P
    PLE = p.shape[3]
    assert NT == 2 and rw_a2.shape[2] == RD and 2 * RD <= 64 and GH % 2 == 0 and MH % 2 == 0

    RING, KS = 4, 2
    KSLOTS = KT // KS
    RW_C0, GQ_C0 = 0, 3 * RW + 2 * RD + RG
    GT_C0 = GQ_C0 + 3 * GW
    MQ_C0 = GT_C0 + GW + 4 * GH
    MT_C0 = MQ_C0 + MH * P
    GT_W, MT_W = GW + 4 * GH, 2 * MW + 4 * MH
    assert MT_C0 + MT_W == N_IN
    blocks = [("rw", b, RW_C0 + RW * b, [P] * RC) for b in range(3)]
    blocks += [("lora", 0, 3 * RW, [2 * RD, RG])]
    blocks += [("gdq", b, GQ_C0 + 3 * P * b, [P] * 3) for b in range(3 * GH // 3)]
    blocks += [("gdt", b, GT_C0 + GT_W // 2 * b, None) for b in range(2)]
    blocks += [("mlq", b, MQ_C0 + 3 * P * b, [P] * 3) for b in range(MH // 3)]
    blocks += [("mlt", b, MT_C0 + MT_W // 4 * b, None) for b in range(4)]
    NB = len(blocks)

    def width(block):
        if block[0] == "lora":
            return 2 * RD + P
        return sum(block[3]) if block[3] else (GT_W // 2 if block[0] == "gdt" else MT_W // 4)

    NO = D // 512
    NU = FT // 4
    SL_IN = 0
    SL_OUT = SL_IN + KSLOTS * NB
    SL_UP = SL_OUT + KSLOTS * NO
    SL_DOWN = SL_UP + 2 * KSLOTS * NU
    SL_PLE = SL_DOWN + NO * FT // KS
    SL = SL_PLE + KSLOTS * NO
    AHEAD = RING - 1

    def slot_width(slot):
        return width(blocks[slot // KSLOTS]) if slot < SL_OUT else 512
    assert SL % RING == 0 and all(s % RING == 0 for s in (SL_OUT, SL_UP, SL_DOWN, SL_PLE, 2 * KSLOTS))

    rows, NR = {}, 0
    for name, n in (("norm0", KT), ("norm1", KT), ("norm2", KT), ("mu", 6 * RC), ("w0", 2 * RC), ("a0", 2 * RC),
                    ("k_k", RC), ("k_a", RC), ("r_k", RC), ("conv", TAPS * 3 * GH), ("fconv", FTAPS * 2 * FT),
                    ("fbias", 2 * FT), ("mu_wa", 2), ("mu_g", 2)):
        rows[name] = NR
        NR += n
    PT = -(-NR // P)

    with ExitStack() as ctx:
        def mono(ap, k=None):
            return ap.rearrange("p a c -> p (a c)")

        def sem(name):
            return ctx.enter_context(nc.semaphore(name))

        place = nc.sbuf_base // 32 * 32 + 32

        def at(name, shape, offset, dt=F32):
            return nc.alloc_sbuf_tensor_at(name, shape, dt, offset=offset)

        def sb(name, shape, dt=F32):
            nonlocal place
            tensor = at(name, shape, place, dt)
            place += -(-math.prod(shape[1:]) * (2 if dt == BF16 else 4) // 32) * 32
            return tensor

        H = sb("H", [P, NT, D])
        ring = sb("ring", [P, RING, KS, 512])
        whi = sb("whi", [P, RING, KS, 512], F32R)
        wlo = sb("wlo", [P, RING, KS, 512], F32R)
        u_place = place
        uhi = sb("uhi", [P, KT, T], F32R)
        ulo = sb("ulo", [P, KT, T], F32R)
        UA = at("UA", [P, KT, T], u_place)
        swa = UA[:, :, :].rearrange("p (k c d) t -> p k d c t", k=2, d=2)
        sc1_place = u_place + 4 * KT * T

        par = sb("par", [P, PT * P])
        mu_mid = sb("mu_mid", [P, 3 * RC + 2])
        lnp = sb("lnp", [P, 2, RW])
        gdn = sb("gdn", [P, P])
        gpar = sb("gpar", [P, 4, 2 * GH])
        ident = sb("ident", [P, P])
        ones = sb("ones", [P, P])
        headones = sb("headones", [P, P])
        incl = [sb(f"incl{d}", [P, P]) for d in range(2)]
        negstrict = [sb(f"negstrict{d}", [P, P]) for d in range(2)]
        LEVELS = 7
        lev = [sb(f"lev{d}", [P, LEVELS, P], BF16) for d in range(2)]
        pred = [sb(f"pred{d}", [P, 4, P], BF16) for d in range(2)]
        one_h = sb("one_h", [P, P], BF16)
        epsb = sb("epsb", [P, 4])
        small = sb("small", [P, 16])
        heads = sb("heads", [P, 12, P])
        OL, OT, Vt = heads[:, 0:4, :], heads[:, 4:8, :], heads[:, 8:12, :]
        prow = heads[:, 0:PT, :]
        pin = mono(heads[:, PT:PT + NT * PLE // P, :]).rearrange("p (t c) -> p t c", t=NT)
        coef = sb("coef", [P, NT, 2])
        st = sb("st", [P, 4, 4])
        mid = [sb(f"mid{d}", [P, 4]) for d in range(2)]
        gates = sb("gates", [P, 6, NT, 2 * GH])
        gs = sb("gs", [P, 24, 2])
        gx = sb("gx", [P, 3, NT, 4 * GH])

        arena = place
        g_bytes = 4 * FT * T
        ghi = at("ghi", [P, FT, T], arena, F32R)
        glo = at("glo", [P, FT, T], arena + g_bytes, F32R)
        zwords = RC * 3 * T + 2 * T + 3 * GH * T + NT * GT_W + MH * T + NT * MT_W
        Z = sb("Z", [P, zwords])
        scores = [sb("scores0", [P, 4, 4, P]), at("scores1", [P, 4, 4, P], sc1_place)]
        TN = [sb(f"TN{d}", [P, 4, P]) for d in range(2)]
        TT = [sb(f"TT{d}", [P, 4, P]) for d in range(2)]
        XS = [sb(f"XS{d}", [P, 4, P]) for d in range(2)]
        AR = [at(f"AR{d}", [P, NT, 2, P], sc1_place + 8192 + 2048 * d) for d in range(2)]
        KB = [at(f"KB{d}", [P, 2, T], sc1_place + 12288 + 2048 * d) for d in range(2)]
        KBt = [sb(f"KBt{d}", [P, 2, P]) for d in range(2)]
        rf = [sb(f"rf{d}", [P, 2, P]) for d in range(2)]
        cs = [sb(f"cs{d}", [P, T]) for d in range(2)]
        sgate = sb("sgate", [P, NT, RW])
        YB = sb("YB", [P, NT, D])
        assert arena + 2 * g_bytes <= place - 8 * D + 4 * RW
        projw = YB[:, :, :].rearrange("p k n -> p (k n)").rearrange("p (k n) -> p k n", k=PLE // P)
        o = 0

        def zpart(n):
            nonlocal o
            o += n
            return Z[:, o - n:o]
        zrw = zpart(3 * RC * T).rearrange("p (c t) -> p c t", t=T)
        zlora = zpart(2 * T).rearrange("p (c t) -> p c t", t=T)
        zgd = zpart(3 * GH * T).rearrange("p (c t) -> p c t", t=T)
        zgt = zpart(NT * GT_W).rearrange("p (t c) -> p t c", t=NT)
        zmq = zpart(MH * T).rearrange("p (c t) -> p c t", t=T)
        zmt = zpart(NT * MT_W).rearrange("p (t c) -> p t c", t=NT)

        w2sb = YB[0:2 * RD, 0, RW:3 * RW].rearrange("p (d c) -> p d c", d=2)
        g2sb = YB[0:RG, 1, RW:2 * RW]
        ew = [YB[:, 1, RW + 3 * T * d:RW + 3 * T * (d + 1)].rearrange("p (k t) -> p k t", k=3) for d in range(2)]
        ch = YB[:, 0, RW:RW + 6 * T].rearrange("p (k t) -> p k t", k=6)
        chg = UA[:, 0:2, :]
        ewg = [UA[:, 2 + 2 * j:4 + 2 * j, :] for j in range(2)]
        mln = UA[:, 6:9, :].rearrange("p k t -> p (k t)")[:, 0:MW]
        V1 = UA[:, 9:12, :].rearrange("p k t -> p (k t)")[:, 0:NT * 2 * (P + 2)]\
            .rearrange("p (j h c) -> p j h c", j=NT, h=2)
        uf = [XS[d][:, 2:4, :] for d in range(2)]
        S0 = [XS[d][:, 0:2, :] for d in range(2)]
        ufg = [scores[d][:, 0, 2:4, :] for d in range(2)]
        S0g = [scores[d][:, 0, 0:2, :] for d in range(2)]
        pT = XS[0][:, :, :].rearrange("p a c -> p (a c)").rearrange("p (k t) -> p k t", t=T)

        ps = [ctx.enter_context(nc.psum_tensor(f"ps{i}", [P, 512], F32)) for i in range(8)]


        NAMES = """consts h_in rows_in mixp_in pin_in proj_in nf_in row_free mixp_free w2_in mln_in
            landed0 landed1 landed2 landed3 hi_ready lo_ready slot_done par_turned par_ready h_ready rms_ready u_ready ut_psum ut_hi ut_ready
            blk_scaled blk_evac lora_act lora_psum lora_ready gate_psum gate_ready
            rw_sq rw_ssq rw_rn rw_vt rw_vtc rw_cs rw_exp rw_cf rw_coef rw_coefc rw_ops rw_sc rw_masked rw_pv rw_rf
            inv_t1 inv_t1p inv_tn1 inv_x inv_xs inv_t inv_tn inv_tt
            rw_u rw_uf rw_state rw_s0 rw_pv2 rw_rf2 rw_u2 rw_uf2 rw_y rw_yc rw_var rw_rstd rw_done
            gd_sp gd_ln gd_gl gd_cum gd_cumc gd_exp gd_silu gd_sq gd_ssq gd_rn gd_vt gd_vtc gd_qk gd_kt gd_ktc gd_sc
            gd_gb gd_arg gd_d gd_dm gd_nt gd_rhs gd_u gd_uf gd_state gd_s0 gd_ks gd_rs gd_us gd_usc gd_y gd_yc
            gd_ss gd_rstd gd_done
            ml_x ml_tanh ml_f ml_ln ml_g ml_rt ml_rows ml_back ml_backc ml_expm ml_sig ml_in ml_sc ml_mb ml_arg ml_d
            ml_dm ml_p ml_num ml_numc ml_ss ml_rstd ml_done
            yt_psum yt_hi yt_ready up_gact up_gconv up_silu up_vact up_vconv up_done p_turned pt_ready ple_psum ple_sig ple_done
            fin_out out_done""".split()
        S = {n: sem(n) for n in NAMES}

        block = ctx.enter_context(nc.Block())
        FIRST = (0, NT - 1)
        LAST_COL = (P - 1, 0)
        LEV = LEVELS - 1

        def bc(ap, n):
            return ap.unsqueeze(2).to_broadcast([ap.shape[0], ap.shape[1], n])

        def bmid(ap, n):
            return ap.unsqueeze(1).to_broadcast([ap.shape[0], n, ap.shape[1]])

        w_in_v = w_in.rearrange("l (k p) n -> l p k n", p=P)
        w_out_v = w_out.rearrange("l (k p) n -> l p k n", p=P)
        w_up_v = w_up.rearrange("l (k p) n -> l p k n", p=P)
        w_down_v = w_down.rearrange("l (k p) n -> l p k n", p=P)
        w_pg_v = w_ple_gate.rearrange("l (k p) n -> l p k n", p=P)


        ROW_SRC = (("norm0", lambda L: norm_mix[L].rearrange("(c p) -> c p", p=P), KT),
                   ("norm1", lambda L: norm_ffn[L].rearrange("(c p) -> c p", p=P), KT),
                   ("norm2", lambda L: norm_ple[L].rearrange("(c p) -> c p", p=P), KT),
                   ("mu", lambda L: rw_shift_mu[L, 0, 0:3 * RW].rearrange("(c p) -> c p", p=P), 3 * RC),
                   ("mu1", lambda L: rw_shift_mu[L, 1, 0:3 * RW].rearrange("(c p) -> c p", p=P), 3 * RC),
                   ("w0", lambda L: rw_w0[L].rearrange("d (c p) -> (d c) p", p=P), 2 * RC),
                   ("a0", lambda L: rw_a0[L].rearrange("d (c p) -> (d c) p", p=P), 2 * RC),
                   ("k_k", lambda L: rw_k_k[L].rearrange("(c p) -> c p", p=P), RC),
                   ("k_a", lambda L: rw_k_a[L].rearrange("(c p) -> c p", p=P), RC),
                   ("r_k", lambda L: rw_r_k[L].rearrange("(c h) j -> c (h j)", h=2), RC),
                   ("conv", lambda L: gd_conv_w[L].rearrange("k (c p) -> (k c) p", p=P), TAPS * 3 * GH),
                   ("fconv", lambda L: ffn_conv_w[L].rearrange("k (c p) -> (k c) p", p=P), FTAPS * 2 * FT),
                   ("fbias", lambda L: ffn_conv_b[L].rearrange("(c p) -> c p", p=P), 2 * FT),
                   ("mu_wa", lambda L: rw_shift_mu[L, :, 3 * RW:3 * RW + 2 * RD], 2),
                   ("mu_g", lambda L: rw_shift_mu[L, :, 3 * RW + 2 * RD:3 * RW + 2 * RD + RG], 2))
        rows["mu1"] = rows["mu"] + 3 * RC

        def row_pieces():
            for name, src, n in ROW_SRC:
                r, done = rows[name], 0
                while done < n:
                    k = min(n - done, P - (r + done) % P)
                    yield done, (r + done) // P, (r + done) % P, k, src
                    done += k
        ROWS_TOTAL = 16 * len(list(row_pieces()))

        def mixer_params(L):
            yield lnp[:, 0, :], rw_ln_g[L].partition_broadcast(P)
            yield lnp[:, 1, :], rw_ln_b[L].partition_broadcast(P)
            yield gdn[:, :], gd_norm_g[L].partition_broadcast(P)
            for i, src in enumerate((gd_dt_bias, gd_a_log, ml_i_bias, ml_f_bias)):
                yield gpar[:, i, :], src[L].rearrange("d h -> (d h)").partition_broadcast(P)
        MIXP_TOTAL = 16 * len(list(mixer_params(0)))

        def ml_flat(d):
            return scores[d][:, :, :, :].rearrange("p a b c -> p (a b c)")[:, 0:4 * T]\
                .rearrange("p (h j t) -> p h j t", h=2, j=2)

        def ml_diag(d):
            flat = scores[d][:, :, :, :].rearrange("p a b c -> p (a b c)")
            return [flat[:, h * 2 * T:(h + 1) * 2 * T].rearrange("p (u c) -> p u c", c=P)[:, 0:4:3, :] for h in range(2)]

        def third(ap, k):
            return ap.rearrange("p (k c) -> p k c", k=k)

        def up_buf(g):
            return YB[:, 1, 4 * T * g:4 * T * (g + 1)].rearrange("p (c t) -> p c t", t=T)

        @block.sync
        def _(sp):
            for t in range(NT):
                sp.dma_start(H[:, t, :], x[0, t * P:(t + 1) * P, :]).then_inc(S["h_in"], 16)
            with sp.Fori(0, DEPTH) as L:
                base = sp.snap(L * SL)

                def load(slot, src, w, n):
                    sp.wait_ge(S["lo_ready"], n + (slot + 1))
                    sp.dma_start(ring[:, slot % RING, :, 0:w], src).then_inc(S[f"landed{slot % RING}"], 16)

                sp.wait_ge(S["consts"], 1)
                sp.wait_ge(S["row_free"], L + 1)
                sp.wait_ge(S["mixp_free"], L + 1)
                for r, tile, p0, k, src in row_pieces():
                    a = src(L)[r:r + k, :]
                    sp.dma_start(prow[p0:p0 + k, tile, 0:a.shape[1]], a).then_inc(S["rows_in"], 16)
                for dst, src in mixer_params(L):
                    sp.dma_start(dst, src).then_inc(S["mixp_in"], 16)
                for i, b in enumerate(blocks):
                    if i == 1:
                        sp.wait_ge(S["ut_ready"], L * 24 + 8)
                        sp.dma_start(w2sb[0:RD], rw_w2[L].rearrange("d r c -> r d c")).then_inc(S["w2_in"], 16)
                        sp.dma_start(w2sb[RD:2 * RD], rw_a2[L].rearrange("d r c -> r d c")).then_inc(S["w2_in"], 16)
                        sp.dma_start(g2sb, rw_g2[L]).then_inc(S["w2_in"], 16)
                    for k in range(KSLOTS):
                        load(SL_IN + KSLOTS * i + k, w_in_v[L, :, KS * k:KS * k + KS, b[2]:b[2] + width(b)], width(b), base)
                for i in range(NO):
                    for k in range(KSLOTS):
                        if i == 0 and k == AHEAD:
                            sp.wait_ge(S["rw_done"], L * RC + RC)
                            sp.dma_start(mln, ml_norm_g[L].partition_broadcast(P)).then_inc(S["mln_in"], 16)
                        load(SL_OUT + KSLOTS * i + k, w_out_v[L, :, KS * k:KS * k + KS, 512 * i:512 * i + 512], 512, base)
                with sp.Fori(0, NU) as i:
                    n = sp.snap(base + i * (2 * KSLOTS))
                    for g in range(2):
                        for k in range(KSLOTS):
                            load(SL_UP + KSLOTS * g + k, w_up_v[L, :, KS * k:KS * k + KS, ds(i * 512 + g * FF, 512)], 512, n)
                sp.wait_ge(S["ut_ready"], L * 24 + 16)
                sp.dma_start(pin, p[L, 0].rearrange("(t q) c -> q t c", q=P)).then_inc(S["pin_in"], 16)
                for i in range(NO):
                    for k in range(FT // KS):
                        load(SL_DOWN + FT // KS * i + k,
                             w_down_v[L, :, KS * k:KS * k + KS, 512 * i:512 * i + 512], 512, base)
                for i in range(NO):
                    if i == 1:
                        sp.wait_ge(S["ut_ready"], L * 24 + 24)
                        sp.dma_start(projw, w_ple_proj[L].rearrange("(k q) n -> q k n", q=P)).then_inc(S["proj_in"], 16)
                    for k in range(KSLOTS):
                        load(SL_PLE + KSLOTS * i + k, w_pg_v[L, :, KS * k:KS * k + KS, 512 * i:512 * i + 512], 512, base)
            sp.wait_ge(S["h_ready"], 3 * DEPTH + 1)
            sp.dma_start(Z[:, 0:D], norm_final.partition_broadcast(P)).then_inc(S["nf_in"], 16)
            for t in range(NT):
                sp.wait_ge(S["fin_out"], t + 1)
                sp.dma_start(out[0, t * P:(t + 1) * P, :], YB[:, t, :]).then_inc(S["out_done"], 16)
            sp.wait_ge(S["out_done"], 16 * NT)

        @block.gpsimd
        def _(pool):
            def sel(dst, src, op, base, pattern, cm, fill=0.0):
                return pool.affine_select(out=dst, in_=src, compare_op=op, fill=fill, base=base,
                                          pattern=pattern, channel_multiplier=cm)
            for dst, v in ((ones[:], 1.0), (one_h[:], 1.0), (ident[:], 0.0), (headones[:], 0.0), (prow, 0.0),
                           (epsb[:, 0:1], EPS), (epsb[:, 1:2], RW_LN_EPS), (epsb[:, 2:3], 1.0)):
                pool.memset(dst, v)
            pool.drain()
            pool.memset(headones[0:64, 0:64], 1.0)
            pool.memset(headones[64:128, 64:128], 1.0)
            pool.drain()
            sel(ident[:], ident[:], ALU.not_equal, 0, [[-1, P]], 1, 1.0)
            sel(incl[0][:], ones[:], ALU.is_ge, 0, [[1, P]], -1)
            sel(incl[1][:], ones[:], ALU.is_ge, 0, [[-1, P]], 1)
            for d in range(2):
                step, cm = ((1, -1), (-1, 1))[d]
                for kind, op in enumerate((ALU.is_gt, ALU.is_ge, ALU.is_gt, ALU.is_ge)):
                    sel(pred[d][:, kind, :], one_h[:], op, 0, [[step, P]], cm)
            pool.drain()
            for m in range(LEVELS):
                b = 1 << m
                for d in range(2):
                    cols = lev[d][:, m, :].rearrange("p (n w) -> p n w", w=2 * b)
                    early, late = (cols[:, :, 0:b], cols[:, :, b:2 * b])[::1 - 2 * d]
                    one3 = one_h[:, :].rearrange("p (n w) -> p n w", w=2 * b)[:, :, 0:b]
                    lo, nb = (b, 0)[d], P // (2 * b)
                    sel(early, one3, ALU.is_ge, -lo, [[-2 * b, nb], [0, b]], 1)
                    pool.memset(late, 0.0)
                    pool.drain()
                    sel(early, early, ALU.is_ge, lo + b - 1, [[2 * b, nb], [0, b]], -1)
                    pool.drain()
                    sel(lev[d][:, m, :], lev[d][:, m, :], ALU.not_equal, 0, [[-1, P]], 1, 1.0)
            for d in range(2):
                pool.tensor_tensor(negstrict[d][:], ident[:], incl[d][:], ALU.subtract)
            pool.drain().then_inc(S["consts"], 1)

            with pool.Fori(0, DEPTH) as L:
                with pool.Fori(0, GP) as i:
                    n = pool.snap(L * (2 * GP) + i * 2)
                    for d in range(2):
                        pool.wait_ge(S["gd_d"], n + (d + 1))
                        pool.tensor_tensor(scores[d][:, 0, :, :], scores[d][:, 0, :, :], bmid(negstrict[d][:], 4),
                                           ALU.mult)
                        pool.tensor_tensor(scores[d][:, 1, :, :], scores[d][:, 1, :, :], bmid(incl[d][:], 4),
                                           ALU.mult).then_inc(S["gd_dm"], 1)
                with pool.Fori(0, MP) as i:
                    n = pool.snap(L * (2 * MP) + i * 2)
                    for d in range(2):
                        pool.wait_ge(S["ml_d"], n + (d + 1))
                        dg = ml_diag(d)
                        for h in range(2):
                            pool.tensor_tensor(dg[h], dg[h], bmid(incl[d][:], 2), ALU.mult)
                        pool.drain().then_inc(S["ml_dm"], 1)
                with pool.Fori(0, NU) as i:
                    pool.wait_ge(S["up_vconv"], L * NU + (i + 2))
                    pool.tensor_tensor(up_buf(0), up_buf(0), up_buf(1), ALU.mult)
                    pool.drain()
                    pool.tensor_copy(ghi[:, ds(i * 4, 4), :], up_buf(0))
                    pool.drain()
                    pool.tensor_tensor(glo[:, ds(i * 4, 4), :], up_buf(0), ghi[:, ds(i * 4, 4), :].bitcast(F32),
                                       ALU.subtract).then_inc(S["up_done"], 1)

        @block.tensor
        def _(pe):
            pe.sem_inc(S["slot_done"], RING)
            pe.sem_inc(S["lo_ready"], RING)
            for credit in ("row_free", "mixp_free", "up_gconv", "up_vconv", "up_done"):
                pe.sem_inc(S[credit], 1)
            pe.wait_ge(S["consts"], 1)

            def mm(o_, a, b, start, stop):
                return pe.matmul(o_, a, b, start=start, stop=stop, skip_group_check=True)

            def turn(o_, a):
                n = a.shape[0]
                return pe.transpose(o_, a, ident[0:n, 0:n])

            def slot_wait(base, slot):
                pe.wait_ge(S["lo_ready"], base + (RING + slot + 1))

            def product(o_, a, b, first, last):
                mm(o_, a[0], b[0], first, False)
                mm(o_, a[0], b[1], False, False)
                return mm(o_, a[1], b[0], False, last)

            def wparts(slot, kk, lo, n):
                return tuple(w[:, slot % RING, kk, lo:lo + n] for w in (whi, wlo))

            def turn_rows(src, psum_sem):
                for g in range(4):
                    for t in range(NT):
                        if psum_sem == "ut_psum" and g == 0:
                            pe.wait_ge(S["u_ready"], uq + (t + 1))
                        for c in range(4):
                            last = turn(ps[2 * g + t][:, c * P:(c + 1) * P], src[:, t, (4 * g + c) * P:(4 * g + c + 1) * P])
                        last.then_inc(S[psum_sem], 1)

            def token_product(hi, lo, slot0, base, kt, bank_of, before=None, after=None):
                for i in range(NO):
                    if before:
                        before(i)
                    for k in range(kt // KS):
                        slot = slot0 + kt // KS * i + k
                        slot_wait(base, slot)
                        for t in range(NT):
                            for kk in range(KS):
                                c = KS * k + kk
                                last = product(ps[bank_of(i, t)][:, :], (hi[:, c, t * P:(t + 1) * P], lo[:, c, t * P:(t + 1) * P]),
                                               wparts(slot, kk, 0, 512), c == 0, c == kt - 1)
                        last.then_inc(S["slot_done"], 1)
                    if after:
                        after(i)

            def invert(m2, nt):
                for d in range(2):
                    pe.wait_ge(S["inv_t1"], m2 + (d + 1))
                    for j in range(4):
                        last = turn(ps[4 * d + 1][:, j * P:(j + 1) * P], TT[d][:, j, :])
                    last.then_inc(S["inv_t1p"], 1)
                ml = pe.snap(m2 * LEV)
                mn = pe.snap(m2 * (LEV - 1))
                for lv in range(LEV):
                    for d in range(2):
                        if lv == 0:
                            pe.wait_ge(S["inv_tn1"], m2 + (d + 1))
                        else:
                            pe.wait_ge(S["inv_tn"], mn + (2 * lv - 1 + d))
                        for j in range(4):
                            last = mm(ps[4 * d][:, j * P:(j + 1) * P], nt(d, j), TN[d][:, j, :], True, True)
                        last.then_inc(S["inv_x"], 1)
                    for d in range(2):
                        pe.wait_ge(S["inv_xs"], ml + (2 * lv + d + 1))
                        if lv:
                            pe.wait_ge(S["inv_tt"], ml + (2 * lv - 1 + d))
                        if lv < LEV - 1:
                            for j in range(4):
                                mm(ps[4 * d + 1][:, j * P:(j + 1) * P], TT[d][:, j, :], XS[d][:, j, :], True, True)
                        for j in range(4):
                            last = mm(ps[4 * d + 2][:, j * P:(j + 1) * P], XS[d][:, j, :], TT[d][:, j, :], True, True)
                        last.then_inc(S["inv_t"], 1)

            with pe.Fori(0, DEPTH) as L:
                base = pe.snap(L * SL)
                pe.wait_ge(S["h_ready"], L * 3 + 1)
                pe.wait_ge(S["rows_in"], L * ROWS_TOTAL + ROWS_TOTAL)
                for j in range(PT):
                    last = turn(ps[j // 4][:, (j % 4) * P:(j % 4 + 1) * P], prow[:, j, :])
                last.then_inc(S["par_turned"], 1)
                pe.wait_ge(S["par_ready"], L + 1)
                uq = pe.snap(L * 6)
                turn_rows(YB, "ut_psum")
                nb = pe.snap(L * NB)
                for i, (kind, b, c0, tiles) in enumerate(blocks):
                    if i >= 2:
                        pe.wait_ge(S["blk_evac"], nb + (i - 1))
                    g = 4 * (i % 2)
                    for k in range(KSLOTS):
                        slot = SL_IN + KSLOTS * i + k
                        if i == 0 and k % 2 == 0:
                            pe.wait_ge(S["ut_ready"], L * 24 + max(4, k + 2))
                        slot_wait(base, slot)
                        for c in range(len(tiles or ())):
                            off = 2 * RD * c if kind == "lora" else P * c
                            for kk in range(KS):
                                u = KS * k + kk
                                last = product(ps[g + c][:, 0:T], wparts(slot, kk, off, P), (uhi[:, u, :], ulo[:, u, :]),
                                               u == 0, u == KT - 1)
                        for t in range(0 if tiles else NT):
                            w = width((kind, b, c0, tiles))
                            for kk in range(KS):
                                u = KS * k + kk
                                last = product(ps[g + t][:, 0:w], (uhi[:, u, t * P:(t + 1) * P], ulo[:, u, t * P:(t + 1) * P]),
                                               wparts(slot, kk, 0, w), u == 0, u == KT - 1)
                        last.then_inc(S["slot_done"], 1)

                pe.wait_ge(S["lora_act"], L + 1)
                pe.wait_ge(S["w2_in"], L * 48 + 48)
                pe.wait_ge(S["blk_evac"], nb + NB)
                for j in range(2):
                    for c in range(RC):
                        for d in range(2):
                            last = mm(ps[4 * j + c][:, d * T:(d + 1) * T], w2sb[RD * j:RD * (j + 1), d, c * P:(c + 1) * P],
                                      zlora[RD * j:RD * (j + 1), 0, :], True, True)
                        last.then_inc(S["lora_psum"], 1)
                pe.wait_ge(S["lora_ready"], L * 8 + 8)
                for t in range(NT):
                    last = mm(ps[t][:, :], zlora[0:RG, 1, t * P:(t + 1) * P], g2sb, True, True)
                last.then_inc(S["gate_psum"], 1)
                with pe.Fori(0, RC) as c:
                    pe.wait_ge(S["gate_ready"], L + 1)
                    n = pe.snap(L * RC + c)
                    n2 = pe.snap(n * 2)
                    m2 = pe.snap(L * (2 * (RC + GP)) + c * 2)
                    pe.wait_ge(S["rw_sq"], n + 1)
                    mm(ps[0][:, 0:T], headones[:], ch[:, 2, :], True, True).then_inc(S["rw_ssq"], 1)
                    for t in range(NT):
                        last = turn(ps[1][:, t * P:(t + 1) * P], ch[:, 0, t * P:(t + 1) * P])
                    last.then_inc(S["rw_vt"], 1)
                    pe.wait_ge(S["rw_cf"], n + 1)
                    for t in range(NT):
                        last = mm(ps[0][:, 2 * t:2 * t + 2], ch[:, 3, t * P:(t + 1) * P], headones[:, 0:P:64], True, True)
                    last.then_inc(S["rw_coef"], 1)
                    pe.wait_ge(S["rw_coefc"], n + 1)
                    pe.wait_ge(S["rw_vtc"], n + 1)
                    for d in range(2):
                        pe.wait_ge(S["rw_ops"], n2 + (d + 1))
                        for h in range(2):
                            for t in range(NT):
                                for j in range(2):
                                    hp = slice(64 * h, 64 * h + 64)
                                    last = mm(ps[4 * d + 2 * h + t][:, j * T:(j + 1) * T], KB[d][hp, j, t * P:(t + 1) * P],
                                              AR[d][hp, t, :, :], True, True)
                        last.then_inc(S["rw_sc"], 1)
                    for d in range(2):
                        F = FIRST[d]
                        pe.wait_ge(S["rw_masked"], n2 + (d + 1))
                        for h in range(2):
                            mm(ps[4 * d + 3][:, 64 * h:64 * h + 64], scores[d][:, 2 * h + F, 0, :],
                               Vt[:, F, 64 * h:64 * h + 64], True, True)
                        for j in range(2):
                            last = turn(ps[4 * d + 3][:, T + j * P:T + (j + 1) * P], KB[d][:, j, F * P:(F + 1) * P])
                        last.then_inc(S["rw_pv"], 1)
                    invert(m2, lambda d, j: scores[d][:, j, 2, :])
                    for d in range(2):
                        F = FIRST[d]
                        pe.wait_ge(S["inv_tt"], m2 * LEV + (2 * LEV - 1 + d))
                        pe.wait_ge(S["rw_rf"], n2 + (d + 1))
                        for h in range(2):
                            last = mm(ps[4 * d][:, 64 * h:64 * h + 64], TT[d][:, 2 * h + F, :], rf[d][:, 0, 64 * h:64 * h + 64],
                                      True, True)
                        last.then_inc(S["rw_u"], 1)
                    for d in range(2):
                        F = FIRST[d]
                        pe.wait_ge(S["rw_uf"], n2 + (d + 1))
                        mm(ps[4 * d + 1][:, 0:P], KBt[d][:, 0, :], Vt[:, F, :], True, False)
                        mm(ps[4 * d + 1][:, 0:P], KBt[d][:, 1, :], uf[d][:, 0, :], False, True).then_inc(S["rw_state"], 1)
                    for d in range(2):
                        B = 1 - FIRST[d]
                        pe.wait_ge(S["rw_s0"], n2 + (d + 1))
                        mm(ps[4 * d + 2][:, 0:P], AR[d][:, B, 0, :], S0[d][:, 0, :], True, False)
                        for h in range(2):
                            last = mm(ps[4 * d + 2][:, 64 * h:64 * h + 64], scores[d][:, 2 * h + B, 0, :],
                                      Vt[:, B, 64 * h:64 * h + 64], False, h == 1)
                        last.then_inc(S["rw_pv2"], 1)
                    for d in range(2):
                        B = 1 - FIRST[d]
                        pe.wait_ge(S["rw_rf2"], n2 + (d + 1))
                        for h in range(2):
                            last = mm(ps[4 * d][:, P + 64 * h:P + 64 * h + 64], TT[d][:, 2 * h + B, :],
                                      rf[d][:, 1, 64 * h:64 * h + 64], True, True)
                        last.then_inc(S["rw_u2"], 1)
                    for d in range(2):
                        F, B = FIRST[d], 1 - FIRST[d]
                        pe.wait_ge(S["rw_uf2"], n2 + (d + 1))
                        y = ps[4 * d + 3]
                        mm(y[:, B * P:(B + 1) * P], AR[d][:, B, 1, :], S0[d][:, 0, :], True, False)
                        for t, u in ((B, 1), (F, 0)):
                            for h in range(2):
                                o_ = y[:, t * P + 64 * h:t * P + 64 * h + 64]
                                mm(o_, scores[d][:, 2 * h + t, 1, :], Vt[:, t, 64 * h:64 * h + 64], False, False)
                                last = mm(o_, scores[d][:, 2 * h + t, 3, :], uf[d][:, u, 64 * h:64 * h + 64], False, True)
                        last.then_inc(S["rw_y"], 1)

                pe.wait_ge(S["gd_gl"], L + 1)
                for d in range(2):
                    for t in range(NT):
                        mm(ps[0][:, 2 * GH * t + GH * d:2 * GH * t + GH * d + GH], incl[d][:],
                           gates[:, 0, t, GH * d:GH * d + GH], True, True)
                for t in range(NT):
                    last = mm(ps[0][:, 64 + 2 * GH * t:64 + 2 * GH * (t + 1)], ones[:], gates[:, 0, t, :], True, True)
                last.then_inc(S["gd_cum"], 1)
                with pe.Fori(0, GP) as i:
                    n = pe.snap(L * GP + i)
                    n2 = pe.snap(n * 2)
                    m2 = pe.snap(L * (2 * (RC + GP)) + (i * 2 + 2 * RC))
                    pe.wait_ge(S["gd_sq"], n + 1)
                    for j in range(2):
                        last = mm(ps[j][:, :], ones[:], mono(KB[j][:, :, :], 2), True, True)
                    last.then_inc(S["gd_ssq"], 1)
                    for h in range(2):
                        for t in range(NT):
                            last = turn(ps[2][:, (2 * h + t) * P:(2 * h + t + 1) * P], chg[:, h, t * P:(t + 1) * P])
                    last.then_inc(S["gd_vt"], 1)
                    pe.wait_ge(S["gd_qk"], n + 1)
                    for h in range(2):
                        for t in range(NT):
                            last = turn(ps[3][:, (2 * h + t) * P:(2 * h + t + 1) * P], AR[h][:, t, 0, :])
                    last.then_inc(S["gd_kt"], 1)
                    for h in range(2):
                        for t in range(NT):
                            last = mm(ps[6 + h][:, t * T:(t + 1) * T], AR[h][:, t, 0, :], AR[h][:, t, :, :], True, True)
                    last.then_inc(S["gd_sc"], 1)
                    for d in range(2):
                        for h in range(2):
                            for t in range(NT):
                                o_ = slice((2 * h + t) * P, (2 * h + t + 1) * P)
                                lg = gs[:, 0 + 2 * t + d, h:h + 1].to_broadcast([P, P])
                                lb = gs[:, 4 + 2 * t + d, h:h + 1].to_broadcast([P, P])
                                mm(ps[4 * d + 1][:, o_], lg, incl[d][:], True, True)
                                mm(ps[4 * d][:, o_], lg, incl[d][:], True, False)
                                last = mm(ps[4 * d][:, o_], lb, ident[:], False, True)
                        last.then_inc(S["gd_gb"], 1)
                    pe.wait_ge(S["gd_nt"], n2 + 2)
                    pe.wait_ge(S["gd_vtc"], n + 1)
                    pe.wait_ge(S["gd_ktc"], n + 1)
                    invert(m2, lambda d, j: scores[d][:, 2, j, :])
                    for d in range(2):
                        F = FIRST[d]
                        pe.wait_ge(S["inv_tt"], m2 * LEV + (2 * LEV - 1 + d))
                        pe.wait_ge(S["gd_rhs"], n2 + (d + 1))
                        for h in range(2):
                            last = mm(ps[4 * d][:, h * P:(h + 1) * P], TT[d][:, 2 * h + F, :], TN[d][:, 2 * h + F, :], True, True)
                        last.then_inc(S["gd_u"], 1)
                    for d in range(2):
                        F = FIRST[d]
                        pe.wait_ge(S["gd_uf"], n2 + (d + 1))
                        for h in range(2):
                            last = mm(ps[4 * d + 1][:, h * P:(h + 1) * P], XS[d][:, h, :], ufg[d][:, h, :], True, True)
                        last.then_inc(S["gd_state"], 1)
                        for h in range(2):
                            j = 2 * h + F
                            mm(ps[4 * d + 3][:, j * P:(j + 1) * P], scores[d][:, 3, j, :], ufg[d][:, h, :], True, True)
                    for d in range(2):
                        B = 1 - FIRST[d]
                        pe.wait_ge(S["gd_s0"], n2 + (d + 1))
                        for j in range(2):
                            for h in range(2):
                                last = mm(ps[4 * d + 2][:, (2 * j + h) * P:(2 * j + h + 1) * P], AR[h][:, B, j, :],
                                          S0g[d][:, h, :], True, True)
                        last.then_inc(S["gd_ks"], 1)
                    for d in range(2):
                        B = 1 - FIRST[d]
                        pe.wait_ge(S["gd_rs"], n2 + (d + 1))
                        for h in range(2):
                            last = mm(ps[4 * d][:, (2 + h) * P:(3 + h) * P], TT[d][:, 2 * h + B, :], rf[d][:, h, :], True, True)
                        last.then_inc(S["gd_us"], 1)
                    for d in range(2):
                        B = 1 - FIRST[d]
                        pe.wait_ge(S["gd_usc"], n2 + (d + 1))
                        for h in range(2):
                            j = 2 * h + B
                            last = mm(ps[4 * d + 3][:, j * P:(j + 1) * P], scores[d][:, 3, j, :], KBt[d][:, h, :], True, True)
                        last.then_inc(S["gd_y"], 1)

                pe.wait_ge(S["ml_g"], L + 1)
                for j in range(2):
                    for d in range(2):
                        for t in range(NT):
                            last = turn(ps[j][0:MH, d * T + t * P:d * T + (t + 1) * P],
                                        gx[:, 0, t, 2 * MH * j + MH * d:2 * MH * j + MH * d + MH])
                last.then_inc(S["ml_rt"], 1)
                pe.wait_ge(S["ml_rows"], L + 1)
                for j, rowt in enumerate((TN[0], TT[0])):
                    rr = mono(rowt[0:MH, :, :], 4)
                    for d in range(2):
                        for t in range(NT):
                            q = (4 * j + 2 * d + t) * MH
                            last = mm(ps[2][:, q:q + MH], rr[:, d * T + t * P:d * T + (t + 1) * P], ident[0:MH, 0:MH], True, True)
                last.then_inc(S["ml_back"], 1)
                with pe.Fori(0, MP) as i:
                    n = pe.snap(L * MP + i)
                    n2 = pe.snap(n * 2)
                    pe.wait_ge(S["ml_in"], n + 1)
                    for h in range(2):
                        hp = slice(64 * h, 64 * h + 64)
                        for j in range(NT):
                            last = mm(ps[h][:, j * T:(j + 1) * T], KB[0][hp, 1, j * P:(j + 1) * P], KB[0][hp, 0, :], True, True)
                    last.then_inc(S["ml_sc"], 1)
                    mrow = mono(TN[1][0:MH, :, :], 4)
                    for d in range(2):
                        for h in range(2):
                            last = mm(ps[4 + d][:, h * T:(h + 1) * T], small[0:MH, 8 + h:9 + h].to_broadcast([MH, P]),
                                      mrow[:, d * T:(d + 1) * T], True, True)
                        last.then_inc(S["ml_mb"], 1)
                    for d in range(2):
                        pe.wait_ge(S["ml_p"], n2 + (d + 1))
                        for h in range(2):
                            for t in range(NT):
                                js = [j for j in range(NT) if (j <= t if d == 0 else j >= t)]
                                for j in js:
                                    last = mm(ps[4 * d + 2 + h][:, t * (P + 1):(t + 1) * (P + 1)],
                                              ml_flat(d)[:, h, j, t * P:(t + 1) * P], V1[:, j, h, 0:P + 1], j == js[0],
                                              j == js[-1])
                        last.then_inc(S["ml_num"], 1)

                pe.wait_ge(S["ml_done"], L * MP + MP)
                turn_rows(YB, "yt_psum")
                pe.wait_ge(S["yt_ready"], L * 8 + 8)
                token_product(uhi, ulo, SL_OUT, base, KT, lambda i, t: 2 * i + t)

                uq = pe.snap(L * 6 + 2)
                turn_rows(YB, "ut_psum")
                with pe.Fori(0, NU) as i:
                    pe.wait_ge(S["ut_ready"], L * 24 + 16)
                    n = pe.snap(L * NU + i)
                    la = pe.snap(base + i * (2 * KSLOTS))
                    for g in range(2):
                        pe.wait_ge(S["up_vconv" if g else "up_gconv"], n + 1)
                        for k in range(KSLOTS):
                            slot = SL_UP + KSLOTS * g + k
                            slot_wait(la, slot)
                            for c in range(4):
                                for kk in range(KS):
                                    u = KS * k + kk
                                    last = product(ps[4 * g + c][:, 0:T], wparts(slot, kk, c * P, P),
                                                   (uhi[:, u, :], ulo[:, u, :]), u == 0, u == KT - 1)
                            last.then_inc(S["slot_done"], 1)
                pe.wait_ge(S["up_done"], L * NU + (NU + 1))
                token_product(ghi, glo, SL_DOWN, base, FT, lambda i, t: 2 * i + t)

                uq = pe.snap(L * 6 + 4)
                turn_rows(YB, "ut_psum")
                pe.wait_ge(S["ut_ready"], L * 24 + 24)
                pe.wait_ge(S["pin_in"], L * 16 + 16)
                for k in range(PLE // P):
                    for t in range(NT):
                        last = turn(ps[7][:, (2 * k + t) * P:(2 * k + t + 1) * P], pin[:, t, k * P:(k + 1) * P])
                last.then_inc(S["p_turned"], 1)
                pe.wait_ge(S["pt_ready"], L + 1)

                def before(i):
                    if i >= 2:
                        pe.wait_ge(S["ple_done"], L * NO + (i - 1))

                def after(i):
                    if i == 0:
                        pe.wait_ge(S["proj_in"], L * 16 + 16)
                    for t in range(NT):
                        for k in range(PLE // P):
                            last = mm(ps[4 * (i % 2) + 2 + t][:, :], pT[:, k, t * P:(t + 1) * P],
                                      projw[:, k, 512 * i:512 * i + 512], k == 0, k == PLE // P - 1)
                    last.then_inc(S["ple_psum"], 1)
                token_product(uhi, ulo, SL_PLE, base, KT, lambda i, t: 4 * (i % 2) + t, before, after)

        @block.scalar
        def _(act):
            act.wait_ge(S["consts"], 1)

            def a(o_, i_, f, **kw):
                return act.activation(o_, i_, f, **kw)

            def rms(q):
                act.wait_ge(S["h_ready"], q)
                for t in range(NT):
                    a(YB[:, t, :], H[:, t, :], ACT.Square, accum_out=small[:, t:t + 1])
                act.drain()
                a(small[:, 2:2 + NT], small[:, 0:NT], ACT.Sqrt, scale=1.0 / D, bias=epsb[:, 0:1]).then_inc(S["rms_ready"], 1)

            def rsqrt(o_, i_, scale, bias):
                a(o_, i_, ACT.Ln, scale=scale, bias=bias)
                act.drain()
                return a(o_, o_, ACT.Exp, scale=-0.5)

            def t1(m2):
                for d in range(2):
                    act.wait_ge(S["inv_t1p"], m2 + (d + 1))
                    a(mono(TN[d][:, :, :], 4), ps[4 * d + 1][:, :], ACT.Copy).then_inc(S["inv_tn1"], 1)
                ml = act.snap(m2 * LEV)
                for lv in range(LEV - 1):
                    for d in range(2):
                        act.wait_ge(S["inv_t"], ml + (2 * lv + d + 1))
                        a(mono(TN[d][:, :, :], 4), ps[4 * d + 1][:, :], ACT.Copy).then_inc(S["inv_tn"], 1)

            def split_hi(base, landed, first, end):
                for slot in range(first, min(end, SL)):
                    w = slot_width(slot)
                    act.wait_ge(S[f"landed{slot % RING}"], landed + 16 * (slot // RING + 1))
                    act.wait_ge(S["slot_done"], base + (slot + 1))
                    a(whi[:, slot % RING, :, 0:w], ring[:, slot % RING, :, 0:w], ACT.Copy).then_inc(S["hi_ready"], 1)

            def turned_hi(psum_sem, hi_sem, q8, row=None):
                for g in range(4):
                    for t in range(NT):
                        act.wait_ge(S[psum_sem], q8 + (2 * g + t + 1))
                        bank = third(ps[2 * g + t][:, :], 4)
                        if row is None:
                            last = a(uhi[:, 4 * g:4 * g + 4, t * P:(t + 1) * P], bank, ACT.Copy)
                        for c in range(4 if row is not None else 0):
                            k = 4 * g + c
                            last = a(uhi[:, k, t * P:(t + 1) * P], bank[:, c, :], ACT.Copy, scale=par[:, row + k:row + k + 1])
                        last.then_inc(S[hi_sem], 1)

            with act.Fori(0, DEPTH) as L:
                sl = act.snap(L * SL)
                la = act.snap(L * (16 * SL // RING))
                split_hi(sl, la, 0, AHEAD)
                rms(L * 3 + 1)
                NSC = sum(b[0] in ("rw", "lora", "gdq") for b in blocks)
                act.wait_ge(S["par_ready"], L + 1)
                turned_hi("ut_psum", "ut_hi", act.snap(L * 24), rows["norm0"])
                for i, (kind, b, c0, tiles) in enumerate(blocks):
                    end = SL_IN + KSLOTS * (i + 1)
                    split_hi(sl, la, end - KSLOTS + AHEAD, end + AHEAD)
                    if kind not in ("rw", "lora", "gdq"):
                        continue
                    act.wait_ge(S["slot_done"], sl + (RING + end))
                    for c, w in enumerate(tiles):
                        if kind == "rw":
                            sc, dst = mu_mid[:, RC * b + c:RC * b + c + 1], zrw[:, RC * b + c, :]
                        elif kind == "lora":
                            sc, dst = mu_mid[0:w, 3 * RC + c:3 * RC + c + 1], zlora[0:w, c, :]
                        else:
                            col = rows["conv"] + TAPS // 2 * 3 * GH + 3 * b + c
                            sc, dst = par[:, col:col + 1], zgd[:, 3 * b + c, :]
                        last = a(dst, ps[4 * (i % 2) + c][0:w, 0:T], ACT.Copy, scale=sc)
                    last.then_inc(S["blk_scaled"], 1)
                act.wait_ge(S["blk_evac"], L * NB + 4)
                a(zlora[0:RD, 0, :], zlora[0:RD, 0, :], ACT.Tanh)
                a(zlora[0:RG, 1, :], zlora[0:RG, 1, :], ACT.Sigmoid).then_inc(S["lora_act"], 1)
                for j, nm in enumerate(("w0", "a0")):
                    for c in range(RC):
                        act.wait_ge(S["lora_psum"], L * 8 + (4 * j + c + 1))
                        for d in range(2):
                            col = rows[nm] + RC * d + c
                            last = a(swa[:, j, d, c, :], ps[4 * j + c][:, d * T:(d + 1) * T], ACT.Sigmoid,
                                     bias=par[:, col:col + 1])
                        last.then_inc(S["lora_ready"], 1)
                act.wait_ge(S["gate_psum"], L + 1)
                for t in range(NT):
                    last = a(sgate[:, t, :], ps[t][:, :], ACT.Copy)
                last.then_inc(S["gate_ready"], 1)
                with act.Fori(0, RC) as c:
                    n = act.snap(L * RC + c)
                    n2 = act.snap(n * 2)
                    m2 = act.snap(L * (2 * (RC + GP)) + c * 2)
                    act.wait_ge(S["rw_ssq"], n + 1)
                    rsqrt(ch[:, 3, :], ps[0][:, 0:T], 1.0, epsb[:, 0:1]).then_inc(S["rw_rn"], 1)
                    act.wait_ge(S["rw_vt"], n + 1)
                    a(mono(Vt[:, 0:2, :], 2), ps[1][:, 0:T], ACT.Copy).then_inc(S["rw_vtc"], 1)
                    for d in range(2):
                        act.wait_ge(S["rw_cs"], n2 + (d + 1))
                        a(ew[d][:, 0, :], cs[d][:, :], ACT.Exp, scale=-KAPPA)
                        a(ew[d][:, 1, :], cs[d][:, :], ACT.Exp, scale=KAPPA)
                        a(ew[d][:, 2, :], ew[d][:, 2, :], ACT.Exp, scale=-KAPPA)
                        a(mid[d][:, 3:4], mid[d][:, 2:3], ACT.Exp, scale=-KAPPA).then_inc(S["rw_exp"], 1)
                    t1(m2)
                    for src, dst, k, done in (("rw_u", uf, 0, "rw_uf"), ("rw_pv2", rf, 1, "rw_rf2"), ("rw_u2", uf, 1, "rw_uf2")):
                        for d in range(2):
                            bank = {"rw_u": ps[4 * d][:, 0:P], "rw_pv2": ps[4 * d + 2][:, 0:P], "rw_u2": ps[4 * d][:, P:2 * P]}[src]
                            act.wait_ge(S[src], n2 + (d + 1))
                            a(dst[d][:, k, :], bank, ACT.Copy).then_inc(S[done], 1)
                    act.wait_ge(S["rw_var"], n + 1)
                    rsqrt(st[:, 2, :], st[:, 1, :], 1.0 / 64, epsb[:, 1:2]).then_inc(S["rw_rstd"], 1)
                act.wait_ge(S["gd_sp"], L + 1)
                a(gpar[:, 1, :], gpar[:, 1, :], ACT.Exp)
                a(gx[:, 1, :, :], gx[:, 1, :, :], ACT.Exp, scale=-1.0)
                act.drain()
                a(gx[:, 1, :, :], gx[:, 1, :, :], ACT.Ln, bias=epsb[:, 2:3]).then_inc(S["gd_ln"], 1)
                act.wait_ge(S["gd_cumc"], L + 1)
                a(gates[:, 3, :, :], gates[:, 2, :, :], ACT.Exp)
                a(gates[:, 4, :, :], gates[:, 4, :, :], ACT.Exp)
                a(gates[:, 5, :, :], gates[:, 1, :, :], ACT.Exp).then_inc(S["gd_exp"], 1)
                a(zgd, zgd, ACT.Silu)
                a(zgt[:, :, 0:GW], zgt[:, :, 0:GW], ACT.Silu).then_inc(S["gd_silu"], 1)
                with act.Fori(0, GP) as i:
                    n = act.snap(L * GP + i)
                    n2 = act.snap(n * 2)
                    m2 = act.snap(L * (2 * (RC + GP)) + (i * 2 + 2 * RC))
                    act.wait_ge(S["gd_ssq"], n + 1)
                    for j in range(2):
                        a(mono(ewg[j], 2), ps[j][:, :], ACT.Ln, bias=epsb[:, 0:1])
                    act.drain()
                    for j in range(2):
                        last = a(ewg[j], ewg[j], ACT.Exp, scale=-0.5)
                    last.then_inc(S["gd_rn"], 1)
                    act.wait_ge(S["gd_vt"], n + 1)
                    a(mono(Vt, 4), ps[2][:, :], ACT.Copy).then_inc(S["gd_vtc"], 1)
                    act.wait_ge(S["gd_kt"], n + 1)
                    a(mono(OT, 4), ps[3][:, :], ACT.Copy).then_inc(S["gd_ktc"], 1)
                    for d in range(2):
                        act.wait_ge(S["gd_arg"], n2 + (d + 1))
                        a(scores[d][:, 0:2, :, :], scores[d][:, 0:2, :, :], ACT.Exp).then_inc(S["gd_d"], 1)
                    t1(m2)
                    for src, dst, lo, done in (("gd_u", ufg, 0, "gd_uf"), ("gd_us", KBt, T, "gd_usc")):
                        for d in range(2):
                            act.wait_ge(S[src], n2 + (d + 1))
                            a(mono(dst[d][:, :, :], 2), ps[4 * d][:, lo:lo + T], ACT.Copy).then_inc(S[done], 1)
                    act.wait_ge(S["gd_ss"], n + 1)
                    rsqrt(st[:, 2, :], st[:, 1, :], 1.0 / P, epsb[:, 0:1]).then_inc(S["gd_rstd"], 1)
                act.wait_ge(S["ml_x"], L + 1)
                a(gx[:, 1, :, :], gx[:, 0, :, :], ACT.Tanh, scale=1.0 / ML_GATE_CAP).then_inc(S["ml_tanh"], 1)
                act.wait_ge(S["ml_f"], L + 1)
                fg = gx[:, 1, :, 2 * MH:4 * MH]
                a(fg, fg, ACT.Exp, scale=-1.0)
                act.drain()
                a(fg, fg, ACT.Ln, bias=epsb[:, 2:3]).then_inc(S["ml_ln"], 1)
                a(zmt[:, :, MW:2 * MW], zmt[:, :, MW:2 * MW], ACT.Sigmoid).then_inc(S["ml_sig"], 1)
                act.wait_ge(S["ml_backc"], L + 1)
                a(gates[:, 2, :, :], gates[:, 1, :, :], ACT.Exp, scale=-1.0).then_inc(S["ml_expm"], 1)
                with act.Fori(0, MP) as i:
                    n = act.snap(L * MP + i)
                    n2 = act.snap(n * 2)
                    for d in range(2):
                        act.wait_ge(S["ml_arg"], n2 + (d + 1))
                        a(ml_flat(d), ml_flat(d), ACT.Exp, scale=-1.0).then_inc(S["ml_d"], 1)
                    act.wait_ge(S["ml_ss"], n + 1)
                    rsqrt(st[:, 2, :], st[:, 1, :], 1.0 / P, epsb[:, 0:1]).then_inc(S["ml_rstd"], 1)
                turned_hi("yt_psum", "yt_hi", act.snap(L * 8))
                split_hi(sl, la, SL_OUT + AHEAD, SL_UP + AHEAD)
                rms(L * 3 + 2)
                turned_hi("ut_psum", "ut_hi", act.snap(L * 24 + 8), rows["norm1"])
                with act.Fori(0, NU) as i:
                    n = act.snap(L * NU + i)
                    sli = act.snap(L * SL + i * (2 * KSLOTS))
                    lai = act.snap(L * (16 * SL // RING) + i * (16 * 2 * KSLOTS // RING))
                    for g in range(2):
                        end = SL_UP + KSLOTS * (g + 1)
                        split_hi(sli, lai, end - KSLOTS + AHEAD, end + AHEAD)
                        if g == 0:
                            act.wait_ge(S["up_done"], n + 1)
                        act.wait_ge(S["slot_done"], sli + (RING + end))
                        for c in range(4):
                            tap = rows["fconv"] + FTAPS // 2 * 2 * FT + FT * g + c
                            bias = rows["fbias"] + FT * g + c
                            last = a(up_buf(g)[:, c, :], ps[4 * g + c][:, 0:T], ACT.Identity, scale=par[:, ds(i * 4 + tap, 1)],
                                     bias=par[:, ds(i * 4 + bias, 1)])
                        last.then_inc(S["up_vact" if g else "up_gact"], 1)
                        if g == 0:
                            act.wait_ge(S["up_gconv"], n + 2)
                            a(up_buf(0), up_buf(0), ACT.Silu).then_inc(S["up_silu"], 1)
                split_hi(sl, la, SL_DOWN + AHEAD, SL_PLE + AHEAD)
                rms(L * 3 + 3)
                turned_hi("ut_psum", "ut_hi", act.snap(L * 24 + 16), rows["norm2"])
                for i in range(NO):
                    end = SL_PLE + KSLOTS * (i + 1)
                    split_hi(sl, la, end - KSLOTS + AHEAD, end + AHEAD)
                    act.wait_ge(S["slot_done"], sl + (RING + end))
                    if i:
                        act.wait_ge(S["ple_done"], L * NO + i)
                    for t in range(NT):
                        last = a(mono(TN[t][:, :, :], 4), ps[4 * (i % 2) + t][:, :], ACT.Sigmoid)
                    last.then_inc(S["ple_sig"], 1)
            rms(3 * DEPTH + 1)

        @block.vector
        def _(v):
            v.wait_ge(S["consts"], 1)
            v.wait_ge(S["h_in"], 16 * NT)
            v.sem_inc(S["h_ready"], 1)
            MUL, ADD, SUB, MAX, MIN = ALU.mult, ALU.add, ALU.subtract, ALU.max, ALU.min

            def norm(q):
                v.wait_ge(S["rms_ready"], q)
                v.reciprocal(small[:, 4:4 + NT], small[:, 2:2 + NT])
                v.drain()
                for t in range(NT):
                    v.tensor_scalar(YB[:, t, :], H[:, t, :], small[:, 4 + t:5 + t], None, MUL).then_inc(S["u_ready"], 1)

            def split_lo(base, first, end):
                for slot in range(first, min(end, SL)):
                    w = slot_width(slot)
                    v.wait_ge(S["hi_ready"], base + (slot + 1))
                    v.tensor_tensor(wlo[:, slot % RING, :, 0:w], ring[:, slot % RING, :, 0:w],
                                    whi[:, slot % RING, :, 0:w].bitcast(F32), SUB).then_inc(S["lo_ready"], 1)

            def turned_lo(hi_sem, ready_sem, q8, row=None):
                for g in range(4):
                    for t in range(NT):
                        v.wait_ge(S[hi_sem], q8 + (2 * g + t + 1))
                        bank = third(ps[2 * g + t][:, :], 4)
                        if row is None:
                            last = v.tensor_tensor(ulo[:, 4 * g:4 * g + 4, t * P:(t + 1) * P], bank,
                                                   uhi[:, 4 * g:4 * g + 4, t * P:(t + 1) * P].bitcast(F32), SUB)
                        for c in range(4 if row is not None else 0):
                            k = 4 * g + c
                            last = v.scalar_tensor_tensor(ulo[:, k, t * P:(t + 1) * P], bank[:, c, :], par[:, row + k:row + k + 1],
                                                          uhi[:, k, t * P:(t + 1) * P].bitcast(F32), MUL, SUB)
                        last.then_inc(S[ready_sem], 1)

            def add_taps(groups):
                for k in range(len(groups[0][2])):
                    for psum, z, taps in groups:
                        off, w = taps[k]
                        lo, hi = max(0, -off), T - max(0, off)
                        last = v.scalar_tensor_tensor(z[:, lo:hi], psum[:, lo + off:hi + off], w, z[:, lo:hi], MUL, ADD)
                    if k < len(groups[0][2]) - 1:
                        v.drain()
                return last

            def residual(slot0, kt, sl):
                for i in range(NO):
                    end = slot0 + kt // KS * (i + 1)
                    split_lo(sl, end - kt // KS + AHEAD, end + AHEAD)
                    v.wait_ge(S["slot_done"], sl + (RING + end))
                    for t in range(NT):
                        hh = H[:, t, 512 * i:512 * i + 512]
                        last = v.tensor_tensor(hh, hh, ps[2 * i + t][:, :], ADD)
                last.then_inc(S["h_ready"], 1)

            def invert(m2, nt):
                for d in range(2):
                    v.tensor_tensor(TT[d][:, :, :], nt(d), bmid(lev[1 - d][:, 0, :], 4), MUL).then_inc(S["inv_t1"], 1)
                ml = v.snap(m2 * LEV)
                for lv in range(LEV):
                    for d in range(2):
                        v.wait_ge(S["inv_x"], ml + (2 * lv + d + 1))
                        v.tensor_tensor(XS[d][:, :, :], third(ps[4 * d][:, :], 4), bmid(lev[d][:, lv + 1, :], 4), MUL)\
                            .then_inc(S["inv_xs"], 1)
                    for d in range(2):
                        v.wait_ge(S["inv_t"], ml + (2 * lv + d + 1))
                        v.tensor_copy(mono(TT[d][:, :, :], 4), ps[4 * d + 2][:, :]).then_inc(S["inv_tt"], 1)

            def head_out(i, n, fam, gain, gate, col):
                v.drain()
                v.tensor_tensor(OT, OL, OL, MUL)
                v.drain()
                v.tensor_reduce(st[:, 1, :], OT, AX_X, ADD).then_inc(S[fam + "_ss"], 1)
                v.wait_ge(S[fam + "_rstd"], n + 1)
                v.tensor_tensor(OL, OL, bc(st[:, 2, :], P), MUL)
                v.drain()
                for h in range(2):
                    v.tensor_tensor(OL[:, 2 * h:2 * h + 2, :], OL[:, 2 * h:2 * h + 2, :], gain(h), MUL)
                v.drain()
                o4 = OL.rearrange("p (h t) c -> p h t c", h=2)
                for t in range(NT):
                    last = v.tensor_tensor(YB[:, t, ds(i * T + col, T)].rearrange("p (h c) -> p h c", h=2), o4[:, :, t, :],
                                           gate(t), MUL)
                last.then_inc(S[fam + "_done"], 1)

            with v.Fori(0, DEPTH) as L:
                sl = v.snap(L * SL)
                split_lo(sl, 0, AHEAD)
                v.wait_ge(S["par_turned"], L + 1)
                v.tensor_copy(par[:, 0:4 * P], ps[0][:, :])
                v.tensor_copy(par[:, 4 * P:PT * P], ps[1][:, 0:(PT - 4) * P])
                v.drain().then_inc(S["row_free"], 1)
                for dst, m0, m1, k in ((0, rows["mu"], rows["mu"] + 3 * RC, 3 * RC), (3 * RC, rows["mu_wa"], rows["mu_wa"] + 1, 1),
                                       (3 * RC + 1, rows["mu_g"], rows["mu_g"] + 1, 1)):
                    v.tensor_tensor(mu_mid[:, dst:dst + k], par[:, m0:m0 + k], par[:, m1:m1 + k], ADD)
                v.drain()
                v.tensor_scalar(mu_mid[:, :], mu_mid[:, :], -1.0, 1.0, MUL, ADD).then_inc(S["par_ready"], 1)
                norm(L * 3 + 1)
                turned_lo("ut_hi", "ut_ready", v.snap(L * 24), rows["norm0"])
                nsc = 0
                NSC = sum(b[0] in ("rw", "lora", "gdq") for b in blocks)
                for i, (kind, b, c0, tiles) in enumerate(blocks):
                    g = 4 * (i % 2)
                    end = SL_IN + KSLOTS * (i + 1)
                    split_lo(sl, end - KSLOTS + AHEAD, end + AHEAD)
                    if kind in ("rw", "lora", "gdq"):
                        nsc += 1
                        v.wait_ge(S["blk_scaled"], L * NSC + nsc)
                        groups = []
                        for c, w in enumerate(tiles):
                            if kind == "gdq":
                                z = zgd[:, 3 * b + c, :]
                                cols = [(k - TAPS // 2, rows["conv"] + k * 3 * GH + 3 * b + c) for k in range(TAPS) if k != TAPS // 2]
                            elif kind == "rw":
                                z = zrw[:, RC * b + c, :]
                                cols = [(-1, rows["mu"] + RC * b + c), (1, rows["mu1"] + RC * b + c)]
                            else:
                                z = zlora[0:w, c, :]
                                m = rows[("mu_wa", "mu_g")[c]]
                                cols = [(-1, m), (1, m + 1)]
                            groups.append((ps[g + c][0:w, :], z, [(o_, par[0:w, m:m + 1]) for o_, m in cols]))
                        last = add_taps(groups)
                    else:
                        v.wait_ge(S["slot_done"], sl + (RING + end))
                        if kind == "mlq":
                            for c in range(3):
                                last = v.tensor_copy(zmq[:, 3 * b + c, :], ps[g + c][:, 0:T])
                        else:
                            zt, w = (zgt, GT_W // 2) if kind == "gdt" else (zmt, MT_W // 4)
                            for t in range(NT):
                                last = v.tensor_copy(zt[:, t, w * b:w * b + w], ps[g + t][:, 0:w])
                    last.then_inc(S["blk_evac"], 1)

                for d in range(2):
                    v.memset(scores[d][:, :, :, :], 0.0)
                v.drain()
                for d in range(2):
                    v.tensor_copy(scores[d][:, :, 2, :], bmid(ident[:, :], 4))
                v.drain()
                with v.Fori(0, RC) as c:
                    v.wait_ge(S["gate_ready"], L + 1)
                    v.wait_ge(S["mixp_in"], L * MIXP_TOTAL + MIXP_TOTAL)
                    n = v.snap(L * RC + c)
                    n2 = v.snap(n * 2)
                    m2 = v.snap(L * (2 * (RC + GP)) + c * 2)
                    r_, k_, v_ = zrw[:, c, :], zrw[:, c + RC, :], zrw[:, c + 2 * RC, :]

                    def pcol(name):
                        return par[:, ds(c + rows[name], 1)]
                    v.tensor_copy(ch[:, 0, :], v_)
                    v.tensor_scalar(ch[:, 1, :], k_, pcol("k_k"), None, MUL)
                    v.drain()
                    v.tensor_tensor(ch[:, 2, :], ch[:, 1, :], ch[:, 1, :], MUL).then_inc(S["rw_sq"], 1)
                    for d in range(2):
                        sw = ew[d][:, 0, :]
                        v.tensor_copy(sw, swa[:, 0, d, c, :])
                        v.drain()
                        for t in range(NT):
                            o_, i_ = cs[d][:, t * P:(t + 1) * P], sw[:, t * P:(t + 1) * P]
                            if d:
                                o_, i_ = o_[:, ::-1], i_[:, ::-1]
                            v.tensor_tensor_scan(o_, i_, i_, 0.0, ADD, ALU.bypass)
                        v.drain()
                        v.tensor_copy(mid[d][:, 0:NT], cs[d][:, P // 2 - 1 + d:T:P])
                        v.drain()
                        for t in range(NT):
                            tt = cs[d][:, t * P:(t + 1) * P]
                            v.tensor_scalar(tt, tt, mid[d][:, t:t + 1], None, SUB)
                        v.drain()
                        F = FIRST[d]
                        e = F * P + LAST_COL[d]
                        v.tensor_tensor(mid[d][:, 2:3], cs[d][:, e:e + 1], mid[d][:, 1 - F:2 - F], ADD)
                        v.tensor_tensor(ew[d][:, 2, :], cs[d][:, :], sw, SUB).then_inc(S["rw_cs"], 1)
                    v.wait_ge(S["rw_rn"], n + 1)
                    v.tensor_tensor(ch[:, 4, :], ch[:, 1, :], ch[:, 3, :], MUL)
                    for d in range(2):
                        v.tensor_scalar(ch[:, 5, :], swa[:, 1, d, c, :], 1.0, pcol("k_a"), SUB, MUL)
                        v.drain()
                        v.scalar_tensor_tensor(KB[d][:, 0, :], ch[:, 5, :], 1.0, k_, ADD, MUL)
                        v.tensor_tensor(KB[d][:, 1, :], ch[:, 4, :], swa[:, 1, d, c, :], MUL)
                        v.drain()
                    v.tensor_tensor(ch[:, 3, :], KB[0][:, 0, :], KB[1][:, 0, :], ADD)
                    v.drain()
                    v.tensor_tensor(ch[:, 3, :], ch[:, 3, :], r_, MUL)
                    v.drain()
                    v.tensor_scalar(ch[:, 3, :], ch[:, 3, :], pcol("r_k"), None, MUL).then_inc(S["rw_cf"], 1)
                    for d in range(2):
                        v.wait_ge(S["rw_exp"], n2 + (d + 1))
                        v.tensor_tensor(KB[d][:, :, :], KB[d][:, :, :], bmid(ew[d][:, 1, :], 2), MUL)
                        v.scalar_tensor_tensor(AR[d][:, :, 0, :], third(ch[:, 4, :], 2), -1.0, third(ew[d][:, 2, :], 2), MUL, MUL)
                        v.tensor_tensor(AR[d][:, :, 1, :], third(r_, 2), third(ew[d][:, 0, :], 2), MUL).then_inc(S["rw_ops"], 1)
                    v.wait_ge(S["rw_coef"], n + 1)
                    v.tensor_copy(coef[:, :, :].rearrange("p t h -> p (t h)"), ps[0][:, 0:2 * NT]).then_inc(S["rw_coefc"], 1)
                    for d in range(2):
                        v.wait_ge(S["rw_sc"], n2 + (d + 1))
                        v.tensor_copy(st[:, 3, d:d + 1], ps[4 * d][:, 0:1])
                        for j in range(4):
                            last = v.copy_predicated(scores[d][:, j, :, :].rearrange("p a c -> p (a c)"),
                                                     pred[d][:, :, :].rearrange("p a c -> p (a c)").bitcast(I16), ps[4 * d + j][:, :])
                        last.then_inc(S["rw_masked"], 1)
                    v.drain()
                    for d in range(2):
                        v.wait_ge(S["rw_pv"], n2 + (d + 1))
                        v.tensor_copy(rf[d][:, 0, :], ps[4 * d + 3][:, 0:P])
                        v.tensor_copy(mono(KBt[d][:, :, :], 2), ps[4 * d + 3][:, T:2 * T]).then_inc(S["rw_rf"], 1)
                    invert(m2, lambda d: scores[d][:, :, 2, :])
                    for d in range(2):
                        v.wait_ge(S["rw_state"], n2 + (d + 1))
                        v.scalar_tensor_tensor(S0[d][:, 0, :], ps[4 * d + 1][:, 0:P], mid[d][:, 3:4], headones[:, :], MUL, MUL)\
                            .then_inc(S["rw_s0"], 1)
                    o2 = mono(OL[:, 0:2, :], 2)
                    v.wait_ge(S["rw_y"], n2 + 1)
                    v.tensor_copy(o2, ps[3][:, 0:T])
                    v.drain()
                    v.wait_ge(S["rw_y"], n2 + 2)
                    v.tensor_tensor(o2, o2, ps[7][:, 0:T], ADD)
                    v.drain()
                    h4 = o2.rearrange("p (g c) -> p g c", c=64)
                    t4 = mono(OT[:, 0:2, :], 2).rearrange("p (g c) -> p g c", c=64)
                    q4 = mono(OT[:, 2:4, :], 2).rearrange("p (g c) -> p g c", c=64)
                    v4 = mono(Vt[:, 0:2, :], 2).rearrange("p (g c) -> p g c", c=64)
                    v.tensor_reduce(st[:, 0, :], h4, AX_X, ADD)
                    v.drain()
                    v.tensor_scalar(st[:, 0, :], st[:, 0, :], 1.0 / 64, None, MUL)
                    v.drain()
                    v.tensor_tensor(t4, h4, bc(st[:, 0, :], 64), SUB)
                    v.drain()
                    v.tensor_tensor(q4, t4, t4, MUL)
                    v.drain()
                    v.tensor_reduce(st[:, 1, :], q4, AX_X, ADD).then_inc(S["rw_var"], 1)
                    v.tensor_tensor(h4, v4, bc(coef[:, :, :].rearrange("p t h -> p (t h)"), 64), MUL)
                    v.wait_ge(S["rw_rstd"], n + 1)
                    v.tensor_tensor(t4, t4, bc(st[:, 2, :], 64), MUL)
                    v.drain()
                    tt = OT[:, 0:2, :]
                    v.tensor_tensor(tt, tt, bmid(lnp[:, 0, ds(c * P, P)], 2), MUL)
                    v.drain()
                    v.tensor_tensor(tt, tt, bmid(lnp[:, 1, ds(c * P, P)], 2), ADD)
                    v.drain()
                    v.tensor_tensor(tt, tt, OL[:, 0:2, :], ADD)
                    v.drain()
                    v.tensor_tensor(YB[:, :, ds(c * P, P)], tt, sgate[:, :, ds(c * P, P)], MUL).then_inc(S["rw_done"], 1)

                NG = 2 * GH
                v.memset(V1[:, :, :, P:P + 1], 1.0)
                v.tensor_tensor(gx[:, 0, :, 0:NG], zgt[:, :, GW:GW + NG], bmid(gpar[:, 0, :], NT), ADD)
                v.tensor_scalar(gx[:, 0, :, NG:2 * NG], zgt[:, :, GW + NG:GW + 2 * NG], -1.0, None, MUL)
                v.drain()
                v.scalar_tensor_tensor(gx[:, 1, :, :], gx[:, 0, :, :], -1.0, gx[:, 0, :, :], MUL, MAX).then_inc(S["gd_sp"], 1)
                v.wait_ge(S["gd_ln"], L + 1)
                v.scalar_tensor_tensor(gx[:, 2, :, :], gx[:, 0, :, :], 0.0, gx[:, 1, :, :], MAX, ADD)
                v.drain()
                v.scalar_tensor_tensor(gates[:, 0, :, :], gx[:, 2, :, 0:NG], -1.0, bmid(gpar[:, 1, :], NT), MUL, MUL)
                v.tensor_scalar(gates[:, 1, :, :], gx[:, 2, :, NG:2 * NG], -1.0, None, MUL).then_inc(S["gd_gl"], 1)
                v.wait_ge(S["gd_cum"], L + 1)
                v.tensor_copy(gates[:, 2, :, :].rearrange("p t g -> p (t g)"), ps[0][:, 0:NT * NG])
                v.drain()
                v.tensor_tensor(gates[:, 4, :, :].rearrange("p t g -> p (t g)"), ps[0][:, 64:64 + NT * NG],
                                gates[:, 2, :, :].rearrange("p t g -> p (t g)"), SUB).then_inc(S["gd_cumc"], 1)
                gflat = gates[:, :, :, :].rearrange("p k t g -> p (k t g)").rearrange("p (a h) -> p a h", h=GH)
                with v.Fori(0, GP) as i:
                    v.wait_ge(S["gd_exp"], L + 1)
                    v.wait_ge(S["gd_silu"], L + 1)
                    n = v.snap(L * GP + i)
                    n2 = v.snap(n * 2)
                    m2 = v.snap(L * (2 * (RC + GP)) + (i * 2 + 2 * RC))
                    q_, k_, v_ = (zgd[:, ds(i * 2 + GH * j, 2), :] for j in range(3))
                    v.tensor_copy(gs[:, :, :], gflat[:, :, ds(i * 2, 2)])
                    v.tensor_copy(chg, v_)
                    v.tensor_tensor(KB[0][:, :, :], q_, q_, MUL)
                    v.tensor_tensor(KB[1][:, :, :], k_, k_, MUL).then_inc(S["gd_sq"], 1)
                    v.wait_ge(S["gd_rn"], n + 1)
                    for h in range(2):
                        kh, qh = zgd[:, i * 2 + (GH + h), :], zgd[:, i * 2 + h, :]
                        v.tensor_tensor(AR[h][:, :, 0, :], third(kh, 2), third(ewg[1][:, h, :], 2), MUL)
                        last = v.scalar_tensor_tensor(AR[h][:, :, 1, :], third(qh, 2), P ** -0.5, third(ewg[0][:, h, :], 2), MUL, MUL)
                    last.then_inc(S["gd_qk"], 1)
                    for d in range(2):
                        v.wait_ge(S["gd_gb"], n2 + (d + 1))
                        for j in range(2):
                            for h in range(2):
                                for t in range(NT):
                                    u = 2 * h + t
                                    last = v.tensor_scalar(scores[d][:, j, u, :], ps[4 * d + j][:, u * P:(u + 1) * P],
                                                           gs[:, 8 + 2 * t + d, h:h + 1], 0.0, SUB, MIN)
                        last.then_inc(S["gd_arg"], 1)
                    v.wait_ge(S["gd_sc"], n + 1)
                    for d in range(2):
                        v.wait_ge(S["gd_dm"], n2 + (d + 1))
                        for h in range(2):
                            pp = ps[6 + h][:, :].rearrange("p (t j c) -> p t j c", t=2, j=2)
                            for j in range(2):
                                v.tensor_tensor(scores[d][:, 2 + j, 2 * h:2 * h + 2, :], pp[:, :, j, :],
                                                scores[d][:, j, 2 * h:2 * h + 2, :], MUL)
                        v.drain()
                        v.tensor_tensor(scores[d][:, 2, :, :], scores[d][:, 2, :, :], bmid(ident[:, :], 4), ADD)\
                            .then_inc(S["gd_nt"], 1)
                    v.drain()
                    invert(m2, lambda d: scores[d][:, 2, :, :])
                    v.wait_ge(S["gd_vtc"], n + 1)
                    v.wait_ge(S["gd_ktc"], n + 1)
                    for d in range(2):
                        F = FIRST[d]
                        for h in range(2):
                            for t in range(NT):
                                v.tensor_scalar(TN[d][:, 2 * h + t, :], Vt[:, 2 * h + t, :], gs[:, 20 + 2 * t + d, h:h + 1], None, MUL)
                            v.tensor_scalar(XS[d][:, h, :], OT[:, 2 * h + F, :], gs[:, 16 + 2 * F + d, h:h + 1], None, MUL)
                        v.scalar_tensor_tensor(gs[:, 4 + d:8 + d:2, :], gs[:, 20 + d:24:2, :], -1.0, gs[:, 12 + d:16:2, :], MUL, MUL)\
                            .then_inc(S["gd_rhs"], 1)
                    for d in range(2):
                        v.wait_ge(S["gd_state"], n2 + (d + 1))
                        v.tensor_copy(mono(S0g[d], 2), ps[4 * d + 1][:, 0:T]).then_inc(S["gd_s0"], 1)
                    for d in range(2):
                        B = 1 - FIRST[d]
                        v.wait_ge(S["gd_ks"], n2 + (d + 1))
                        for h in range(2):
                            v.scalar_tensor_tensor(rf[d][:, h, :], ps[4 * d + 2][:, h * P:(h + 1) * P], gs[:, 4 + 2 * B + d, h:h + 1],
                                                   TN[d][:, 2 * h + B, :], MUL, ADD)
                            last = v.tensor_scalar(XS[d][:, 2 + h, :], ps[4 * d + 2][:, (2 + h) * P:(3 + h) * P],
                                                   gs[:, 12 + 2 * B + d, h:h + 1], None, MUL)
                        last.then_inc(S["gd_rs"], 1)
                    o4 = OL.rearrange("p (h t) c -> p h t c", h=2)
                    for d in range(2):
                        v.wait_ge(S["gd_y"], n2 + (d + 1))
                        if d == 0:
                            v.tensor_copy(mono(OL, 4), ps[3][:, :])
                        else:
                            v.tensor_tensor(mono(OL, 4), mono(OL, 4), ps[7][:, :], ADD)
                        v.drain()
                        ob = o4[:, :, 1 - FIRST[d], :]
                        v.tensor_tensor(ob, ob, XS[d][:, 2:4, :], ADD)
                        v.drain()
                    head_out(i, n, "gd", lambda h: bmid(gdn[:, :], 2),
                             lambda t: zgt[:, t, ds(i * T, T)].rearrange("p (h c) -> p h c", h=2), RW)

                NM = 2 * MH
                for j in range(2):
                    last = v.tensor_tensor(gx[:, 0, :, NM * j:NM * (j + 1)], zmt[:, :, 2 * MW + NM * j:2 * MW + NM * (j + 1)],
                                           bmid(gpar[:, 2 + j, :], NT), ADD)
                last.then_inc(S["ml_x"], 1)
                v.wait_ge(S["ml_tanh"], L + 1)
                v.tensor_scalar(gx[:, 0, :, 0:NM], gx[:, 1, :, 0:NM], ML_GATE_CAP, None, MUL)
                v.tensor_scalar(gx[:, 0, :, NM:2 * NM], gx[:, 1, :, NM:2 * NM], -ML_GATE_CAP, None, MUL)
                v.drain()
                fy = gx[:, 0, :, NM:2 * NM]
                v.scalar_tensor_tensor(gx[:, 1, :, NM:2 * NM], fy, -1.0, fy, MUL, MAX).then_inc(S["ml_f"], 1)
                v.wait_ge(S["ml_ln"], L + 1)
                v.scalar_tensor_tensor(fy, fy, 0.0, gx[:, 1, :, NM:2 * NM], MAX, ADD)
                v.drain()
                v.tensor_scalar(fy, fy, -1.0, None, MUL).then_inc(S["ml_g"], 1)
                v.wait_ge(S["ml_rt"], L + 1)
                lf_r, F_r, e_r, M_r, m_r = (mono(b_[0:MH, :, :], 4) for b_ in (XS[0], XS[1], TN[0], TN[1], TT[0]))
                v.tensor_copy(lf_r, ps[1][0:MH, :])
                v.drain()

                def halves(ap):
                    return ap[:, 0:T], ap[:, T:2 * T][:, ::-1]
                for o_, i_ in zip(halves(F_r), halves(lf_r)):
                    v.tensor_tensor_scan(o_, i_, i_, 0.0, ADD, ALU.bypass)
                v.drain()
                v.tensor_tensor(e_r, ps[0][0:MH, :], F_r, SUB)
                v.drain()
                for o_, i_ in zip(halves(M_r), halves(e_r)):
                    v.tensor_tensor_scan(o_, i_, i_, 0.0, MAX, ALU.bypass)
                v.drain()
                v.tensor_tensor(m_r, F_r, M_r, ADD).then_inc(S["ml_rows"], 1)
                v.wait_ge(S["ml_back"], L + 1)
                v.tensor_copy(gates[:, 0:2, :, :].rearrange("p k t g -> p (k t g)"), ps[2][:, 0:8 * MH]).then_inc(S["ml_backc"], 1)
                with v.Fori(0, MP) as i:
                    v.wait_ge(S["ml_expm"], L + 1)
                    v.wait_ge(S["ml_sig"], L + 1)
                    v.wait_ge(S["mln_in"], L * 16 + 16)
                    n = v.snap(L * MP + i)
                    n2 = v.snap(n * 2)
                    v.tensor_copy(gs[:, 0:12, :], gflat[:, 0:12, ds(i * 2, 2)])
                    v.tensor_scalar(KB[0][:, 0, :], zmq[:, i, :], 64 ** -0.5, None, MUL)
                    v.tensor_copy(KB[0][:, 1, :], zmq[:, i + MP, :])
                    for j in range(NT):
                        v.tensor_copy(V1[:, j, :, 0:P], zmt[:, j, ds(i * T, T)].rearrange("p (h c) -> p h c", h=2))
                    v.tensor_copy(small[0:MH, 8:10], ident[0:MH, ds(i * 2, 2)]).then_inc(S["ml_in"], 1)
                    v.drain()
                    for d in range(2):
                        v.wait_ge(S["ml_mb"], n2 + (d + 1))
                        for h in range(2):
                            for j in range(NT):
                                last = v.tensor_scalar(ml_flat(d)[:, h, j, :], ps[4 + d][:, h * T:(h + 1) * T],
                                                       gs[:, 2 * d + j, h:h + 1], 0.0, SUB, MAX)
                        last.then_inc(S["ml_arg"], 1)
                    v.wait_ge(S["ml_sc"], n + 1)
                    for d in range(2):
                        v.wait_ge(S["ml_dm"], n2 + (d + 1))
                        for h in range(2):
                            w = ml_flat(d)[:, h, :, :].rearrange("p j t -> p (j t)")
                            last = v.tensor_tensor(w, w, ps[h][:, :], MUL)
                        last.then_inc(S["ml_p"], 1)
                    o4 = OL.rearrange("p (h t) c -> p h t c", h=2)
                    for d in range(2):
                        v.wait_ge(S["ml_num"], n2 + (d + 1))
                        nd = [ps[4 * d + 2 + h][:, 0:2 * (P + 1)].rearrange("p (t c) -> p t c", t=2) for h in range(2)]
                        for h in range(2):
                            v.tensor_scalar(st[:, 3, 2 * h:2 * h + 2], nd[h][:, :, P], -1.0, None, MUL)
                        v.drain()
                        for h in range(2):
                            v.tensor_tensor(st[:, 0, 2 * h:2 * h + 2], nd[h][:, :, P], st[:, 3, 2 * h:2 * h + 2], MAX)
                        v.drain()
                        for h in range(2):
                            v.tensor_tensor(st[:, 0, 2 * h:2 * h + 2], st[:, 0, 2 * h:2 * h + 2], gs[:, 8 + 2 * d:10 + 2 * d, h], MAX)
                        v.drain()
                        v.reciprocal(st[:, 0, :], st[:, 0, :])
                        v.drain()
                        dst = OL if d == 0 else OT
                        for h in range(2):
                            v.tensor_tensor(dst[:, 2 * h:2 * h + 2, :], nd[h][:, :, 0:P], bc(st[:, 0, 2 * h:2 * h + 2], P), MUL)
                        v.drain()
                    v.tensor_tensor(OL, OL, OT, ADD)
                    head_out(i, n, "ml", lambda h: bmid(mln[:, ds(i * T + h * P, P)], 2),
                             lambda t: zmt[:, t, ds(i * T + MW, T)].rearrange("p (h c) -> p h c", h=2), RW + GW)
                v.drain().then_inc(S["mixp_free"], 1)

                turned_lo("yt_hi", "yt_ready", v.snap(L * 8))
                residual(SL_OUT, KT, sl)
                norm(L * 3 + 2)
                turned_lo("ut_hi", "ut_ready", v.snap(L * 24 + 8), rows["norm1"])
                with v.Fori(0, NU) as i:
                    n = v.snap(L * NU + i)
                    sli = v.snap(L * SL + i * (2 * KSLOTS))
                    for g in range(2):
                        end = SL_UP + KSLOTS * (g + 1)
                        split_lo(sli, end - KSLOTS + AHEAD, end + AHEAD)
                        if g == 1:
                            v.wait_ge(S["up_silu"], n + 1)
                        v.wait_ge(S["up_vact" if g else "up_gact"], n + 1)
                        groups = []
                        for c in range(4):
                            taps = [(k - FTAPS // 2, par[:, ds(i * 4 + (rows["fconv"] + k * 2 * FT + FT * g + c), 1)])
                                    for k in range(FTAPS) if k != FTAPS // 2]
                            groups.append((ps[4 * g + c], up_buf(g)[:, c, :], taps))
                        last = add_taps(groups)
                        last.then_inc(S["up_vconv" if g else "up_gconv"], 1)
                residual(SL_DOWN, FT, sl)
                norm(L * 3 + 3)
                turned_lo("ut_hi", "ut_ready", v.snap(L * 24 + 16), rows["norm2"])
                v.wait_ge(S["p_turned"], L + 1)
                v.tensor_copy(pT[:, :, :].rearrange("p k t -> p (k t)"), ps[7][:, :])
                v.drain().then_inc(S["pt_ready"], 1)
                for i in range(NO):
                    end = SL_PLE + KSLOTS * (i + 1)
                    split_lo(sl, end - KSLOTS + AHEAD, end + AHEAD)
                    v.wait_ge(S["ple_sig"], L * NO + (i + 1))
                    v.wait_ge(S["ple_psum"], L * NO + (i + 1))
                    for t in range(NT):
                        s_ = mono(TN[t][:, :, :], 4)
                        v.tensor_tensor(s_, s_, ps[4 * (i % 2) + 2 + t][:, :], MUL)
                    v.drain()
                    for t in range(NT):
                        hh = H[:, t, 512 * i:512 * i + 512]
                        last = v.tensor_tensor(hh, hh, mono(TN[t][:, :, :], 4), ADD)
                    last.then_inc(S["ple_done"], 1)
                v.drain().then_inc(S["h_ready"], 1)
            v.wait_ge(S["rms_ready"], 3 * DEPTH + 1)
            v.reciprocal(small[:, 4:4 + NT], small[:, 2:2 + NT])
            v.wait_ge(S["nf_in"], 16)
            v.drain()
            for t in range(NT):
                v.scalar_tensor_tensor(YB[:, t, :], H[:, t, :], small[:, 4 + t:5 + t], Z[:, 0:D], MUL, MUL).then_inc(S["fin_out"], 1)


_INS = ["x", "p", "norm_mix", "w_in", "rw_shift_mu", "rw_w0", "rw_w2", "rw_a0", "rw_a2", "rw_g2", "rw_k_k", "rw_k_a",
        "rw_r_k", "rw_ln_g", "rw_ln_b", "gd_conv_w", "gd_a_log", "gd_dt_bias", "gd_norm_g", "ml_i_bias", "ml_f_bias",
        "ml_norm_g", "w_out", "norm_ffn", "w_up", "ffn_conv_w", "ffn_conv_b", "w_down", "norm_ple", "w_ple_gate",
        "w_ple_proj", "norm_final"]


def kernel(**inputs):
    import numpy as _np
    import concourse.bacc as _bacc
    from concourse import mybir as _mybir
    from concourse.bass_utils import run_bass_kernel_spmd as _run

    nc = _bacc.Bacc("TRN2", target_bir_lowering=False, num_devices=1, dynamic_dma_scratch_size=256)
    arrays, args = {}, []
    for name in _INS:
        a = _np.ascontiguousarray(inputs[name])
        arrays[f"in_{name}_dram"] = a
        args.append(nc.dram_tensor(f"in_{name}_dram", a.shape, _mybir.dt.from_np(a.dtype), kind="ExternalInput").ap())
    shape = _np.asarray(inputs["x"]).shape
    args.append(nc.dram_tensor("out_0_dram", shape, _mybir.dt.float32, kind="ExternalOutput").ap())
    trunk(nc, *args)
    r = _run(nc, [arrays], core_ids=[0])
    return r.results[0]["out_0_dram"]
```

```python
from contextlib import ExitStack
import math

import concourse.bass as bass
from concourse import mybir
from concourse.bass import ds

F32 = mybir.dt.float32
F32R = mybir.dt.float32r
BF16 = mybir.dt.bfloat16
I16 = mybir.dt.int16
ALU = mybir.AluOpType
ACT = mybir.ActivationFunctionType
AX_X = mybir.AxisListType.X

P = 128
EPS = 1e-6
RW_LN_EPS = 64e-5
ML_GATE_CAP = 15.0
KAPPA = math.exp(-0.5)


def trunk(nc, x, p, norm_mix, w_in, rw_shift_mu, rw_w0, rw_w2, rw_a0, rw_a2, rw_g2, rw_k_k, rw_k_a,
          rw_r_k, rw_ln_g, rw_ln_b, gd_conv_w, gd_a_log, gd_dt_bias, gd_norm_g, ml_i_bias, ml_f_bias,
          ml_norm_g, w_out, norm_ffn, w_up, ffn_conv_w, ffn_conv_b, w_down, norm_ple, w_ple_gate,
          w_ple_proj, norm_final, out):
    DEPTH, D, N_IN = w_in.shape
    T = x.shape[1]
    NT = T // P
    KT = D // P
    RW = rw_w0.shape[2]
    RC = RW // P
    RD, RG = rw_w2.shape[2], rw_g2.shape[1]
    GH = gd_a_log.shape[2]
    GW = GH * P
    MH = ml_i_bias.shape[2]
    MW = MH * P
    GP, MP = GH // 2, MH // 2
    TAPS, FTAPS = gd_conv_w.shape[1], ffn_conv_w.shape[1]
    FF = w_down.shape[1]
    FT = FF // P
    PLE = p.shape[3]
    assert NT == 2 and GP == MP and rw_a2.shape[2] == RD and 2 * RD <= 64 and GH % 2 == 0 and MH % 2 == 0

    RING, KS = 4, 2
    KSLOTS = KT // KS
    RW_C0, GQ_C0 = 0, 3 * RW + 2 * RD + RG
    GT_C0 = GQ_C0 + 3 * GW
    MQ_C0 = GT_C0 + GW + 4 * GH
    MT_C0 = MQ_C0 + MH * P
    GT_W, MT_W = GW + 4 * GH, 2 * MW + 4 * MH
    assert MT_C0 + MT_W == N_IN
    blocks = [("rw", b, RW_C0 + RW * b, [P] * RC) for b in range(3)]
    blocks += [("lora", 0, 3 * RW, [2 * RD, RG])]
    blocks += [("gdq", b, GQ_C0 + 3 * P * b, [P] * 3) for b in range(3 * GH // 3)]
    blocks += [("gdt", b, GT_C0 + GT_W // 2 * b, None) for b in range(2)]
    blocks += [("mlq", b, MQ_C0 + 3 * P * b, [P] * 3) for b in range(MH // 3)]
    blocks += [("mlt", b, MT_C0 + MT_W // 4 * b, None) for b in range(4)]
    NB = len(blocks)

    def width(block):
        if block[0] == "lora":
            return 2 * RD + P
        return sum(block[3]) if block[3] else (GT_W // 2 if block[0] == "gdt" else MT_W // 4)

    NO = D // 512
    NU = FT // 4
    SL_IN = 0
    SL_OUT = SL_IN + KSLOTS * NB
    SL_UP = SL_OUT + KSLOTS * NO
    SL_DOWN = SL_UP + 2 * KSLOTS * NU
    SL_PLE = SL_DOWN + NO * FT // KS
    SL = SL_PLE + KSLOTS * NO
    AHEAD = RING - 1

    def slot_width(slot):
        return width(blocks[slot // KSLOTS]) if slot < SL_OUT else 512
    assert SL % RING == 0 and all(s % RING == 0 for s in (SL_OUT, SL_UP, SL_DOWN, SL_PLE, 2 * KSLOTS))

    rows, NR = {}, 0
    for name, n in (("norm0", KT), ("norm1", KT), ("norm2", KT), ("mu", 6 * RC), ("w0", 2 * RC), ("a0", 2 * RC),
                    ("k_k", RC), ("k_a", RC), ("r_k", RC), ("conv", TAPS * 3 * GH), ("fconv", FTAPS * 2 * FT),
                    ("fbias", 2 * FT), ("mu_wa", 2), ("mu_g", 2)):
        rows[name] = NR
        NR += n
    PT = -(-NR // P)

    with ExitStack() as ctx:
        def mono(ap, k=None):
            return ap.rearrange("p a c -> p (a c)")

        def sem(name):
            return ctx.enter_context(nc.semaphore(name))

        place = nc.sbuf_base // 32 * 32 + 32

        def at(name, shape, offset, dt=F32):
            return nc.alloc_sbuf_tensor_at(name, shape, dt, offset=offset)

        def sb(name, shape, dt=F32):
            nonlocal place
            tensor = at(name, shape, place, dt)
            place += -(-math.prod(shape[1:]) * (2 if dt == BF16 else 4) // 32) * 32
            return tensor

        H = sb("H", [P, NT, D])
        ring = sb("ring", [P, RING, KS, 512])
        whi = sb("whi", [P, RING, KS, 512], F32R)
        wlo = sb("wlo", [P, RING, KS, 512], F32R)
        u_place = place
        uhi = sb("uhi", [P, KT, T], F32R)
        ulo = sb("ulo", [P, KT, T], F32R)
        UA = at("UA", [P, KT, T], u_place)
        swa = UA[:, :, :].rearrange("p (k c d) t -> p k d c t", k=2, d=2)
        sc1_place = u_place + 4 * KT * T

        par = sb("par", [P, PT * P])
        mu_mid = sb("mu_mid", [P, 3 * RC + 2])
        lnp = sb("lnp", [P, 2, RW])
        gdn = sb("gdn", [P, P])
        gpar = sb("gpar", [P, 4, 2 * GH])
        ident = sb("ident", [P, P])
        ones = sb("ones", [P, P])
        headones = sb("headones", [P, P])
        incl = [sb(f"incl{d}", [P, P]) for d in range(2)]
        negstrict = [sb(f"negstrict{d}", [P, P]) for d in range(2)]
        LEVELS = 7
        lev = [sb(f"lev{d}", [P, LEVELS, P], BF16) for d in range(2)]
        pred = [sb(f"pred{d}", [P, 4, P], BF16) for d in range(2)]
        one_h = sb("one_h", [P, P], BF16)
        epsb = sb("epsb", [P, 4])
        small = sb("small", [P, 16])
        ssum = sb("ssum", [P, NT * D // 512])
        heads = sb("heads", [P, 12, P])
        OL, OT, Vt = heads[:, 0:4, :], heads[:, 4:8, :], heads[:, 8:12, :]
        prow = heads[:, 0:PT, :]
        pin = mono(heads[:, PT:PT + NT * PLE // P, :]).rearrange("p (t c) -> p t c", t=NT)
        coef = sb("coef", [P, NT, 2])
        st = sb("st", [P, 4, 4])
        mid = [sb(f"mid{d}", [P, 8]) for d in range(2)]
        gates = sb("gates", [P, 6, NT, 2 * GH])
        gs = sb("gs", [P, 24, 2])
        gx = sb("gx", [P, 3, NT, 4 * GH])
        gy = sb("gy", [P, 2, NT, 4 * MH])
        mgates = sb("mgates", [P, 3, NT, 2 * MH])
        mgs = sb("mgs", [P, 12, 2])

        arena = place
        g_bytes = 4 * FT * T
        ghi = at("ghi", [P, FT, T], arena, F32R)
        glo = at("glo", [P, FT, T], arena + g_bytes, F32R)
        zwords = RC * 3 * T + 2 * T + 3 * GH * T + NT * GT_W + MH * T + NT * MT_W
        Z = sb("Z", [P, zwords])
        scores = [sb("scores0", [P, 4, 4, P]), at("scores1", [P, 4, 4, P], sc1_place)]
        TN = [sb(f"TN{d}", [P, 4, P]) for d in range(2)]
        TT = [sb(f"TT{d}", [P, 4, P]) for d in range(2)]
        XS = [sb(f"XS{d}", [P, 4, P]) for d in range(2)]
        AR = [at(f"AR{d}", [P, NT, 2, P], sc1_place + 8192 + 2048 * d) for d in range(2)]
        KB = [at(f"KB{d}", [P, 2, T], sc1_place + 12288 + 2048 * d) for d in range(2)]
        KBt = [sb(f"KBt{d}", [P, 2, P]) for d in range(2)]
        rf = [sb(f"rf{d}", [P, 2, P]) for d in range(2)]
        cs = [sb(f"cs{d}", [P, T]) for d in range(2)]
        sgate = sb("sgate", [P, NT, RW])
        YB = sb("YB", [P, NT, D])
        assert arena + 2 * g_bytes <= place - 8 * D + 4 * RW
        projw = YB[:, :, :].rearrange("p k n -> p (k n)").rearrange("p (k n) -> p k n", k=PLE // P)
        o = 0

        def zpart(n):
            nonlocal o
            o += n
            return Z[:, o - n:o]
        zrw = zpart(3 * RC * T).rearrange("p (c t) -> p c t", t=T)
        zlora = zpart(2 * T).rearrange("p (c t) -> p c t", t=T)
        zgd = zpart(3 * GH * T).rearrange("p (c t) -> p c t", t=T)
        zgt = zpart(NT * GT_W).rearrange("p (t c) -> p t c", t=NT)
        zmq = zpart(MH * T).rearrange("p (c t) -> p c t", t=T)
        zmt = zpart(NT * MT_W).rearrange("p (t c) -> p t c", t=NT)

        w2sb = YB[0:2 * RD, 0, RW:3 * RW].rearrange("p (d c) -> p d c", d=2)
        g2sb = YB[0:RG, 1, RW:2 * RW]
        ew = [YB[:, 1, RW + 3 * T * d:RW + 3 * T * (d + 1)].rearrange("p (k t) -> p k t", k=3) for d in range(2)]
        ch = YB[:, 0, RW:RW + 6 * T].rearrange("p (k t) -> p k t", k=6)
        chg = UA[:, 0:2, :]
        ewg = [UA[:, 2 + 2 * j:4 + 2 * j, :] for j in range(2)]
        mln = UA[:, 6:9, :].rearrange("p k t -> p (k t)")[:, 0:MW]
        V1 = UA[:, 9:12, :].rearrange("p k t -> p (k t)")[:, 0:NT * 2 * (P + 2)]\
            .rearrange("p (j h c) -> p j h c", j=NT, h=2)
        mrow = [cs[d][0:MH, 0:T] for d in range(2)]
        msq = mono(KB[1][:, :, :]).rearrange("p (k c) -> p k c", c=P)
        uf = [XS[d][:, 2:4, :] for d in range(2)]
        S0 = [XS[d][:, 0:2, :] for d in range(2)]
        ufg = [scores[d][:, 0, 2:4, :] for d in range(2)]
        S0g = [scores[d][:, 0, 0:2, :] for d in range(2)]
        pT = XS[0][:, :, :].rearrange("p a c -> p (a c)").rearrange("p (k t) -> p k t", t=T)

        ps = [ctx.enter_context(nc.psum_tensor(f"ps{i}", [P, 512], F32)) for i in range(8)]


        NAMES = """consts masks h_in rows_in mixp_in pin_in proj_in nf_in row_free mixp_free w2_in mln_in
            landed0 landed1 landed2 landed3 hi_ready lo_ready slot_done par_turned par_ready h_ready h_chunk rms_ready rstd_ready u_ready0 u_ready1 ut_psum ut_hi ut_ready
            blk_scaled blk_evac lora_act lora_psum lora_ready gate_psum gate_ready
            rw_sq rw_ssq rw_rn rw_vt rw_vtc rw_cs rw_exp rw_cf rw_coef rw_coefc rw_ops rw_sc rw_masked rw_pv rw_rf
            inv_t1 inv_t1p inv_tn1 inv_x inv_xs inv_t inv_tn inv_tt0 inv_tt1
            rw_u rw_uf rw_state rw_s0 rw_pv2 rw_rf2 rw_u2 rw_uf2 rw_y rw_yc rw_var rw_rstd rw_done
            gd_sp gd_ln gd_gl gd_cum gd_cumc gd_exp gd_silu gd_sq gd_ssq gd_rn gd_vt gd_vtc gd_qk gd_kt gd_ktc gd_sc
            gd_gb gd_arg gd_d gd_dm gd_nt gd_rhs gd_u gd_uf gd_state gd_s0 gd_ks gd_rs gd_us gd_usc gd_y gd_yc
            gd_ss gd_rstd gd_done
            ml_x ml_tanh ml_f ml_ln ml_g ml_rt ml_rows ml_back ml_backc ml_expm ml_sig ml_in ml_sc ml_mb ml_arg ml_d
            ml_dm ml_p ml_num ml_numc ml_ss ml_rstd ml_done
            yt_psum yt_hi yt_ready up_gact up_gconv up_silu up_vact up_vconv up_done p_turned pt_ready ple_psum ple_sig
            fin_out out_done""".split()
        S = {n: sem(n) for n in NAMES}

        block = ctx.enter_context(nc.Block())
        FIRST = (0, NT - 1)
        LAST_COL = (P - 1, 0)
        LEV = LEVELS - 1
        assert LEV % 2 == 0

        def bc(ap, n):
            return ap.unsqueeze(2).to_broadcast([ap.shape[0], ap.shape[1], n])

        def bmid(ap, n):
            return ap.unsqueeze(1).to_broadcast([ap.shape[0], n, ap.shape[1]])

        w_in_v = w_in.rearrange("l (k p) n -> l p k n", p=P)
        w_out_v = w_out.rearrange("l (k p) n -> l p k n", p=P)
        w_up_v = w_up.rearrange("l (k p) n -> l p k n", p=P)
        w_down_v = w_down.rearrange("l (k p) n -> l p k n", p=P)
        w_pg_v = w_ple_gate.rearrange("l (k p) n -> l p k n", p=P)


        ROW_SRC = (("norm0", lambda L: norm_mix[L].rearrange("(c p) -> c p", p=P), KT),
                   ("norm1", lambda L: norm_ffn[L].rearrange("(c p) -> c p", p=P), KT),
                   ("norm2", lambda L: norm_ple[L].rearrange("(c p) -> c p", p=P), KT),
                   ("mu", lambda L: rw_shift_mu[L, 0, 0:3 * RW].rearrange("(c p) -> c p", p=P), 3 * RC),
                   ("mu1", lambda L: rw_shift_mu[L, 1, 0:3 * RW].rearrange("(c p) -> c p", p=P), 3 * RC),
                   ("w0", lambda L: rw_w0[L].rearrange("d (c p) -> (d c) p", p=P), 2 * RC),
                   ("a0", lambda L: rw_a0[L].rearrange("d (c p) -> (d c) p", p=P), 2 * RC),
                   ("k_k", lambda L: rw_k_k[L].rearrange("(c p) -> c p", p=P), RC),
                   ("k_a", lambda L: rw_k_a[L].rearrange("(c p) -> c p", p=P), RC),
                   ("r_k", lambda L: rw_r_k[L].rearrange("(c h) j -> c (h j)", h=2), RC),
                   ("conv", lambda L: gd_conv_w[L].rearrange("k (c p) -> (k c) p", p=P), TAPS * 3 * GH),
                   ("fconv", lambda L: ffn_conv_w[L].rearrange("k (c p) -> (k c) p", p=P), FTAPS * 2 * FT),
                   ("fbias", lambda L: ffn_conv_b[L].rearrange("(c p) -> c p", p=P), 2 * FT),
                   ("mu_wa", lambda L: rw_shift_mu[L, :, 3 * RW:3 * RW + 2 * RD], 2),
                   ("mu_g", lambda L: rw_shift_mu[L, :, 3 * RW + 2 * RD:3 * RW + 2 * RD + RG], 2))
        rows["mu1"] = rows["mu"] + 3 * RC

        def row_pieces():
            for name, src, n in ROW_SRC:
                r, done = rows[name], 0
                while done < n:
                    k = min(n - done, P - (r + done) % P)
                    yield done, (r + done) // P, (r + done) % P, k, src
                    done += k
        ROWS_TOTAL = 16 * len(list(row_pieces()))

        def mixer_params(L):
            yield lnp[:, 0, :], rw_ln_g[L].partition_broadcast(P)
            yield lnp[:, 1, :], rw_ln_b[L].partition_broadcast(P)
            yield gdn[:, :], gd_norm_g[L].partition_broadcast(P)
            for i, src in enumerate((gd_dt_bias, gd_a_log, ml_i_bias, ml_f_bias)):
                yield gpar[:, i, :], src[L].rearrange("d h -> (d h)").partition_broadcast(P)
        MIXP_TOTAL = 16 * len(list(mixer_params(0)))

        def ml_flat(d):
            return scores[d][:, :, :, :].rearrange("p a b c -> p (a b c)")[:, 0:4 * T]\
                .rearrange("p (h j t) -> p h j t", h=2, j=2)

        def ml_diag(d):
            flat = scores[d][:, :, :, :].rearrange("p a b c -> p (a b c)")
            return [flat[:, h * 2 * T:(h + 1) * 2 * T].rearrange("p (u c) -> p u c", c=P)[:, 0:4:3, :] for h in range(2)]

        def third(ap, k):
            return ap.rearrange("p (k c) -> p k c", k=k)

        def up_buf(g):
            return YB[:, 1, 4 * T * g:4 * T * (g + 1)].rearrange("p (c t) -> p c t", t=T)

        @block.sync
        def _(sp):
            for t in range(NT):
                sp.dma_start(H[:, t, :], x[0, t * P:(t + 1) * P, :]).then_inc(S["h_in"], 16)
            with sp.Fori(0, DEPTH) as L:
                base = sp.snap(L * SL)

                def load(slot, src, w, n):
                    sp.wait_ge(S["lo_ready"], n + (slot + 1))
                    sp.dma_start(ring[:, slot % RING, :, 0:w], src).then_inc(S[f"landed{slot % RING}"], 16)

                sp.wait_ge(S["consts"], 1)
                sp.wait_ge(S["row_free"], L + 1)
                sp.wait_ge(S["mixp_free"], L + 1)
                for r, tile, p0, k, src in row_pieces():
                    a = src(L)[r:r + k, :]
                    sp.dma_start(prow[p0:p0 + k, tile, 0:a.shape[1]], a).then_inc(S["rows_in"], 16)
                for dst, src in mixer_params(L):
                    sp.dma_start(dst, src).then_inc(S["mixp_in"], 16)
                for i, b in enumerate(blocks):
                    if i == 1:
                        sp.wait_ge(S["ut_ready"], L * 24 + 8)
                        sp.dma_start(w2sb[0:RD], rw_w2[L].rearrange("d r c -> r d c")).then_inc(S["w2_in"], 16)
                        sp.dma_start(w2sb[RD:2 * RD], rw_a2[L].rearrange("d r c -> r d c")).then_inc(S["w2_in"], 16)
                        sp.dma_start(g2sb, rw_g2[L]).then_inc(S["w2_in"], 16)
                    for k in range(KSLOTS):
                        load(SL_IN + KSLOTS * i + k, w_in_v[L, :, KS * k:KS * k + KS, b[2]:b[2] + width(b)], width(b), base)
                for i in range(NO):
                    for k in range(KSLOTS):
                        if i == 0 and k == AHEAD:
                            sp.wait_ge(S["rw_done"], L * RC + RC)
                            sp.dma_start(mln, ml_norm_g[L].partition_broadcast(P)).then_inc(S["mln_in"], 16)
                        load(SL_OUT + KSLOTS * i + k, w_out_v[L, :, KS * k:KS * k + KS, 512 * i:512 * i + 512], 512, base)
                with sp.Fori(0, NU) as i:
                    n = sp.snap(base + i * (2 * KSLOTS))
                    for g in range(2):
                        for k in range(KSLOTS):
                            load(SL_UP + KSLOTS * g + k, w_up_v[L, :, KS * k:KS * k + KS, ds(i * 512 + g * FF, 512)], 512, n)
                sp.wait_ge(S["ut_ready"], L * 24 + 16)
                sp.dma_start(pin, p[L, 0].rearrange("(t q) c -> q t c", q=P)).then_inc(S["pin_in"], 16)
                for i in range(NO):
                    for k in range(FT // KS):
                        load(SL_DOWN + FT // KS * i + k,
                             w_down_v[L, :, KS * k:KS * k + KS, 512 * i:512 * i + 512], 512, base)
                for i in range(NO):
                    if i == 1:
                        sp.wait_ge(S["ut_ready"], L * 24 + 24)
                        sp.dma_start(projw, w_ple_proj[L].rearrange("(k q) n -> q k n", q=P)).then_inc(S["proj_in"], 16)
                    for k in range(KSLOTS):
                        load(SL_PLE + KSLOTS * i + k, w_pg_v[L, :, KS * k:KS * k + KS, 512 * i:512 * i + 512], 512, base)
            sp.wait_ge(S["h_ready"], 3 * DEPTH + 1)
            sp.dma_start(Z[:, 0:D], norm_final.partition_broadcast(P)).then_inc(S["nf_in"], 16)
            for t in range(NT):
                sp.wait_ge(S["fin_out"], t + 1)
                sp.dma_start(out[0, t * P:(t + 1) * P, :], YB[:, t, :]).then_inc(S["out_done"], 16)
            sp.wait_ge(S["out_done"], 16 * NT)

        @block.gpsimd
        def _(pool):
            def sel(dst, src, op, base, pattern, cm, fill=0.0):
                return pool.affine_select(out=dst, in_=src, compare_op=op, fill=fill, base=base,
                                          pattern=pattern, channel_multiplier=cm)
            for dst, v in ((ones[:], 1.0), (one_h[:], 1.0), (ident[:], 0.0), (headones[:], 0.0), (prow, 0.0),
                           (epsb[:, 0:1], EPS), (epsb[:, 1:2], RW_LN_EPS), (epsb[:, 2:3], 1.0)):
                pool.memset(dst, v)
            pool.drain()
            pool.memset(headones[0:64, 0:64], 1.0)
            pool.memset(headones[64:128, 64:128], 1.0)
            pool.drain()
            sel(ident[:], ident[:], ALU.not_equal, 0, [[-1, P]], 1, 1.0)
            pool.drain().then_inc(S["consts"], 1)
            sel(incl[0][:], ones[:], ALU.is_ge, 0, [[1, P]], -1)
            sel(incl[1][:], ones[:], ALU.is_ge, 0, [[-1, P]], 1)
            for d in range(2):
                step, cm = ((1, -1), (-1, 1))[d]
                for kind, op in enumerate((ALU.is_gt, ALU.is_ge, ALU.is_gt, ALU.is_ge)):
                    sel(pred[d][:, kind, :], one_h[:], op, 0, [[step, P]], cm)
            pool.drain()
            for m in range(LEVELS):
                b = 1 << m
                for d in range(2):
                    cols = lev[d][:, m, :].rearrange("p (n w) -> p n w", w=2 * b)
                    early, late = (cols[:, :, 0:b], cols[:, :, b:2 * b])[::1 - 2 * d]
                    one3 = one_h[:, :].rearrange("p (n w) -> p n w", w=2 * b)[:, :, 0:b]
                    lo, nb = (b, 0)[d], P // (2 * b)
                    sel(early, one3, ALU.is_ge, -lo, [[-2 * b, nb], [0, b]], 1)
                    pool.memset(late, 0.0)
                    pool.drain()
                    sel(early, early, ALU.is_ge, lo + b - 1, [[2 * b, nb], [0, b]], -1)
                    pool.drain()
                    sel(lev[d][:, m, :], lev[d][:, m, :], ALU.not_equal, 0, [[-1, P]], 1, 1.0)
            for d in range(2):
                pool.tensor_tensor(negstrict[d][:], ident[:], incl[d][:], ALU.subtract)
            pool.drain().then_inc(S["masks"], 1)

            with pool.Fori(0, DEPTH) as L:
                with pool.Fori(0, GP) as i:
                    n = pool.snap(L * (2 * GP) + i * 2)
                    for d in range(2):
                        pool.wait_ge(S["gd_d"], n + (d + 1))
                        pool.tensor_tensor(scores[d][:, 0, :, :], scores[d][:, 0, :, :], bmid(negstrict[d][:], 4),
                                           ALU.mult)
                        pool.tensor_tensor(scores[d][:, 1, :, :], scores[d][:, 1, :, :], bmid(incl[d][:], 4),
                                           ALU.mult).then_inc(S["gd_dm"], 1)
                    for d in range(2):
                        pool.wait_ge(S["ml_d"], n + (d + 1))
                        dg = ml_diag(d)
                        for h in range(2):
                            pool.tensor_tensor(dg[h], dg[h], bmid(incl[d][:], 2), ALU.mult)
                        pool.drain().then_inc(S["ml_dm"], 1)
                with pool.Fori(0, NU) as i:
                    pool.wait_ge(S["up_vconv"], L * NU + (i + 2))
                    pool.tensor_tensor(up_buf(0), up_buf(0), up_buf(1), ALU.mult)
                    pool.drain()
                    pool.tensor_copy(ghi[:, ds(i * 4, 4), :], up_buf(0))
                    pool.drain()
                    pool.tensor_tensor(glo[:, ds(i * 4, 4), :], up_buf(0), ghi[:, ds(i * 4, 4), :].bitcast(F32),
                                       ALU.subtract).then_inc(S["up_done"], 1)

        @block.tensor
        def _(pe):
            pe.sem_inc(S["slot_done"], RING)
            pe.sem_inc(S["lo_ready"], RING)
            for credit in ("row_free", "mixp_free", "up_gconv", "up_vconv", "up_done"):
                pe.sem_inc(S[credit], 1)
            pe.wait_ge(S["consts"], 1)

            def mm(o_, a, b, start, stop):
                return pe.matmul(o_, a, b, start=start, stop=stop, skip_group_check=True)

            def turn(o_, a):
                n = a.shape[0]
                return pe.transpose(o_, a, ident[0:n, 0:n])

            def slot_wait(base, slot):
                pe.wait_ge(S["lo_ready"], base + (RING + slot + 1))

            def product(o_, a, b, first, last):
                mm(o_, a[0], b[0], first, False)
                mm(o_, a[0], b[1], False, False)
                return mm(o_, a[1], b[0], False, last)

            def wparts(slot, kk, lo, n):
                return tuple(w[:, slot % RING, kk, lo:lo + n] for w in (whi, wlo))

            def turn_rows(src, psum_sem):
                for g in range(4):
                    for t in range(NT):
                        if psum_sem == "ut_psum" and g % 2 == 0:
                            pe.wait_ge(S[f"u_ready{t}"], uq + (g // 2 + 1))
                        for c in range(4):
                            last = turn(ps[2 * g + t][:, c * P:(c + 1) * P], src[:, t, (4 * g + c) * P:(4 * g + c + 1) * P])
                        last.then_inc(S[psum_sem], 1)

            def token_product(hi, lo, slot0, base, kt, bank_of, before=None, after=None, at_slot=None):
                for i in range(NO):
                    if before:
                        before(i)
                    for k in range(kt // KS):
                        slot = slot0 + kt // KS * i + k
                        if at_slot:
                            at_slot(i, k)
                        slot_wait(base, slot)
                        for t in range(NT):
                            for kk in range(KS):
                                c = KS * k + kk
                                last = product(ps[bank_of(i, t)][:, :], (hi[:, c, t * P:(t + 1) * P], lo[:, c, t * P:(t + 1) * P]),
                                               wparts(slot, kk, 0, 512), c == 0, c == kt - 1)
                        last.then_inc(S["slot_done"], 1)
                    if after:
                        after(i)

            def rw_prepare(c, n, stage):
                if stage == 0:
                    pe.wait_ge(S["rw_sq"], n + 1)
                    mm(ps[7][:, 0:T], headones[:], ch[:, 2, :], True, True).then_inc(S["rw_ssq"], 1)
                    for t in range(NT):
                        last = turn(ps[3][:, t * P:(t + 1) * P], ch[:, 0, t * P:(t + 1) * P])
                    last.then_inc(S["rw_vt"], 1)
                if stage == 1:
                    pe.wait_ge(S["rw_cf"], n + 1)
                    for t in range(NT):
                        last = mm(ps[7][:, 2 * t:2 * t + 2], ch[:, 3, t * P:(t + 1) * P], headones[:, 0:P:64], True, True)
                    last.then_inc(S["rw_coef"], 1)

            def invert_start(m2, d):
                pe.wait_ge(S["inv_t1"], m2 + (d + 1))
                for j in range(4):
                    last = turn(ps[4 * d + 1][:, j * P:(j + 1) * P], TT[d][:, j, :])
                last.then_inc(S["inv_t1p"], 1)

            def invert(m2, nt, between=None):
                ml = pe.snap(m2 * LEV)
                mh = pe.snap(m2 * (LEV // 2))
                mn = pe.snap(m2 * (LEV - 1))
                for lv in range(LEV):
                    for d in range(2):
                        if lv == 0:
                            pe.wait_ge(S["inv_tn1"], m2 + (d + 1))
                        else:
                            pe.wait_ge(S["inv_tn"], mn + (2 * lv - 1 + d))
                        for j in range(4):
                            last = mm(ps[4 * d][:, j * P:(j + 1) * P], nt(d, j), TN[d][:, j, :], True, True)
                        last.then_inc(S["inv_x"], 1)
                    for d in range(2):
                        pe.wait_ge(S["inv_xs"], ml + (2 * lv + d + 1))
                        if lv:
                            pe.wait_ge(S[f"inv_tt{d}"], mh + lv)
                        if lv < LEV - 1:
                            for j in range(4):
                                mm(ps[4 * d + 1][:, j * P:(j + 1) * P], TT[d][:, j, :], XS[d][:, j, :], True, True)
                        for j in range(4):
                            last = mm(ps[4 * d + 2][:, j * P:(j + 1) * P], XS[d][:, j, :], TT[d][:, j, :], True, True)
                        last.then_inc(S["inv_t"], 1)
                    if between and lv in between:
                        between[lv]()

            with pe.Fori(0, DEPTH) as L:
                base = pe.snap(L * SL)
                pe.wait_ge(S["h_ready"], L * 3 + 1)
                pe.wait_ge(S["rows_in"], L * ROWS_TOTAL + ROWS_TOTAL)
                for j in range(PT):
                    last = turn(ps[j // 4][:, (j % 4) * P:(j % 4 + 1) * P], prow[:, j, :])
                last.then_inc(S["par_turned"], 1)
                pe.wait_ge(S["par_ready"], L + 1)
                uq = pe.snap(L * 6)
                turn_rows(YB, "ut_psum")
                nb = pe.snap(L * NB)
                for i, (kind, b, c0, tiles) in enumerate(blocks):
                    if i >= 2:
                        pe.wait_ge(S["blk_evac"], nb + (i - 1))
                    g = 4 * (i % 2)
                    for k in range(KSLOTS):
                        slot = SL_IN + KSLOTS * i + k
                        if i == 0 and k % 2 == 0:
                            pe.wait_ge(S["ut_ready"], L * 24 + max(4, k + 2))
                        slot_wait(base, slot)
                        for c in range(len(tiles or ())):
                            off = 2 * RD * c if kind == "lora" else P * c
                            for kk in range(KS):
                                u = KS * k + kk
                                last = product(ps[g + c][:, 0:T], wparts(slot, kk, off, P), (uhi[:, u, :], ulo[:, u, :]),
                                               u == 0, u == KT - 1)
                        for t in range(0 if tiles else NT):
                            w = width((kind, b, c0, tiles))
                            for kk in range(KS):
                                u = KS * k + kk
                                last = product(ps[g + t][:, 0:w], (uhi[:, u, t * P:(t + 1) * P], ulo[:, u, t * P:(t + 1) * P]),
                                               wparts(slot, kk, 0, w), u == 0, u == KT - 1)
                        last.then_inc(S["slot_done"], 1)

                pe.wait_ge(S["masks"], 1)
                pe.wait_ge(S["lora_act"], L + 1)
                pe.wait_ge(S["w2_in"], L * 48 + 48)
                pe.wait_ge(S["blk_evac"], nb + NB)
                for j in range(2):
                    for c in range(RC):
                        for d in range(2):
                            last = mm(ps[4 * j + c][:, d * T:(d + 1) * T], w2sb[RD * j:RD * (j + 1), d, c * P:(c + 1) * P],
                                      zlora[RD * j:RD * (j + 1), 0, :], True, True)
                        last.then_inc(S["lora_psum"], 1)
                pe.wait_ge(S["lora_ready"], L * 8 + 8)
                for t in range(NT):
                    last = mm(ps[t][:, :], zlora[0:RG, 1, t * P:(t + 1) * P], g2sb, True, True)
                last.then_inc(S["gate_psum"], 1)
                def gate_sums():
                    pe.wait_ge(S["gd_gl"], L + 1)
                    for d in range(2):
                        for t in range(NT):
                            mm(ps[7][:, 2 * GH * t + GH * d:2 * GH * t + GH * d + GH], incl[d][:],
                               gates[:, 0, t, GH * d:GH * d + GH], True, True)
                    for t in range(NT):
                        last = mm(ps[7][:, 64 + 2 * GH * t:64 + 2 * GH * (t + 1)], ones[:], gates[:, 0, t, :], True, True)
                    last.then_inc(S["gd_cum"], 1)

                def rw_pair(c, more):
                    n = pe.snap(L * RC + c)
                    n2 = pe.snap(n * 2)
                    m2 = pe.snap(L * (2 * (RC + GP)) + c * 2)
                    pe.wait_ge(S["rw_vtc"], n + 1)
                    pe.wait_ge(S["rw_coefc"], n + 1)
                    for d in range(2):
                        pe.wait_ge(S["rw_ops"], n2 + (d + 1))
                        for h in range(2):
                            for t in range(NT):
                                for j in range(2):
                                    hp = slice(64 * h, 64 * h + 64)
                                    last = mm(ps[4 * d + 2 * h + t][:, j * T:(j + 1) * T], KB[d][hp, j, t * P:(t + 1) * P],
                                              AR[d][hp, t, :, :], True, True)
                        last.then_inc(S["rw_sc"], 1)
                    for d in range(2):
                        F = FIRST[d]
                        pe.wait_ge(S["rw_masked"], n2 + (d + 1))
                        for h in range(2):
                            mm(ps[4 * d + 3][:, 64 * h:64 * h + 64], scores[d][:, 2 * h + F, 0, :],
                               Vt[:, F, 64 * h:64 * h + 64], True, True)
                        for j in range(2):
                            last = turn(ps[4 * d + 3][:, T + j * P:T + (j + 1) * P], KB[d][:, j, F * P:(F + 1) * P])
                        last.then_inc(S["rw_pv"], 1)
                        invert_start(m2, d)
                    invert(m2, lambda d, j: scores[d][:, j, 2, :],
                           {1: lambda: rw_prepare(c + 1, n + 1, 0), 5: lambda: rw_prepare(c + 1, n + 1, 1)} if more
                           else {3: gate_sums})
                    for d in range(2):
                        F = FIRST[d]
                        pe.wait_ge(S[f"inv_tt{d}"], m2 * (LEV // 2) + LEV)
                        pe.wait_ge(S["rw_rf"], n2 + (d + 1))
                        for h in range(2):
                            last = mm(ps[4 * d][:, 64 * h:64 * h + 64], TT[d][:, 2 * h + F, :], rf[d][:, 0, 64 * h:64 * h + 64],
                                      True, True)
                        last.then_inc(S["rw_u"], 1)
                    for d in range(2):
                        F = FIRST[d]
                        pe.wait_ge(S["rw_uf"], n2 + (d + 1))
                        mm(ps[4 * d + 1][:, 0:P], KBt[d][:, 0, :], Vt[:, F, :], True, False)
                        mm(ps[4 * d + 1][:, 0:P], KBt[d][:, 1, :], uf[d][:, 0, :], False, True).then_inc(S["rw_state"], 1)
                    for d in range(2):
                        B = 1 - FIRST[d]
                        pe.wait_ge(S["rw_s0"], n2 + (d + 1))
                        mm(ps[4 * d + 2][:, 0:P], AR[d][:, B, 0, :], S0[d][:, 0, :], True, False)
                        for h in range(2):
                            last = mm(ps[4 * d + 2][:, 64 * h:64 * h + 64], scores[d][:, 2 * h + B, 0, :],
                                      Vt[:, B, 64 * h:64 * h + 64], False, h == 1)
                        last.then_inc(S["rw_pv2"], 1)
                    for d in range(2):
                        B = 1 - FIRST[d]
                        pe.wait_ge(S["rw_rf2"], n2 + (d + 1))
                        for h in range(2):
                            last = mm(ps[4 * d][:, P + 64 * h:P + 64 * h + 64], TT[d][:, 2 * h + B, :],
                                      rf[d][:, 1, 64 * h:64 * h + 64], True, True)
                        last.then_inc(S["rw_u2"], 1)
                    if more:
                        pe.wait_ge(S["rw_vtc"], n + 2)
                        pe.wait_ge(S["rw_coefc"], n + 2)
                    else:
                        pe.wait_ge(S["gd_cumc"], L + 1)
                    for d in range(2):
                        F, B = FIRST[d], 1 - FIRST[d]
                        pe.wait_ge(S["rw_uf2"], n2 + (d + 1))
                        y = ps[4 * d + 3]
                        mm(y[:, B * P:(B + 1) * P], AR[d][:, B, 1, :], S0[d][:, 0, :], True, False)
                        for t, u in ((B, 1), (F, 0)):
                            for h in range(2):
                                o_ = y[:, t * P + 64 * h:t * P + 64 * h + 64]
                                mm(o_, scores[d][:, 2 * h + t, 1, :], Vt[:, t, 64 * h:64 * h + 64], False, False)
                                last = mm(o_, scores[d][:, 2 * h + t, 3, :], uf[d][:, u, 64 * h:64 * h + 64], False, True)
                        last.then_inc(S["rw_y"], 1)

                pe.wait_ge(S["gate_ready"], L + 1)
                rw_prepare(0, pe.snap(L * RC), 0)
                rw_prepare(0, pe.snap(L * RC), 1)
                with pe.Fori(0, RC - 1) as c:
                    rw_pair(c, True)
                rw_pair(RC - 1, False)

                pe.wait_ge(S["ml_g"], L + 1)
                for j in range(2):
                    for d in range(2):
                        for t in range(NT):
                            last = turn(ps[j][0:MH, d * T + t * P:d * T + (t + 1) * P],
                                        gy[:, 0, t, 2 * MH * j + MH * d:2 * MH * j + MH * d + MH])
                last.then_inc(S["ml_rt"], 1)
                pe.wait_ge(S["ml_rows"], L + 1)
                for j, rowt in enumerate((TN[0], TT[0])):
                    rr = mono(rowt[0:MH, :, :], 4)
                    for d in range(2):
                        for t in range(NT):
                            q = (4 * j + 2 * d + t) * MH
                            last = mm(ps[2][:, q:q + MH], rr[:, d * T + t * P:d * T + (t + 1) * P], ident[0:MH, 0:MH], True, True)
                last.then_inc(S["ml_back"], 1)
                mh = slice(0, MH)

                def ml_pair(n, n2, stage):
                    if stage == 1:
                        pe.wait_ge(S["ml_in"], n + 1)
                        for d in range(2):
                            for h in range(2):
                                last = mm(ps[4 * d + 3][:, h * T:(h + 1) * T], small[mh, 8 + h:9 + h].to_broadcast([MH, P]),
                                          mrow[d], True, True)
                            last.then_inc(S["ml_mb"], 1)
                    if stage == 2:
                        pe.wait_ge(S["ml_arg"], n2 + 2)
                        for h in range(2):
                            hp = slice(64 * h, 64 * h + 64)
                            for j in range(NT):
                                last = mm(ps[4 * h + 3][:, j * T:(j + 1) * T], KB[0][hp, 1, j * P:(j + 1) * P],
                                          KB[0][hp, 0, :], True, True)
                        last.then_inc(S["ml_sc"], 1)
                    if stage in (4, 5):
                        d = stage - 4
                        if d == 0:
                            pe.wait_ge(S["ml_p"], n2 + 2)
                        else:
                            pe.wait_ge(S["ml_numc"], n2 + 1)
                        for h in range(2):
                            for t in range(NT):
                                js = [j for j in range(NT) if (j <= t if d == 0 else j >= t)]
                                for j in js:
                                    last = mm(ps[4 * h + 3][:, t * (P + 1):(t + 1) * (P + 1)],
                                              ml_flat(d)[:, h, j, t * P:(t + 1) * P], V1[:, j, h, 0:P + 1], j == js[0],
                                              j == js[-1])
                        last.then_inc(S["ml_num"], 1)

                with pe.Fori(0, GP) as i:
                    n = pe.snap(L * GP + i)
                    n2 = pe.snap(n * 2)
                    m2 = pe.snap(L * (2 * (RC + GP)) + (i * 2 + 2 * RC))
                    pe.wait_ge(S["gd_sq"], n + 1)
                    for j in range(2):
                        last = mm(ps[j][:, :], ones[:], mono(KB[j][:, :, :], 2), True, True)
                    last.then_inc(S["gd_ssq"], 1)
                    for h in range(2):
                        for t in range(NT):
                            last = turn(ps[2][:, (2 * h + t) * P:(2 * h + t + 1) * P], chg[:, h, t * P:(t + 1) * P])
                    last.then_inc(S["gd_vt"], 1)
                    pe.wait_ge(S["gd_qk"], n + 1)
                    for h in range(2):
                        for t in range(NT):
                            last = turn(ps[3][:, (2 * h + t) * P:(2 * h + t + 1) * P], AR[h][:, t, 0, :])
                    last.then_inc(S["gd_kt"], 1)
                    for h in range(2):
                        for t in range(NT):
                            last = mm(ps[6 + h][:, t * T:(t + 1) * T], AR[h][:, t, 0, :], AR[h][:, t, :, :], True, True)
                    last.then_inc(S["gd_sc"], 1)
                    for d in range(2):
                        for h in range(2):
                            for t in range(NT):
                                o_ = slice((2 * h + t) * P, (2 * h + t + 1) * P)
                                lg = gs[:, 0 + 2 * t + d, h:h + 1].to_broadcast([P, P])
                                lb = gs[:, 4 + 2 * t + d, h:h + 1].to_broadcast([P, P])
                                mm(ps[4 * d + 1][:, o_], lg, incl[d][:], True, True)
                                mm(ps[4 * d][:, o_], lg, incl[d][:], True, False)
                                last = mm(ps[4 * d][:, o_], lb, ident[:], False, True)
                        last.then_inc(S["gd_gb"], 1)
                    for d in range(2):
                        invert_start(m2, d)
                    pe.wait_ge(S["gd_nt"], n2 + 2)
                    pe.wait_ge(S["gd_vtc"], n + 1)
                    pe.wait_ge(S["gd_ktc"], n + 1)
                    invert(m2, lambda d, j: scores[d][:, 2, j, :], {lv: lambda lv=lv: ml_pair(n, n2, lv) for lv in (1, 2, 4, 5)})
                    for d in range(2):
                        F = FIRST[d]
                        pe.wait_ge(S[f"inv_tt{d}"], m2 * (LEV // 2) + LEV)
                        pe.wait_ge(S["gd_rhs"], n2 + (d + 1))
                        for h in range(2):
                            last = mm(ps[4 * d][:, h * P:(h + 1) * P], TT[d][:, 2 * h + F, :], TN[d][:, 2 * h + F, :], True, True)
                        last.then_inc(S["gd_u"], 1)
                    pe.wait_ge(S["ml_numc"], n2 + 2)
                    for d in range(2):
                        F = FIRST[d]
                        pe.wait_ge(S["gd_uf"], n2 + (d + 1))
                        for h in range(2):
                            last = mm(ps[4 * d + 1][:, h * P:(h + 1) * P], XS[d][:, h, :], ufg[d][:, h, :], True, True)
                        last.then_inc(S["gd_state"], 1)
                        for h in range(2):
                            j = 2 * h + F
                            mm(ps[4 * d + 3][:, j * P:(j + 1) * P], scores[d][:, 3, j, :], ufg[d][:, h, :], True, True)
                    for d in range(2):
                        B = 1 - FIRST[d]
                        pe.wait_ge(S["gd_s0"], n2 + (d + 1))
                        for j in range(2):
                            for h in range(2):
                                last = mm(ps[4 * d + 2][:, (2 * j + h) * P:(2 * j + h + 1) * P], AR[h][:, B, j, :],
                                          S0g[d][:, h, :], True, True)
                        last.then_inc(S["gd_ks"], 1)
                    for d in range(2):
                        B = 1 - FIRST[d]
                        pe.wait_ge(S["gd_rs"], n2 + (d + 1))
                        for h in range(2):
                            last = mm(ps[4 * d][:, (2 + h) * P:(3 + h) * P], TT[d][:, 2 * h + B, :], rf[d][:, h, :], True, True)
                        last.then_inc(S["gd_us"], 1)
                    for d in range(2):
                        B = 1 - FIRST[d]
                        pe.wait_ge(S["gd_usc"], n2 + (d + 1))
                        for h in range(2):
                            j = 2 * h + B
                            last = mm(ps[4 * d + 3][:, j * P:(j + 1) * P], scores[d][:, 3, j, :], KBt[d][:, h, :], True, True)
                        last.then_inc(S["gd_y"], 1)

                pe.wait_ge(S["gd_done"], L * GP + GP)
                turn_rows(YB, "yt_psum")
                pe.wait_ge(S["yt_ready"], L * 8 + 8)
                token_product(uhi, ulo, SL_OUT, base, KT, lambda i, t: 2 * i + t)

                uq = pe.snap(L * 6 + 2)
                turn_rows(YB, "ut_psum")
                with pe.Fori(0, NU) as i:
                    pe.wait_ge(S["ut_ready"], L * 24 + 16)
                    n = pe.snap(L * NU + i)
                    la = pe.snap(base + i * (2 * KSLOTS))
                    for g in range(2):
                        pe.wait_ge(S["up_vconv" if g else "up_gconv"], n + 1)
                        for k in range(KSLOTS):
                            slot = SL_UP + KSLOTS * g + k
                            slot_wait(la, slot)
                            for c in range(4):
                                for kk in range(KS):
                                    u = KS * k + kk
                                    last = product(ps[4 * g + c][:, 0:T], wparts(slot, kk, c * P, P),
                                                   (uhi[:, u, :], ulo[:, u, :]), u == 0, u == KT - 1)
                            last.then_inc(S["slot_done"], 1)
                pe.wait_ge(S["up_gconv"], L * NU + (NU + 1))

                def last_channels(i, k):
                    if i == 0 and k == (FT - 4) // KS:
                        pe.wait_ge(S["up_done"], L * NU + (NU + 1))
                token_product(ghi, glo, SL_DOWN, base, FT, lambda i, t: 2 * i + t, at_slot=last_channels)

                uq = pe.snap(L * 6 + 4)
                turn_rows(YB, "ut_psum")
                pe.wait_ge(S["ut_ready"], L * 24 + 24)
                pe.wait_ge(S["pin_in"], L * 16 + 16)
                for k in range(PLE // P):
                    for t in range(NT):
                        last = turn(ps[7][:, (2 * k + t) * P:(2 * k + t + 1) * P], pin[:, t, k * P:(k + 1) * P])
                last.then_inc(S["p_turned"], 1)
                pe.wait_ge(S["pt_ready"], L + 1)

                def before(i):
                    if i >= 2:
                        pe.wait_ge(S["h_chunk"], L * (3 * NO) + (3 * NO + i - 1))

                def after(i):
                    if i == 0:
                        pe.wait_ge(S["proj_in"], L * 16 + 16)
                    for t in range(NT):
                        for k in range(PLE // P):
                            last = mm(ps[4 * (i % 2) + 2 + t][:, :], pT[:, k, t * P:(t + 1) * P],
                                      projw[:, k, 512 * i:512 * i + 512], k == 0, k == PLE // P - 1)
                    last.then_inc(S["ple_psum"], 1)
                token_product(uhi, ulo, SL_PLE, base, KT, lambda i, t: 4 * (i % 2) + t, before, after)

        @block.scalar
        def _(act):
            act.wait_ge(S["consts"], 1)

            def a(o_, i_, f, **kw):
                return act.activation(o_, i_, f, **kw)

            def squares(n, i, junk):
                act.drain()
                act.wait_ge(S["h_chunk"], n + (i + 1))
                for t in range(NT):
                    k = NO * t + i
                    if t:
                        act.drain()
                    a(junk, H[:, t, 512 * i:512 * i + 512], ACT.Square, accum_out=ssum[:, k:k + 1])

            def rms(q):
                for t in range(NT):
                    act.drain()
                    a(small[:, 12:12 + NO], ssum[:, NO * t:NO * (t + 1)], ACT.Copy, accum_out=small[:, t:t + 1])
                act.drain()
                return a(small[:, 2:2 + NT], small[:, 0:NT], ACT.Sqrt, scale=1.0 / D, bias=epsb[:, 0:1])\
                    .then_inc(S["rms_ready"], 1)

            def normalise(q):
                act.wait_ge(S["rstd_ready"], q)
                for h in range(2):
                    cols = slice(h * D // 2, (h + 1) * D // 2)
                    a(YB[:, 1, cols], H[:, 1, cols], ACT.Copy, scale=small[:, 5:6]).then_inc(S["u_ready1"], 1)

            def rsqrt(o_, i_, scale, bias):
                a(o_, i_, ACT.Ln, scale=scale, bias=bias)
                act.drain()
                return a(o_, o_, ACT.Exp, scale=-0.5)

            def rw_prepare(n, n2, stage):
                if stage == 0:
                    act.wait_ge(S["rw_ssq"], n + 1)
                    rsqrt(ch[:, 3, :], ps[7][:, 0:T], 1.0, epsb[:, 0:1]).then_inc(S["rw_rn"], 1)
                    act.wait_ge(S["rw_vt"], n + 1)
                    a(mono(Vt[:, 2:4, :], 2), ps[3][:, 0:T], ACT.Copy).then_inc(S["rw_vtc"], 1)
                if stage in (1, 2):
                    d = stage - 1
                    act.wait_ge(S["rw_cs"], n2 + stage)
                    a(ew[d][:, 0, :], cs[d][:, :], ACT.Exp, scale=-KAPPA)
                    a(ew[d][:, 1, :], cs[d][:, :], ACT.Exp, scale=KAPPA)
                    a(ew[d][:, 2, :], ew[d][:, 2, :], ACT.Exp, scale=-KAPPA)
                    a(mid[d][:, 3:4], mid[d][:, 2:3], ACT.Exp, scale=-KAPPA).then_inc(S["rw_exp"], 1)

            def t1(m2, between=None):
                for d in range(2):
                    act.wait_ge(S["inv_t1p"], m2 + (d + 1))
                    a(mono(TN[d][:, :, :], 4), ps[4 * d + 1][:, :], ACT.Copy).then_inc(S["inv_tn1"], 1)
                ml = act.snap(m2 * LEV)
                for lv in range(LEV):
                    for d in range(2):
                        if lv < LEV - 1:
                            act.wait_ge(S["inv_t"], ml + (2 * lv + d + 1))
                            a(mono(TN[d][:, :, :], 4), ps[4 * d + 1][:, :], ACT.Copy).then_inc(S["inv_tn"], 1)
                    if lv == LEV - 1:
                        act.wait_ge(S["inv_t"], ml + (2 * lv + 2))
                    a(mono(TT[1][:, :, :], 4), ps[6][:, :], ACT.Copy).then_inc(S["inv_tt1"], 1)
                    if between:
                        between(lv)

            def split_hi(base, landed, first, end):
                for slot in range(first, min(end, SL)):
                    w = slot_width(slot)
                    act.wait_ge(S[f"landed{slot % RING}"], landed + 16 * (slot // RING + 1))
                    act.wait_ge(S["slot_done"], base + (slot + 1))
                    a(whi[:, slot % RING, :, 0:w], ring[:, slot % RING, :, 0:w], ACT.Copy).then_inc(S["hi_ready"], 1)

            def turned_hi(psum_sem, hi_sem, q8, row=None):
                for g in range(4):
                    for t in range(NT):
                        act.wait_ge(S[psum_sem], q8 + (2 * g + t + 1))
                        bank = third(ps[2 * g + t][:, :], 4)
                        if row is None:
                            last = a(uhi[:, 4 * g:4 * g + 4, t * P:(t + 1) * P], bank, ACT.Copy)
                        for c in range(4 if row is not None else 0):
                            k = 4 * g + c
                            last = a(uhi[:, k, t * P:(t + 1) * P], bank[:, c, :], ACT.Copy, scale=par[:, row + k:row + k + 1])
                        last.then_inc(S[hi_sem], 1)

            for i in range(NO - 1):
                squares(0, i, mono(XS[1][:, :, :]))
            with act.Fori(0, DEPTH) as L:
                sl = act.snap(L * SL)
                la = act.snap(L * (16 * SL // RING))
                split_hi(sl, la, 0, AHEAD)
                squares(act.snap(L * (3 * NO)), NO - 1, mono(XS[1][:, :, :]))
                rms(L * 3 + 1)
                normalise(L * 3 + 1)
                NSC = sum(b[0] in ("rw", "lora", "gdq") for b in blocks)
                act.wait_ge(S["par_ready"], L + 1)
                turned_hi("ut_psum", "ut_hi", act.snap(L * 24), rows["norm0"])
                def activated(i):
                    kind, b = blocks[i][:2]
                    if kind in ("rw", "mlq") or (kind, b) == ("mlt", 0):
                        return
                    act.wait_ge(S["blk_evac"], L * NB + (i + 1))
                    if kind == "lora":
                        a(zlora[0:RD, 0, :], zlora[0:RD, 0, :], ACT.Tanh)
                        a(zlora[0:RG, 1, :], zlora[0:RG, 1, :], ACT.Sigmoid).then_inc(S["lora_act"], 1)
                    if kind == "gdq":
                        z = zgd[:, 3 * b:3 * b + 3, :]
                        a(z, z, ACT.Silu)
                    if kind == "gdt":
                        z = zgt[:, :, GT_W // 2 * b:min(GW, GT_W // 2 * (b + 1))]
                        a(z, z, ACT.Silu).then_inc(S["gd_silu"], 1)
                    if kind == "mlt":
                        z = zmt[:, :, max(MW, MT_W // 4 * b):min(2 * MW, MT_W // 4 * (b + 1))]
                        a(z, z, ACT.Sigmoid).then_inc(S["ml_sig"], 1)

                for i, (kind, b, c0, tiles) in enumerate(blocks):
                    end = SL_IN + KSLOTS * (i + 1)
                    split_hi(sl, la, end - KSLOTS + AHEAD, end + AHEAD)
                    if i:
                        activated(i - 1)
                    if kind not in ("rw", "lora", "gdq"):
                        continue
                    act.wait_ge(S["slot_done"], sl + (RING + end))
                    for c, w in enumerate(tiles):
                        if kind == "rw":
                            sc, dst = mu_mid[:, RC * b + c:RC * b + c + 1], zrw[:, RC * b + c, :]
                        elif kind == "lora":
                            sc, dst = mu_mid[0:w, 3 * RC + c:3 * RC + c + 1], zlora[0:w, c, :]
                        else:
                            col = rows["conv"] + TAPS // 2 * 3 * GH + 3 * b + c
                            sc, dst = par[:, col:col + 1], zgd[:, 3 * b + c, :]
                        last = a(dst, ps[4 * (i % 2) + c][0:w, 0:T], ACT.Copy, scale=sc)
                    last.then_inc(S["blk_scaled"], 1)
                for j, nm in enumerate(("w0", "a0")):
                    for c in range(RC):
                        act.wait_ge(S["lora_psum"], L * 8 + (4 * j + c + 1))
                        for d in range(2):
                            col = rows[nm] + RC * d + c
                            last = a(swa[:, j, d, c, :], ps[4 * j + c][:, d * T:(d + 1) * T], ACT.Sigmoid,
                                     bias=par[:, col:col + 1])
                        last.then_inc(S["lora_ready"], 1)
                act.wait_ge(S["gate_psum"], L + 1)
                for t in range(NT):
                    last = a(sgate[:, t, :], ps[t][:, :], ACT.Copy)
                last.then_inc(S["gate_ready"], 1)
                activated(NB - 1)
                def gate_factors(lv):
                    if lv == 1:
                        act.wait_ge(S["gd_sp"], L + 1)
                        a(gpar[:, 1, :], gpar[:, 1, :], ACT.Exp)
                        a(gx[:, 1, :, :], gx[:, 1, :, :], ACT.Exp, scale=-1.0)
                        act.drain()
                        a(gx[:, 1, :, :], gx[:, 1, :, :], ACT.Ln, bias=epsb[:, 2:3]).then_inc(S["gd_ln"], 1)
                        act.wait_ge(S["ml_x"], L + 1)
                        a(gy[:, 1, :, :], gy[:, 0, :, :], ACT.Tanh, scale=1.0 / ML_GATE_CAP).then_inc(S["ml_tanh"], 1)
                    if lv == 3:
                        act.wait_ge(S["ml_f"], L + 1)
                        fg = gy[:, 1, :, 2 * MH:4 * MH]
                        a(fg, fg, ACT.Exp, scale=-1.0)
                        act.drain()
                        a(fg, fg, ACT.Ln, bias=epsb[:, 2:3]).then_inc(S["ml_ln"], 1)
                    if lv == 5:
                        act.wait_ge(S["gd_cumc"], L + 1)
                        a(gates[:, 3, :, :], gates[:, 2, :, :], ACT.Exp)
                        a(gates[:, 4, :, :], gates[:, 4, :, :], ACT.Exp)
                        a(gates[:, 5, :, :], gates[:, 1, :, :], ACT.Exp).then_inc(S["gd_exp"], 1)

                def rw_pair(c, more):
                    n = act.snap(L * RC + c)
                    n2 = act.snap(n * 2)
                    m2 = act.snap(L * (2 * (RC + GP)) + c * 2)
                    t1(m2, (lambda lv: rw_prepare(n + 1, n2 + 2, lv - 2)) if more else gate_factors)
                    for src, dst, k, done in (("rw_u", uf, 0, "rw_uf"), ("rw_pv2", rf, 1, "rw_rf2"), ("rw_u2", uf, 1, "rw_uf2")):
                        for d in range(2):
                            bank = {"rw_u": ps[4 * d][:, 0:P], "rw_pv2": ps[4 * d + 2][:, 0:P], "rw_u2": ps[4 * d][:, P:2 * P]}[src]
                            act.wait_ge(S[src], n2 + (d + 1))
                            a(dst[d][:, k, :], bank, ACT.Copy).then_inc(S[done], 1)
                    act.wait_ge(S["rw_var"], n + 1)
                    rsqrt(st[:, 2, :], st[:, 1, :], 1.0 / 64, epsb[:, 1:2]).then_inc(S["rw_rstd"], 1)

                for stage in range(3):
                    rw_prepare(act.snap(L * RC), act.snap(L * (2 * RC)), stage)
                with act.Fori(0, RC - 1) as c:
                    rw_pair(c, True)
                rw_pair(RC - 1, False)
                act.wait_ge(S["ml_backc"], L + 1)
                a(mgates[:, 2, :, :], mgates[:, 1, :, :], ACT.Exp, scale=-1.0).then_inc(S["ml_expm"], 1)

                def ml_pair(n2, lv):
                    if lv == 2:
                        for d in range(2):
                            act.wait_ge(S["ml_arg"], n2 + (d + 1))
                            a(ml_flat(d), ml_flat(d), ACT.Exp, scale=-1.0).then_inc(S["ml_d"], 1)

                with act.Fori(0, GP) as i:
                    n = act.snap(L * GP + i)
                    n2 = act.snap(n * 2)
                    m2 = act.snap(L * (2 * (RC + GP)) + (i * 2 + 2 * RC))
                    act.wait_ge(S["gd_ssq"], n + 1)
                    for j in range(2):
                        a(mono(ewg[j], 2), ps[j][:, :], ACT.Ln, bias=epsb[:, 0:1])
                    act.drain()
                    for j in range(2):
                        last = a(ewg[j], ewg[j], ACT.Exp, scale=-0.5)
                    last.then_inc(S["gd_rn"], 1)
                    act.wait_ge(S["gd_vt"], n + 1)
                    a(mono(Vt, 4), ps[2][:, :], ACT.Copy).then_inc(S["gd_vtc"], 1)
                    act.wait_ge(S["gd_kt"], n + 1)
                    a(mono(OT, 4), ps[3][:, :], ACT.Copy).then_inc(S["gd_ktc"], 1)
                    for d in range(2):
                        act.wait_ge(S["gd_arg"], n2 + (d + 1))
                        a(scores[d][:, 0:2, :, :], scores[d][:, 0:2, :, :], ACT.Exp).then_inc(S["gd_d"], 1)
                    t1(m2, lambda lv: ml_pair(n2, lv))
                    for src, dst, lo, done in (("gd_u", ufg, 0, "gd_uf"), ("gd_us", KBt, T, "gd_usc")):
                        if src == "gd_us":
                            act.wait_ge(S["ml_ss"], n + 1)
                            rsqrt(st[:, 2, :], st[:, 1, :], 1.0 / P, epsb[:, 0:1]).then_inc(S["ml_rstd"], 1)
                        for d in range(2):
                            act.wait_ge(S[src], n2 + (d + 1))
                            a(mono(dst[d][:, :, :], 2), ps[4 * d][:, lo:lo + T], ACT.Copy).then_inc(S[done], 1)
                    act.wait_ge(S["gd_ss"], n + 1)
                    rsqrt(st[:, 2, :], st[:, 1, :], 1.0 / P, epsb[:, 0:1]).then_inc(S["gd_rstd"], 1)
                turned_hi("yt_psum", "yt_hi", act.snap(L * 8))
                for i in range(NO):
                    split_hi(sl, la, SL_OUT + KSLOTS * i + AHEAD, SL_OUT + KSLOTS * (i + 1) + AHEAD)
                    squares(act.snap(L * (3 * NO) + NO), i, mono(XS[1][:, :, :]))
                rms(L * 3 + 2)
                normalise(L * 3 + 2)
                turned_hi("ut_psum", "ut_hi", act.snap(L * 24 + 8), rows["norm1"])
                with act.Fori(0, NU) as i:
                    n = act.snap(L * NU + i)
                    sli = act.snap(L * SL + i * (2 * KSLOTS))
                    lai = act.snap(L * (16 * SL // RING) + i * (16 * 2 * KSLOTS // RING))
                    for g in range(2):
                        end = SL_UP + KSLOTS * (g + 1)
                        split_hi(sli, lai, end - KSLOTS + AHEAD, end + AHEAD)
                        if g == 0:
                            act.wait_ge(S["up_done"], n + 1)
                        act.wait_ge(S["slot_done"], sli + (RING + end))
                        for c in range(4):
                            tap = rows["fconv"] + FTAPS // 2 * 2 * FT + FT * g + c
                            bias = rows["fbias"] + FT * g + c
                            last = a(up_buf(g)[:, c, :], ps[4 * g + c][:, 0:T], ACT.Identity, scale=par[:, ds(i * 4 + tap, 1)],
                                     bias=par[:, ds(i * 4 + bias, 1)])
                        last.then_inc(S["up_vact" if g else "up_gact"], 1)
                        if g == 0:
                            act.wait_ge(S["up_gconv"], n + 2)
                            a(up_buf(0), up_buf(0), ACT.Silu).then_inc(S["up_silu"], 1)
                for i in range(NO):
                    split_hi(sl, la, SL_DOWN + FT // KS * i + AHEAD, SL_DOWN + FT // KS * (i + 1) + AHEAD)
                    squares(act.snap(L * (3 * NO) + 2 * NO), i, YB[:, 1, 0:512])
                rms(L * 3 + 3)
                normalise(L * 3 + 3)
                turned_hi("ut_psum", "ut_hi", act.snap(L * 24 + 16), rows["norm2"])
                for i in range(NO):
                    end = SL_PLE + KSLOTS * (i + 1)
                    split_hi(sl, la, end - KSLOTS + AHEAD, end + AHEAD)
                    if i:
                        squares(act.snap(L * (3 * NO) + 3 * NO), i - 1, mono(XS[1][:, :, :]))
                    act.wait_ge(S["slot_done"], sl + (RING + end))
                    for t in range(NT):
                        last = a(mono(TN[t][:, :, :], 4), ps[4 * (i % 2) + t][:, :], ACT.Sigmoid)
                    last.then_inc(S["ple_sig"], 1)
            squares(3 * NO * DEPTH, NO - 1, mono(XS[1][:, :, :]))
            rms(3 * DEPTH + 1)

        @block.vector
        def _(v):
            v.wait_ge(S["consts"], 1)
            v.wait_ge(S["h_in"], 16 * NT)
            v.sem_inc(S["h_ready"], 1)
            v.sem_inc(S["h_chunk"], NO)
            MUL, ADD, SUB, MAX, MIN = ALU.mult, ALU.add, ALU.subtract, ALU.max, ALU.min

            def norm(q):
                v.wait_ge(S["rms_ready"], q)
                v.reciprocal(small[:, 4:4 + NT], small[:, 2:2 + NT]).then_inc(S["rstd_ready"], 1)
                v.drain()
                for h in range(2):
                    cols = slice(h * D // 2, (h + 1) * D // 2)
                    v.tensor_scalar(YB[:, 0, cols], H[:, 0, cols], small[:, 4:5], None, MUL).then_inc(S["u_ready0"], 1)

            def split_lo(base, first, end):
                for slot in range(first, min(end, SL)):
                    w = slot_width(slot)
                    v.wait_ge(S["hi_ready"], base + (slot + 1))
                    v.tensor_tensor(wlo[:, slot % RING, :, 0:w], ring[:, slot % RING, :, 0:w],
                                    whi[:, slot % RING, :, 0:w].bitcast(F32), SUB).then_inc(S["lo_ready"], 1)

            def turned_lo(hi_sem, ready_sem, q8, row=None):
                for g in range(4):
                    for t in range(NT):
                        v.wait_ge(S[hi_sem], q8 + (2 * g + t + 1))
                        bank = third(ps[2 * g + t][:, :], 4)
                        if row is None:
                            last = v.tensor_tensor(ulo[:, 4 * g:4 * g + 4, t * P:(t + 1) * P], bank,
                                                   uhi[:, 4 * g:4 * g + 4, t * P:(t + 1) * P].bitcast(F32), SUB)
                        for c in range(4 if row is not None else 0):
                            k = 4 * g + c
                            last = v.scalar_tensor_tensor(ulo[:, k, t * P:(t + 1) * P], bank[:, c, :], par[:, row + k:row + k + 1],
                                                          uhi[:, k, t * P:(t + 1) * P].bitcast(F32), MUL, SUB)
                        last.then_inc(S[ready_sem], 1)

            def add_taps(groups):
                for k in range(len(groups[0][2])):
                    for psum, z, taps in groups:
                        off, w = taps[k]
                        lo, hi = max(0, -off), T - max(0, off)
                        last = v.scalar_tensor_tensor(z[:, lo:hi], psum[:, lo + off:hi + off], w, z[:, lo:hi], MUL, ADD)
                    if k < len(groups[0][2]) - 1:
                        v.drain()
                return last

            def residual(slot0, kt, sl):
                for i in range(NO):
                    end = slot0 + kt // KS * (i + 1)
                    split_lo(sl, end - kt // KS + AHEAD, end + AHEAD)
                    v.wait_ge(S["slot_done"], sl + (RING + end))
                    for t in range(NT):
                        hh = H[:, t, 512 * i:512 * i + 512]
                        last = v.tensor_tensor(hh, hh, ps[2 * i + t][:, :], ADD)
                    last.then_inc(S["h_chunk"], 1)
                v.drain().then_inc(S["h_ready"], 1)

            def invert_start(d, nt):
                v.drain()
                v.tensor_tensor(TT[d][:, :, :], nt, bmid(lev[1 - d][:, 0, :], 4), MUL).then_inc(S["inv_t1"], 1)

            def invert(m2, between=None):
                ml = v.snap(m2 * LEV)
                for lv in range(LEV):
                    for d in range(2):
                        v.wait_ge(S["inv_x"], ml + (2 * lv + d + 1))
                        v.tensor_tensor(XS[d][:, :, :], third(ps[4 * d][:, :], 4), bmid(lev[d][:, lv + 1, :], 4), MUL)\
                            .then_inc(S["inv_xs"], 1)
                    v.wait_ge(S["inv_t"], ml + (2 * lv + 1))
                    v.tensor_copy(mono(TT[0][:, :, :], 4), ps[2][:, :]).then_inc(S["inv_tt0"], 1)
                    if between:
                        between(lv)

            def head_squares(fam, sq):
                v.drain()
                v.tensor_tensor(sq, OL, OL, MUL)
                v.drain()
                v.tensor_reduce(st[:, 1, :], sq, AX_X, ADD).then_inc(S[fam + "_ss"], 1)

            def head_out(i, n, fam, gain, gate, col):
                v.wait_ge(S[fam + "_rstd"], n + 1)
                v.tensor_tensor(OL, OL, bc(st[:, 2, :], P), MUL)
                v.drain()
                for h in range(2):
                    v.tensor_tensor(OL[:, 2 * h:2 * h + 2, :], OL[:, 2 * h:2 * h + 2, :], gain(h), MUL)
                v.drain()
                o4 = OL.rearrange("p (h t) c -> p h t c", h=2)
                for t in range(NT):
                    last = v.tensor_tensor(YB[:, t, ds(i * T + col, T)].rearrange("p (h c) -> p h c", h=2), o4[:, :, t, :],
                                           gate(t), MUL)
                last.then_inc(S[fam + "_done"], 1)

            with v.Fori(0, DEPTH) as L:
                sl = v.snap(L * SL)
                split_lo(sl, 0, AHEAD)
                v.wait_ge(S["par_turned"], L + 1)
                v.tensor_copy(par[:, 0:4 * P], ps[0][:, :])
                v.tensor_copy(par[:, 4 * P:PT * P], ps[1][:, 0:(PT - 4) * P])
                v.drain().then_inc(S["row_free"], 1)
                for dst, m0, m1, k in ((0, rows["mu"], rows["mu"] + 3 * RC, 3 * RC), (3 * RC, rows["mu_wa"], rows["mu_wa"] + 1, 1),
                                       (3 * RC + 1, rows["mu_g"], rows["mu_g"] + 1, 1)):
                    v.tensor_tensor(mu_mid[:, dst:dst + k], par[:, m0:m0 + k], par[:, m1:m1 + k], ADD)
                v.drain()
                v.tensor_scalar(mu_mid[:, :], mu_mid[:, :], -1.0, 1.0, MUL, ADD).then_inc(S["par_ready"], 1)
                norm(L * 3 + 1)
                turned_lo("ut_hi", "ut_ready", v.snap(L * 24), rows["norm0"])
                nsc = 0
                NSC = sum(b[0] in ("rw", "lora", "gdq") for b in blocks)
                for i, (kind, b, c0, tiles) in enumerate(blocks):
                    g = 4 * (i % 2)
                    end = SL_IN + KSLOTS * (i + 1)
                    split_lo(sl, end - KSLOTS + AHEAD, end + AHEAD)
                    if kind in ("rw", "lora", "gdq"):
                        nsc += 1
                        v.wait_ge(S["blk_scaled"], L * NSC + nsc)
                        groups = []
                        for c, w in enumerate(tiles):
                            if kind == "gdq":
                                z = zgd[:, 3 * b + c, :]
                                cols = [(k - TAPS // 2, rows["conv"] + k * 3 * GH + 3 * b + c) for k in range(TAPS) if k != TAPS // 2]
                            elif kind == "rw":
                                z = zrw[:, RC * b + c, :]
                                cols = [(-1, rows["mu"] + RC * b + c), (1, rows["mu1"] + RC * b + c)]
                            else:
                                z = zlora[0:w, c, :]
                                m = rows[("mu_wa", "mu_g")[c]]
                                cols = [(-1, m), (1, m + 1)]
                            groups.append((ps[g + c][0:w, :], z, [(o_, par[0:w, m:m + 1]) for o_, m in cols]))
                        last = add_taps(groups)
                    else:
                        v.wait_ge(S["slot_done"], sl + (RING + end))
                        if kind == "mlq":
                            for c in range(3):
                                last = v.tensor_copy(zmq[:, 3 * b + c, :], ps[g + c][:, 0:T])
                        else:
                            zt, w = (zgt, GT_W // 2) if kind == "gdt" else (zmt, MT_W // 4)
                            for t in range(NT):
                                last = v.tensor_copy(zt[:, t, w * b:w * b + w], ps[g + t][:, 0:w])
                    last.then_inc(S["blk_evac"], 1)

                v.wait_ge(S["masks"], 1)
                for d in range(2):
                    v.memset(scores[d][:, :, :, :], 0.0)
                v.drain()
                for d in range(2):
                    v.tensor_copy(scores[d][:, :, 2, :], bmid(ident[:, :], 4))
                v.drain()
                def rw_prepare(c, n, stage):
                    r_, k_, v_ = zrw[:, c, :], zrw[:, c + RC, :], zrw[:, c + 2 * RC, :]

                    def pcol(name):
                        return par[:, ds(c + rows[name], 1)]
                    if stage == 0:
                        v.tensor_copy(ch[:, 0, :], v_)
                        v.tensor_scalar(ch[:, 1, :], k_, pcol("k_k"), None, MUL)
                        v.drain()
                        v.tensor_tensor(ch[:, 2, :], ch[:, 1, :], ch[:, 1, :], MUL).then_inc(S["rw_sq"], 1)
                    if stage in (1, 2):
                        d = stage - 1
                        sw = ew[d][:, 0, :]
                        v.tensor_copy(sw, swa[:, 0, d, c, :])
                        v.drain()
                        for t in range(NT):
                            o_, i_ = cs[d][:, t * P:(t + 1) * P], sw[:, t * P:(t + 1) * P]
                            if d:
                                o_, i_ = o_[:, ::-1], i_[:, ::-1]
                            v.tensor_tensor_scan(o_, i_, i_, 0.0, ADD, ALU.bypass)
                        v.drain()
                        v.tensor_copy(mid[d][:, 0:NT], cs[d][:, P // 2 - 1 + d:T:P])
                        v.drain()
                        for t in range(NT):
                            tt = cs[d][:, t * P:(t + 1) * P]
                            v.tensor_scalar(tt, tt, mid[d][:, t:t + 1], None, SUB)
                        v.drain()
                        F = FIRST[d]
                        e = F * P + LAST_COL[d]
                        v.tensor_tensor(mid[d][:, 2:3], cs[d][:, e:e + 1], mid[d][:, 1 - F:2 - F], ADD)
                        v.tensor_tensor(ew[d][:, 2, :], cs[d][:, :], sw, SUB).then_inc(S["rw_cs"], 1)
                    if stage == 3:
                        v.wait_ge(S["rw_rn"], n + 1)
                        v.tensor_tensor(ch[:, 4, :], ch[:, 1, :], ch[:, 3, :], MUL)
                        for d in range(2):
                            v.tensor_scalar(ch[:, 5, :], swa[:, 1, d, c, :], 1.0, pcol("k_a"), SUB, MUL)
                            v.drain()
                            v.scalar_tensor_tensor(KB[d][:, 0, :], ch[:, 5, :], 1.0, k_, ADD, MUL)
                            v.tensor_tensor(KB[d][:, 1, :], ch[:, 4, :], swa[:, 1, d, c, :], MUL)
                            v.drain()
                    if stage == 4:
                        v.tensor_tensor(ch[:, 3, :], KB[0][:, 0, :], KB[1][:, 0, :], ADD)
                        v.drain()
                        v.tensor_tensor(ch[:, 3, :], ch[:, 3, :], r_, MUL)
                        v.drain()
                        v.tensor_scalar(ch[:, 3, :], ch[:, 3, :], pcol("r_k"), None, MUL).then_inc(S["rw_cf"], 1)
                    if stage == 5:
                        for d in range(2):
                            v.wait_ge(S["rw_exp"], n * 2 + (d + 1))
                            v.tensor_tensor(KB[d][:, :, :], KB[d][:, :, :], bmid(ew[d][:, 1, :], 2), MUL)

                def rw_coefficients(n):
                    v.wait_ge(S["rw_coef"], n + 1)
                    v.tensor_copy(coef[:, :, :].rearrange("p t h -> p (t h)"), ps[7][:, 0:2 * NT]).then_inc(S["rw_coefc"], 1)

                def rw_operands(c, n):
                    v.wait_ge(S["rw_vtc"], n + 1)
                    v.tensor_copy(Vt[:, 0:2, :], Vt[:, 2:4, :])
                    for d in range(2):
                        v.tensor_copy(mid[d][:, 4:5], mid[d][:, 3:4])
                        v.scalar_tensor_tensor(AR[d][:, :, 0, :], third(ch[:, 4, :], 2), -1.0, third(ew[d][:, 2, :], 2), MUL, MUL)
                        v.tensor_tensor(AR[d][:, :, 1, :], third(zrw[:, c, :], 2), third(ew[d][:, 0, :], 2), MUL)\
                            .then_inc(S["rw_ops"], 1)

                NG, NM = 2 * GH, 2 * MH
                fy = gy[:, 0, :, NM:2 * NM]

                def gate_logs(lv):
                    if lv == 0:
                        v.tensor_tensor(gx[:, 0, :, 0:NG], zgt[:, :, GW:GW + NG], bmid(gpar[:, 0, :], NT), ADD)
                        v.tensor_scalar(gx[:, 0, :, NG:2 * NG], zgt[:, :, GW + NG:GW + 2 * NG], -1.0, None, MUL)
                        for j in range(2):
                            last = v.tensor_tensor(gy[:, 0, :, NM * j:NM * (j + 1)],
                                                   zmt[:, :, 2 * MW + NM * j:2 * MW + NM * (j + 1)], bmid(gpar[:, 2 + j, :], NT), ADD)
                        last.then_inc(S["ml_x"], 1)
                        v.drain()
                        v.scalar_tensor_tensor(gx[:, 1, :, :], gx[:, 0, :, :], -1.0, gx[:, 0, :, :], MUL, MAX).then_inc(S["gd_sp"], 1)
                    if lv == 2:
                        v.wait_ge(S["gd_ln"], L + 1)
                        v.scalar_tensor_tensor(gx[:, 2, :, :], gx[:, 0, :, :], 0.0, gx[:, 1, :, :], MAX, ADD)
                        v.drain()
                        v.scalar_tensor_tensor(gates[:, 0, :, :], gx[:, 2, :, 0:NG], -1.0, bmid(gpar[:, 1, :], NT), MUL, MUL)
                        v.tensor_scalar(gates[:, 1, :, :], gx[:, 2, :, NG:2 * NG], -1.0, None, MUL).then_inc(S["gd_gl"], 1)
                        v.wait_ge(S["ml_tanh"], L + 1)
                        v.tensor_scalar(gy[:, 0, :, 0:NM], gy[:, 1, :, 0:NM], ML_GATE_CAP, None, MUL)
                        v.tensor_scalar(fy, gy[:, 1, :, NM:2 * NM], -ML_GATE_CAP, None, MUL)
                        v.drain()
                        v.scalar_tensor_tensor(gy[:, 1, :, NM:2 * NM], fy, -1.0, fy, MUL, MAX).then_inc(S["ml_f"], 1)
                    if lv == 4:
                        v.wait_ge(S["gd_cum"], L + 1)
                        v.tensor_copy(gates[:, 2, :, :].rearrange("p t g -> p (t g)"), ps[7][:, 0:NT * NG])
                        v.drain()
                        v.tensor_tensor(gates[:, 4, :, :].rearrange("p t g -> p (t g)"), ps[7][:, 64:64 + NT * NG],
                                        gates[:, 2, :, :].rearrange("p t g -> p (t g)"), SUB).then_inc(S["gd_cumc"], 1)
                        v.wait_ge(S["ml_ln"], L + 1)
                        v.scalar_tensor_tensor(fy, fy, 0.0, gy[:, 1, :, NM:2 * NM], MAX, ADD)
                        v.drain()
                        v.tensor_scalar(fy, fy, -1.0, None, MUL).then_inc(S["ml_g"], 1)

                def rw_pair(c, more):
                    n = v.snap(L * RC + c)
                    n2 = v.snap(n * 2)
                    m2 = v.snap(L * (2 * (RC + GP)) + c * 2)
                    v4 = mono(Vt[:, 0:2, :], 2).rearrange("p (g c) -> p g c", c=64)
                    b4 = mono(OL[:, 2:4, :], 2).rearrange("p (g c) -> p g c", c=64)
                    v.tensor_tensor(b4, v4, bc(coef[:, :, :].rearrange("p t h -> p (t h)"), 64), MUL)
                    for d in range(2):
                        v.wait_ge(S["rw_sc"], n2 + (d + 1))
                        v.tensor_copy(st[:, 3, d:d + 1], ps[4 * d][:, 0:1])
                        for j in range(4):
                            last = v.copy_predicated(scores[d][:, j, :, :].rearrange("p a c -> p (a c)"),
                                                     pred[d][:, :, :].rearrange("p a c -> p (a c)").bitcast(I16), ps[4 * d + j][:, :])
                        last.then_inc(S["rw_masked"], 1)
                        invert_start(d, scores[d][:, :, 2, :])
                    for d in range(2):
                        v.wait_ge(S["rw_pv"], n2 + (d + 1))
                        v.tensor_copy(rf[d][:, 0, :], ps[4 * d + 3][:, 0:P])
                        v.tensor_copy(mono(KBt[d][:, :, :], 2), ps[4 * d + 3][:, T:2 * T]).then_inc(S["rw_rf"], 1)
                    invert(m2, (lambda lv: rw_prepare(c + 1, n + 1, lv)) if more else gate_logs)
                    for d in range(2):
                        v.wait_ge(S["rw_state"], n2 + (d + 1))
                        v.scalar_tensor_tensor(S0[d][:, 0, :], ps[4 * d + 1][:, 0:P], mid[d][:, 4:5], headones[:, :], MUL, MUL)\
                            .then_inc(S["rw_s0"], 1)
                    if more:
                        rw_coefficients(n + 1)
                    o2 = mono(OL[:, 0:2, :], 2)
                    v.wait_ge(S["rw_y"], n2 + 1)
                    v.tensor_copy(o2, ps[3][:, 0:T])
                    v.drain()
                    v.wait_ge(S["rw_y"], n2 + 2)
                    v.tensor_tensor(o2, o2, ps[7][:, 0:T], ADD)
                    if more:
                        rw_operands(c + 1, n + 1)
                    v.drain()
                    h4 = o2.rearrange("p (g c) -> p g c", c=64)
                    t4 = mono(OT[:, 0:2, :], 2).rearrange("p (g c) -> p g c", c=64)
                    q4 = mono(OT[:, 2:4, :], 2).rearrange("p (g c) -> p g c", c=64)
                    v.tensor_reduce(st[:, 0, :], h4, AX_X, ADD)
                    v.drain()
                    v.tensor_scalar(st[:, 0, :], st[:, 0, :], 1.0 / 64, None, MUL)
                    v.drain()
                    v.tensor_tensor(t4, h4, bc(st[:, 0, :], 64), SUB)
                    v.drain()
                    v.tensor_tensor(q4, t4, t4, MUL)
                    v.drain()
                    v.tensor_reduce(st[:, 1, :], q4, AX_X, ADD).then_inc(S["rw_var"], 1)
                    v.wait_ge(S["rw_rstd"], n + 1)
                    v.tensor_tensor(t4, t4, bc(st[:, 2, :], 64), MUL)
                    v.drain()
                    tt = OT[:, 0:2, :]
                    v.tensor_tensor(tt, tt, bmid(lnp[:, 0, ds(c * P, P)], 2), MUL)
                    v.drain()
                    v.tensor_tensor(tt, tt, bmid(lnp[:, 1, ds(c * P, P)], 2), ADD)
                    v.drain()
                    v.tensor_tensor(tt, tt, OL[:, 2:4, :], ADD)
                    v.drain()
                    v.tensor_tensor(YB[:, :, ds(c * P, P)], tt, sgate[:, :, ds(c * P, P)], MUL).then_inc(S["rw_done"], 1)

                v.wait_ge(S["gate_ready"], L + 1)
                v.wait_ge(S["mixp_in"], L * MIXP_TOTAL + MIXP_TOTAL)
                for stage in range(6):
                    rw_prepare(0, v.snap(L * RC), stage)
                rw_coefficients(v.snap(L * RC))
                rw_operands(0, v.snap(L * RC))
                v.drain()
                with v.Fori(0, RC - 1) as c:
                    rw_pair(c, True)
                rw_pair(RC - 1, False)

                v.memset(V1[:, :, :, P:P + 1], 1.0)
                gflat = gates[:, :, :, :].rearrange("p k t g -> p (k t g)").rearrange("p (a h) -> p a h", h=GH)
                v.wait_ge(S["ml_rt"], L + 1)
                lf_r, F_r, e_r, M_r, m_r = (mono(b_[0:MH, :, :], 4) for b_ in (XS[0], XS[1], TN[0], TN[1], TT[0]))
                v.tensor_copy(lf_r, ps[1][0:MH, :])
                v.drain()

                def halves(ap):
                    return ap[:, 0:T], ap[:, T:2 * T][:, ::-1]
                for o_, i_ in zip(halves(F_r), halves(lf_r)):
                    v.tensor_tensor_scan(o_, i_, i_, 0.0, ADD, ALU.bypass)
                v.drain()
                v.tensor_tensor(e_r, ps[0][0:MH, :], F_r, SUB)
                v.drain()
                for o_, i_ in zip(halves(M_r), halves(e_r)):
                    v.tensor_tensor_scan(o_, i_, i_, 0.0, MAX, ALU.bypass)
                v.drain()
                for d in range(2):
                    v.tensor_copy(mrow[d], M_r[:, d * T:(d + 1) * T])
                v.tensor_tensor(m_r, F_r, M_r, ADD).then_inc(S["ml_rows"], 1)
                v.wait_ge(S["ml_back"], L + 1)
                v.tensor_copy(mgates[:, 0:2, :, :].rearrange("p k t g -> p (k t g)"), ps[2][:, 0:8 * MH]).then_inc(S["ml_backc"], 1)
                mflat = mgates[:, :, :, :].rearrange("p k t g -> p (k t g)").rearrange("p (a h) -> p a h", h=MH)

                def ml_pair(i, n, n2, stage):
                    if stage == 0:
                        v.tensor_copy(mgs[:, :, :], mflat[:, :, ds(i * 2, 2)])
                        v.tensor_scalar(KB[0][:, 0, :], zmq[:, i, :], 64 ** -0.5, None, MUL)
                        v.tensor_copy(KB[0][:, 1, :], zmq[:, i + MP, :])
                        for j in range(NT):
                            v.tensor_copy(V1[:, j, :, 0:P], zmt[:, j, ds(i * T, T)].rearrange("p (h c) -> p h c", h=2))
                        v.tensor_copy(small[0:MH, 8:10], ident[0:MH, ds(i * 2, 2)]).then_inc(S["ml_in"], 1)
                    if stage == 1:
                        for d in range(2):
                            v.wait_ge(S["ml_mb"], n2 + (d + 1))
                            for h in range(2):
                                for j in range(NT):
                                    last = v.tensor_scalar(ml_flat(d)[:, h, j, :], ps[4 * d + 3][:, h * T:(h + 1) * T],
                                                           mgs[:, 2 * d + j, h:h + 1], 0.0, SUB, MAX)
                            last.then_inc(S["ml_arg"], 1)
                    if stage == 3:
                        v.wait_ge(S["ml_sc"], n + 1)
                        for d in range(2):
                            v.wait_ge(S["ml_dm"], n2 + (d + 1))
                            for h in range(2):
                                w = ml_flat(d)[:, h, :, :].rearrange("p j t -> p (j t)")
                                last = v.tensor_tensor(w, w, ps[4 * h + 3][:, :], MUL)
                            last.then_inc(S["ml_p"], 1)
                    if stage in (4, 5):
                        d = stage - 4
                        v.wait_ge(S["ml_num"], n2 + (d + 1))
                        nd = [ps[4 * h + 3][:, 0:2 * (P + 1)].rearrange("p (t c) -> p t c", t=2) for h in range(2)]
                        for h in range(2):
                            v.tensor_scalar(st[:, 3, 2 * h:2 * h + 2], nd[h][:, :, P], -1.0, None, MUL)
                        v.drain()
                        for h in range(2):
                            v.tensor_tensor(st[:, 0, 2 * h:2 * h + 2], nd[h][:, :, P], st[:, 3, 2 * h:2 * h + 2], MAX)
                        v.drain()
                        for h in range(2):
                            v.tensor_tensor(st[:, 0, 2 * h:2 * h + 2], st[:, 0, 2 * h:2 * h + 2], mgs[:, 8 + 2 * d:10 + 2 * d, h], MAX)
                        v.drain()
                        v.reciprocal(st[:, 0, :], st[:, 0, :])
                        v.drain()
                        dst = OL if d == 0 else msq
                        for h in range(2):
                            last = v.tensor_tensor(dst[:, 2 * h:2 * h + 2, :], nd[h][:, :, 0:P], bc(st[:, 0, 2 * h:2 * h + 2], P), MUL)
                        last.then_inc(S["ml_numc"], 1)

                with v.Fori(0, GP) as i:
                    v.wait_ge(S["ml_expm"], L + 1)
                    v.wait_ge(S["ml_sig"], L * 3 + 3)
                    v.wait_ge(S["mln_in"], L * 16 + 16)
                    v.wait_ge(S["gd_exp"], L + 1)
                    v.wait_ge(S["gd_silu"], L * 2 + 2)
                    n = v.snap(L * GP + i)
                    n2 = v.snap(n * 2)
                    m2 = v.snap(L * (2 * (RC + GP)) + (i * 2 + 2 * RC))
                    q_, k_, v_ = (zgd[:, ds(i * 2 + GH * j, 2), :] for j in range(3))
                    v.tensor_copy(gs[:, :, :], gflat[:, :, ds(i * 2, 2)])
                    v.tensor_copy(chg, v_)
                    v.tensor_tensor(KB[0][:, :, :], q_, q_, MUL)
                    v.tensor_tensor(KB[1][:, :, :], k_, k_, MUL).then_inc(S["gd_sq"], 1)
                    v.wait_ge(S["gd_rn"], n + 1)
                    for h in range(2):
                        kh, qh = zgd[:, i * 2 + (GH + h), :], zgd[:, i * 2 + h, :]
                        v.tensor_tensor(AR[h][:, :, 0, :], third(kh, 2), third(ewg[1][:, h, :], 2), MUL)
                        last = v.scalar_tensor_tensor(AR[h][:, :, 1, :], third(qh, 2), P ** -0.5, third(ewg[0][:, h, :], 2), MUL, MUL)
                    last.then_inc(S["gd_qk"], 1)
                    for d in range(2):
                        v.wait_ge(S["gd_gb"], n2 + (d + 1))
                        for j in range(2):
                            for h in range(2):
                                for t in range(NT):
                                    u = 2 * h + t
                                    last = v.tensor_scalar(scores[d][:, j, u, :], ps[4 * d + j][:, u * P:(u + 1) * P],
                                                           gs[:, 8 + 2 * t + d, h:h + 1], 0.0, SUB, MIN)
                        last.then_inc(S["gd_arg"], 1)
                    v.wait_ge(S["gd_sc"], n + 1)
                    for d in range(2):
                        v.wait_ge(S["gd_dm"], n2 + (d + 1))
                        for h in range(2):
                            pp = ps[6 + h][:, :].rearrange("p (t j c) -> p t j c", t=2, j=2)
                            for j in range(2):
                                v.tensor_tensor(scores[d][:, 2 + j, 2 * h:2 * h + 2, :], pp[:, :, j, :],
                                                scores[d][:, j, 2 * h:2 * h + 2, :], MUL)
                        v.drain()
                        v.tensor_tensor(scores[d][:, 2, :, :], scores[d][:, 2, :, :], bmid(ident[:, :], 4), ADD)\
                            .then_inc(S["gd_nt"], 1)
                        invert_start(d, scores[d][:, 2, :, :])
                    invert(m2, lambda lv: ml_pair(i, n, n2, lv))
                    v.wait_ge(S["gd_vtc"], n + 1)
                    v.wait_ge(S["gd_ktc"], n + 1)
                    for d in range(2):
                        F = FIRST[d]
                        v.wait_ge(S["inv_t"], m2 * LEV + (2 * LEV - 1 + d))
                        for h in range(2):
                            for t in range(NT):
                                v.tensor_scalar(TN[d][:, 2 * h + t, :], Vt[:, 2 * h + t, :], gs[:, 20 + 2 * t + d, h:h + 1], None, MUL)
                            v.tensor_scalar(XS[d][:, h, :], OT[:, 2 * h + F, :], gs[:, 16 + 2 * F + d, h:h + 1], None, MUL)
                        v.scalar_tensor_tensor(gs[:, 4 + d:8 + d:2, :], gs[:, 20 + d:24:2, :], -1.0, gs[:, 12 + d:16:2, :], MUL, MUL)\
                            .then_inc(S["gd_rhs"], 1)
                    v.drain()
                    v.tensor_tensor(OL, OL, msq, ADD)
                    head_squares("ml", msq)
                    for d in range(2):
                        v.wait_ge(S["gd_state"], n2 + (d + 1))
                        v.tensor_copy(mono(S0g[d], 2), ps[4 * d + 1][:, 0:T]).then_inc(S["gd_s0"], 1)
                    for d in range(2):
                        B = 1 - FIRST[d]
                        v.wait_ge(S["gd_ks"], n2 + (d + 1))
                        for h in range(2):
                            v.scalar_tensor_tensor(rf[d][:, h, :], ps[4 * d + 2][:, h * P:(h + 1) * P], gs[:, 4 + 2 * B + d, h:h + 1],
                                                   TN[d][:, 2 * h + B, :], MUL, ADD)
                            last = v.tensor_scalar(XS[d][:, 2 + h, :], ps[4 * d + 2][:, (2 + h) * P:(3 + h) * P],
                                                   gs[:, 12 + 2 * B + d, h:h + 1], None, MUL)
                        last.then_inc(S["gd_rs"], 1)
                    head_out(i, n, "ml", lambda h: bmid(mln[:, ds(i * T + h * P, P)], 2),
                             lambda t: zmt[:, t, ds(i * T + MW, T)].rearrange("p (h c) -> p h c", h=2), RW + GW)
                    o4 = OL.rearrange("p (h t) c -> p h t c", h=2)
                    v.drain()
                    for d in range(2):
                        v.wait_ge(S["gd_y"], n2 + (d + 1))
                        if d == 0:
                            v.tensor_copy(mono(OL, 4), ps[3][:, :])
                        else:
                            v.tensor_tensor(mono(OL, 4), mono(OL, 4), ps[7][:, :], ADD)
                        v.drain()
                        ob = o4[:, :, 1 - FIRST[d], :]
                        v.tensor_tensor(ob, ob, XS[d][:, 2:4, :], ADD)
                        v.drain()
                    head_squares("gd", OT)
                    head_out(i, n, "gd", lambda h: bmid(gdn[:, :], 2),
                             lambda t: zgt[:, t, ds(i * T, T)].rearrange("p (h c) -> p h c", h=2), RW)

                v.drain().then_inc(S["mixp_free"], 1)

                turned_lo("yt_hi", "yt_ready", v.snap(L * 8))
                residual(SL_OUT, KT, sl)
                norm(L * 3 + 2)
                turned_lo("ut_hi", "ut_ready", v.snap(L * 24 + 8), rows["norm1"])
                with v.Fori(0, NU) as i:
                    n = v.snap(L * NU + i)
                    sli = v.snap(L * SL + i * (2 * KSLOTS))
                    for g in range(2):
                        end = SL_UP + KSLOTS * (g + 1)
                        split_lo(sli, end - KSLOTS + AHEAD, end + AHEAD)
                        if g == 1:
                            v.wait_ge(S["up_silu"], n + 1)
                        v.wait_ge(S["up_vact" if g else "up_gact"], n + 1)
                        groups = []
                        for c in range(4):
                            taps = [(k - FTAPS // 2, par[:, ds(i * 4 + (rows["fconv"] + k * 2 * FT + FT * g + c), 1)])
                                    for k in range(FTAPS) if k != FTAPS // 2]
                            groups.append((ps[4 * g + c], up_buf(g)[:, c, :], taps))
                        last = add_taps(groups)
                        last.then_inc(S["up_vconv" if g else "up_gconv"], 1)
                residual(SL_DOWN, FT, sl)
                norm(L * 3 + 3)
                turned_lo("ut_hi", "ut_ready", v.snap(L * 24 + 16), rows["norm2"])
                v.wait_ge(S["p_turned"], L + 1)
                v.tensor_copy(pT[:, :, :].rearrange("p k t -> p (k t)"), ps[7][:, :])
                v.drain().then_inc(S["pt_ready"], 1)
                for i in range(NO):
                    end = SL_PLE + KSLOTS * (i + 1)
                    split_lo(sl, end - KSLOTS + AHEAD, end + AHEAD)
                    v.wait_ge(S["ple_sig"], L * NO + (i + 1))
                    v.wait_ge(S["ple_psum"], L * NO + (i + 1))
                    for t in range(NT):
                        s_ = mono(TN[t][:, :, :], 4)
                        v.tensor_tensor(s_, s_, ps[4 * (i % 2) + 2 + t][:, :], MUL)
                    v.drain()
                    for t in range(NT):
                        hh = H[:, t, 512 * i:512 * i + 512]
                        last = v.tensor_tensor(hh, hh, mono(TN[t][:, :, :], 4), ADD)
                    last.then_inc(S["h_chunk"], 1)
                v.drain().then_inc(S["h_ready"], 1)
            v.wait_ge(S["rms_ready"], 3 * DEPTH + 1)
            v.reciprocal(small[:, 4:4 + NT], small[:, 2:2 + NT])
            v.wait_ge(S["nf_in"], 16)
            v.drain()
            for t in range(NT):
                v.scalar_tensor_tensor(YB[:, t, :], H[:, t, :], small[:, 4 + t:5 + t], Z[:, 0:D], MUL, MUL).then_inc(S["fin_out"], 1)


_INS = ["x", "p", "norm_mix", "w_in", "rw_shift_mu", "rw_w0", "rw_w2", "rw_a0", "rw_a2", "rw_g2", "rw_k_k", "rw_k_a",
        "rw_r_k", "rw_ln_g", "rw_ln_b", "gd_conv_w", "gd_a_log", "gd_dt_bias", "gd_norm_g", "ml_i_bias", "ml_f_bias",
        "ml_norm_g", "w_out", "norm_ffn", "w_up", "ffn_conv_w", "ffn_conv_b", "w_down", "norm_ple", "w_ple_gate",
        "w_ple_proj", "norm_final"]


def kernel(**inputs):
    import numpy as _np
    import concourse.bacc as _bacc
    from concourse import mybir as _mybir
    from concourse.bass_utils import run_bass_kernel_spmd as _run

    nc = _bacc.Bacc("TRN2", target_bir_lowering=False, num_devices=1, dynamic_dma_scratch_size=256)
    arrays, args = {}, []
    for name in _INS:
        a = _np.ascontiguousarray(inputs[name])
        arrays[f"in_{name}_dram"] = a
        args.append(nc.dram_tensor(f"in_{name}_dram", a.shape, _mybir.dt.from_np(a.dtype), kind="ExternalInput").ap())
    shape = _np.asarray(inputs["x"]).shape
    args.append(nc.dram_tensor("out_0_dram", shape, _mybir.dt.float32, kind="ExternalOutput").ap())
    trunk(nc, *args)
    r = _run(nc, [arrays], core_ids=[0])
    return r.results[0]["out_0_dram"]
```
